# Optimizing a Trainium2 kernel written in Bass

```python
import jax, jax.numpy as jnp
from jax import lax
import numpy as np

'''Hybrid parallel-head-group decoder (GLA + Gated DeltaNet head groups in every layer),
adaLN-conditioned, alternating dense SwiGLU / top-2-of-8 SwiGLU experts; one inference step.

Inputs: x_prompt (BATCH,SEQ,D_MODEL), x_sample (DEC_BATCH,DEC_SEQ,D_MODEL),
        c_prompt (BATCH,D_MODEL), c_sample (DEC_BATCH,D_MODEL),
        state_gla  (DEPTH,DEC_BATCH,GLA_HEADS,GLA_DK,GLA_DV)   GLA recurrent state,
        state_gdn  (DEPTH,DEC_BATCH,GDN_HEADS,GDN_DK,GDN_DV)   gated-delta recurrent state,
        state_conv (DEPTH,DEC_BATCH,CONV_W-1,GDN_CONV_DIM)     last pre-conv q/k/v rows,
        then the weights.
Returns the tuple
  (y_prompt (BATCH,SEQ,D_MODEL), y_sample (DEC_BATCH,DEC_SEQ,D_MODEL),
   new_gla_prompt (DEPTH,BATCH,GLA_HEADS,GLA_DK,GLA_DV), new_gdn_prompt (DEPTH,BATCH,GDN_HEADS,GDN_DK,GDN_DV),
   new_conv_prompt (DEPTH,BATCH,CONV_W-1,GDN_CONV_DIM),
   new_gla_sample (DEPTH,DEC_BATCH,...), new_gdn_sample (DEPTH,DEC_BATCH,...), new_conv_sample (DEPTH,DEC_BATCH,...)).
'''

D_MODEL = 1024
BATCH = 1
SEQ = 256
DEPTH = 2
DEC_BATCH = 8
DEC_SEQ = 8
PAST_LEN = 2048
PAGE_SIZE = 128

GLA_HEADS = 4
GLA_DK = 64
GLA_DV = 128
GLA_LOWRANK = 16
GLA_GATE_NORMALIZER = 16.0
GLA_CHUNK = 16
GDN_HEADS = 4
GDN_DK = 128
GDN_DV = 128
GDN_CHUNK = 64
CONV_W = 4
GDN_CONV_DIM = GDN_HEADS * (2 * GDN_DK + GDN_DV)
MIX_WIDTH = GLA_HEADS * GLA_DV + GDN_HEADS * GDN_DV
D_FF_DENSE = 2816
N_EXPERTS = 8
TOP_K = 2
D_FF_EXPERT = 3584
N_DENSE = (DEPTH + 1) // 2
N_MOE = DEPTH // 2
EPS = 1e-6

_SIZES = (GLA_HEADS * GLA_DK, GLA_HEADS * GLA_DK, GLA_HEADS * GLA_DV, GLA_LOWRANK, GLA_HEADS * GLA_DV,
          GDN_CONV_DIM, GDN_HEADS, GDN_HEADS, GDN_HEADS * GDN_DV)
PROJ_DIM = int(sum(_SIZES))
SPLIT_IDX = tuple(int(s) for s in np.cumsum(_SIZES)[:-1])

kernel_name = 'hymba_gla_gdn_adaln_decoder_step'

def rmsnorm(x, w):
    xf = x.astype(jnp.float32)
    y = xf * lax.rsqrt(jnp.mean(xf * xf, axis=-1, keepdims=True) + EPS)
    return (y * w.astype(jnp.float32)).astype(x.dtype)

def l2norm(x):
    xf = x.astype(jnp.float32)
    return xf * lax.rsqrt(jnp.sum(xf * xf, axis=-1, keepdims=True) + EPS)

def gla_chunked(q, k, v, log_a, s0):
    f32 = jnp.float32
    bsz, t_len, nh, _ = q.shape
    dv = v.shape[-1]
    cl = GLA_CHUNK
    n = -(-t_len // cl)
    pw = ((0, 0), (0, n * cl - t_len), (0, 0), (0, 0))
    q, k, v, la = [jnp.pad(a.astype(f32), pw).reshape(bsz, n, cl, nh, a.shape[-1]) for a in (q, k, v, log_a)]
    b = jnp.cumsum(la, axis=2)
    causal = jnp.tril(jnp.ones((cl, cl), dtype=bool))[None, None, :, :, None, None]
    decay = jnp.exp(jnp.where(causal, b[:, :, :, None] - b[:, :, None, :], -jnp.inf))
    attn = jnp.einsum('bntshk,bnthk,bnshk->bnhts', decay, q, k)
    o_intra = jnp.einsum('bnhts,bnshv->bnthv', attn, v)
    b_last = b[:, :, -1]
    q_dec = q * jnp.exp(b)
    k_dec = k * jnp.exp(b_last[:, :, None] - b)

    def step(s, inp):
        qd, kd, vv, bl = inp
        o = jnp.einsum('bthk,bhkv->bthv', qd, s)
        s = s * jnp.exp(bl)[..., None] + jnp.einsum('bthk,bthv->bhkv', kd, vv)
        return s, o

    xs = tuple(jnp.moveaxis(a, 1, 0) for a in (q_dec, k_dec, v, b_last))
    s_fin, o_inter = lax.scan(step, s0.astype(f32), xs)
    o = (o_intra + jnp.moveaxis(o_inter, 0, 1)).reshape(bsz, n * cl, nh, dv)[:, :t_len]
    return o, s_fin.astype(s0.dtype)

def gdn_chunked(q, k, v, g, beta, s0):
    f32 = jnp.float32
    bsz, t_len, nh, _ = q.shape
    dv = v.shape[-1]
    cl = GDN_CHUNK
    n = -(-t_len // cl)
    pad = n * cl - t_len
    q, k, v = [jnp.pad(a.astype(f32), ((0, 0), (0, pad), (0, 0), (0, 0))).reshape(bsz, n, cl, nh, a.shape[-1])
               for a in (q, k, v)]
    g, beta = [jnp.pad(a.astype(f32), ((0, 0), (0, pad), (0, 0))).reshape(bsz, n, cl, nh) for a in (g, beta)]
    gam = jnp.cumsum(g, axis=2)
    gam_h = jnp.moveaxis(gam, 3, 2)
    incl = jnp.tril(jnp.ones((cl, cl), dtype=bool))
    strict = jnp.tril(jnp.ones((cl, cl), dtype=bool), -1)
    lmask = jnp.exp(jnp.where(incl, gam_h[..., :, None] - gam_h[..., None, :], -jnp.inf))
    beta_h = jnp.moveaxis(beta, 3, 2)
    kk = jnp.einsum('bnthk,bnshk->bnhts', k, k)
    m = jnp.where(strict, beta_h[..., :, None] * kk * lmask, 0.0)
    eye = jnp.eye(cl, dtype=f32)
    t_inv = lax.linalg.triangular_solve(eye + m, jnp.broadcast_to(eye, m.shape),
                                        left_side=True, lower=True, unit_diagonal=True)
    u = jnp.einsum('bnhts,bnshv->bnthv', t_inv, v * beta[..., None])
    w = jnp.einsum('bnhts,bnshk->bnthk', t_inv, k * (beta * jnp.exp(gam))[..., None])
    a_qk = jnp.einsum('bnthk,bnshk->bnhts', q, k) * lmask
    q_dec = q * jnp.exp(gam)[..., None]
    g_last = gam[:, :, -1]
    k_dec = k * jnp.exp(g_last[:, :, None] - gam)[..., None]

    def step(s, inp):
        uu, ww, aa, qd, kd, gl = inp
        v_new = uu - jnp.einsum('bthk,bhkv->bthv', ww, s)
        o = jnp.einsum('bthk,bhkv->bthv', qd, s) + jnp.einsum('bhts,bshv->bthv', aa, v_new)
        s = s * jnp.exp(gl)[..., None, None] + jnp.einsum('bthk,bthv->bhkv', kd, v_new)
        return s, o

    xs = tuple(jnp.moveaxis(a, 1, 0) for a in (u, w, a_qk, q_dec, k_dec, g_last))
    s_fin, o = lax.scan(step, s0.astype(f32), xs)
    o = jnp.moveaxis(o, 0, 1).reshape(bsz, n * cl, nh, dv)[:, :t_len]
    return o, s_fin.astype(s0.dtype)

def mixer(h, s_gla, s_gdn, s_conv, w_in, w_gla_gate, b_gla_gate, gla_norm, w_conv, a_log, dt_bias, gdn_norm, w_out):
    f32 = jnp.float32
    bsz, t_len, _ = h.shape
    proj = h @ w_in
    q1, k1, v1, lr, g1, qkv, a_raw, b_raw, z = jnp.split(proj, SPLIT_IDX, axis=-1)
    q1 = q1.reshape(bsz, t_len, GLA_HEADS, GLA_DK) * (GLA_DK ** -0.5)
    k1 = k1.reshape(bsz, t_len, GLA_HEADS, GLA_DK)
    v1 = v1.reshape(bsz, t_len, GLA_HEADS, GLA_DV)
    log_a = jax.nn.log_sigmoid((lr @ w_gla_gate + b_gla_gate).astype(f32)) / GLA_GATE_NORMALIZER
    o1, s_gla_new = gla_chunked(q1, k1, v1, log_a.reshape(bsz, t_len, GLA_HEADS, GLA_DK), s_gla)
    o1 = rmsnorm(o1, gla_norm) * jax.nn.silu(g1.reshape(bsz, t_len, GLA_HEADS, GLA_DV).astype(f32))
    xc = jnp.concatenate([s_conv.astype(qkv.dtype), qkv], axis=1)
    conv = xc[:, 0:t_len] * w_conv[0]
    for j in range(1, CONV_W):
        conv = conv + xc[:, j:j + t_len] * w_conv[j]
    conv = jax.nn.silu(conv)
    s_conv_new = xc[:, t_len:].astype(s_conv.dtype)
    qg, kg, vg = jnp.split(conv, [GDN_HEADS * GDN_DK, 2 * GDN_HEADS * GDN_DK], axis=-1)
    qg = l2norm(qg.reshape(bsz, t_len, GDN_HEADS, GDN_DK)) * (GDN_DK ** -0.5)
    kg = l2norm(kg.reshape(bsz, t_len, GDN_HEADS, GDN_DK))
    vg = vg.reshape(bsz, t_len, GDN_HEADS, GDN_DV)
    g = -jnp.exp(a_log.astype(f32)) * jax.nn.softplus(a_raw.astype(f32) + dt_bias.astype(f32))
    beta = jax.nn.sigmoid(b_raw.astype(f32))
    o2, s_gdn_new = gdn_chunked(qg, kg, vg, g, beta, s_gdn)
    o2 = rmsnorm(o2, gdn_norm) * jax.nn.silu(z.reshape(bsz, t_len, GDN_HEADS, GDN_DV).astype(f32))
    o = jnp.concatenate([o1.reshape(bsz, t_len, -1), o2.reshape(bsz, t_len, -1)], axis=-1).astype(h.dtype)
    return o @ w_out, s_gla_new, s_gdn_new, s_conv_new

def swiglu(h, w_gate, w_up, w_down):
    return (jax.nn.silu(h @ w_gate) * (h @ w_up)) @ w_down

def moe(h, w_router, w_gate, w_up, w_down):
    logits = (h @ w_router).astype(jnp.float32)
    top_v, top_i = lax.top_k(logits, TOP_K)
    top_w = jax.nn.softmax(top_v, axis=-1)
    combine = jnp.sum(jax.nn.one_hot(top_i, N_EXPERTS, dtype=jnp.float32) * top_w[..., None], axis=-2)
    combine = combine.astype(h.dtype)
    y = jnp.zeros_like(h)
    for e in range(N_EXPERTS):
        y = y + combine[..., e:e + 1] * swiglu(h, w_gate[e], w_up[e], w_down[e])
    return y

def setup_inputs(seed: int = 0) -> dict:
    key = jax.random.key(seed)
    ks = jax.random.split(key, 40)
    nrm = lambda i, shape, s: jax.random.normal(ks[i], shape, jnp.float32) * s
    dt = jnp.exp(jax.random.uniform(ks[12], (DEPTH, GDN_HEADS)) * (jnp.log(0.1) - jnp.log(0.001)) + jnp.log(0.001))
    return {
        'x_prompt': nrm(0, (BATCH, SEQ, D_MODEL), 1.0),
        'x_sample': nrm(1, (DEC_BATCH, DEC_SEQ, D_MODEL), 1.0),
        'c_prompt': nrm(2, (BATCH, D_MODEL), 1.0),
        'c_sample': nrm(3, (DEC_BATCH, D_MODEL), 1.0),
        'state_gla': nrm(4, (DEPTH, DEC_BATCH, GLA_HEADS, GLA_DK, GLA_DV), 0.5),
        'state_gdn': nrm(5, (DEPTH, DEC_BATCH, GDN_HEADS, GDN_DK, GDN_DV), 0.1),
        'state_conv': nrm(6, (DEPTH, DEC_BATCH, CONV_W - 1, GDN_CONV_DIM), 1.0),
        'w_ada': nrm(7, (DEPTH, D_MODEL, 6 * D_MODEL), 0.5 * D_MODEL ** -0.5),
        'b_ada': nrm(8, (DEPTH, 6 * D_MODEL), 0.02),
        'norm_mix': 1.0 + nrm(9, (DEPTH, D_MODEL), 0.02),
        'w_in': nrm(10, (DEPTH, D_MODEL, PROJ_DIM), D_MODEL ** -0.5),
        'w_gla_gate': nrm(11, (DEPTH, GLA_LOWRANK, GLA_HEADS * GLA_DK), GLA_LOWRANK ** -0.5),
        'b_gla_gate': nrm(13, (DEPTH, GLA_HEADS * GLA_DK), 0.02),
        'gla_norm': 1.0 + nrm(14, (DEPTH, GLA_DV), 0.02),
        'w_conv': nrm(15, (DEPTH, CONV_W, GDN_CONV_DIM), 0.5),
        'a_log': jnp.log(jax.random.uniform(ks[16], (DEPTH, GDN_HEADS), minval=1.0, maxval=16.0)),
        'dt_bias': dt + jnp.log(-jnp.expm1(-dt)),
        'gdn_norm': 1.0 + nrm(17, (DEPTH, GDN_DV), 0.02),
        'w_out': nrm(18, (DEPTH, MIX_WIDTH, D_MODEL), MIX_WIDTH ** -0.5),
        'norm_ffn': 1.0 + nrm(19, (DEPTH, D_MODEL), 0.02),
        'w_ff_gate': nrm(20, (N_DENSE, D_MODEL, D_FF_DENSE), D_MODEL ** -0.5),
        'w_ff_up': nrm(21, (N_DENSE, D_MODEL, D_FF_DENSE), D_MODEL ** -0.5),
        'w_ff_down': nrm(22, (N_DENSE, D_FF_DENSE, D_MODEL), D_FF_DENSE ** -0.5),
        'w_router': nrm(23, (N_MOE, D_MODEL, N_EXPERTS), D_MODEL ** -0.5),
        'w_exp_gate': nrm(24, (N_MOE, N_EXPERTS, D_MODEL, D_FF_EXPERT), D_MODEL ** -0.5),
        'w_exp_up': nrm(25, (N_MOE, N_EXPERTS, D_MODEL, D_FF_EXPERT), D_MODEL ** -0.5),
        'w_exp_down': nrm(26, (N_MOE, N_EXPERTS, D_FF_EXPERT, D_MODEL), D_FF_EXPERT ** -0.5),
        'w_ada_final': nrm(27, (D_MODEL, 2 * D_MODEL), 0.5 * D_MODEL ** -0.5),
        'b_ada_final': nrm(28, (2 * D_MODEL,), 0.02),
        'norm_final': 1.0 + nrm(29, (D_MODEL,), 0.02),
    }

def reference(x_prompt, x_sample, c_prompt, c_sample, state_gla, state_gdn, state_conv,
              w_ada, b_ada, norm_mix, w_in, w_gla_gate, b_gla_gate, gla_norm, w_conv, a_log, dt_bias,
              gdn_norm, w_out, norm_ffn, w_ff_gate, w_ff_up, w_ff_down, w_router, w_exp_gate, w_exp_up,
              w_exp_down, w_ada_final, b_ada_final, norm_final):

    def trunk(x, c, s_gla, s_gdn, s_conv):
        new_gla, new_gdn, new_conv = [], [], []
        cs = jax.nn.silu(c)
        for l in range(DEPTH):
            mod = (cs @ w_ada[l] + b_ada[l])[:, None, :]
            sh1, sc1, gt1, sh2, sc2, gt2 = jnp.split(mod, 6, axis=-1)
            h = rmsnorm(x, norm_mix[l]) * (1 + sc1) + sh1
            mix, sa, sb, sc_ = mixer(h, s_gla[l], s_gdn[l], s_conv[l], w_in[l], w_gla_gate[l], b_gla_gate[l],
                                     gla_norm[l], w_conv[l], a_log[l], dt_bias[l], gdn_norm[l], w_out[l])
            x = x + gt1 * mix
            h = rmsnorm(x, norm_ffn[l]) * (1 + sc2) + sh2
            i = l // 2
            if l % 2 == 0:
                f = swiglu(h, w_ff_gate[i], w_ff_up[i], w_ff_down[i])
            else:
                f = moe(h, w_router[i], w_exp_gate[i], w_exp_up[i], w_exp_down[i])
            x = x + gt2 * f
            new_gla.append(sa)
            new_gdn.append(sb)
            new_conv.append(sc_)
        shf, scf = jnp.split((cs @ w_ada_final + b_ada_final)[:, None, :], 2, axis=-1)
        y = rmsnorm(x, norm_final) * (1 + scf) + shf
        return y, jnp.stack(new_gla), jnp.stack(new_gdn), jnp.stack(new_conv)

    bp = x_prompt.shape[0]
    dt_ = x_prompt.dtype
    z_gla = jnp.zeros((DEPTH, bp, GLA_HEADS, GLA_DK, GLA_DV), dt_)
    z_gdn = jnp.zeros((DEPTH, bp, GDN_HEADS, GDN_DK, GDN_DV), dt_)
    z_conv = jnp.zeros((DEPTH, bp, CONV_W - 1, GDN_CONV_DIM), dt_)
    y_prompt, gla_p, gdn_p, conv_p = trunk(x_prompt, c_prompt, z_gla, z_gdn, z_conv)
    y_sample, gla_s, gdn_s, conv_s = trunk(x_sample, c_sample, state_gla, state_gdn, state_conv)
    return (y_prompt, y_sample, gla_p, gdn_p, conv_p, gla_s, gdn_s, conv_s)


_drawn_inputs = setup_inputs


def setup_inputs(seed=0):
    import zlib

    import numpy as np

    out = dict(_drawn_inputs(seed))
    spreads = {}
    factors = {'b_gla_gate': 5.737,
     'gla_norm': 6.456,
     'gdn_norm': 6.514,
     'norm_ffn': 3.19,
     'norm_final': 3.057}
    for name, (base, spread) in spreads.items():
        noise = np.random.default_rng([zlib.crc32(name.encode()), seed]).standard_normal(out[name].shape)
        drawn = base * np.exp(spread * noise) if base else spread * noise
        out[name] = __import__('jax').numpy.asarray(drawn.astype(out[name].dtype))
    for name, factor in factors.items():
        out[name] = (out[name] * factor).astype(out[name].dtype)
    return out
```

```python
from contextlib import ExitStack

import numpy as np

import concourse.bass as bass
from concourse import mybir

ALU = mybir.AluOpType
ACT = mybir.ActivationFunctionType
AX = mybir.AxisListType
F32 = mybir.dt.float32
BF16 = mybir.dt.bfloat16
I32 = mybir.dt.int32

P = 128
D = 1024
KD = D // P
TP, NSEQ, LSEQ = 256, 8, 8
TS = NSEQ * LSEQ
T = TP + TS
DEPTH = 2
NC_ = 1 + NSEQ
GH, GK, GV = 4, 64, 128
NH, NK = 4, 128
CT = 12
CW = 4
LR = 16
GATE_NORM = 16.0
EPS = 1e-6
FD = 2816 // P
NE = 8
FE = 3584
CH = 512
NCH = FE // CH
SLOTS = 7
SLOT = KD * CH
N_ADA = 28
N_IN = 7
N_GU = FD // 2
N_OUT = 2
SUB = 32
WORK = 14592
BIG = -1.0e30
CAP = P
MAXPASS = -(-T // CAP)
FAR = 4096.0
TILES = [(0, P), (P, P), (TP, TS)]
LEVELS = [1, 2, 4, 8, 16, 32, 64]

AT_IN = [N_ADA, N_ADA + N_IN + N_OUT + N_GU + KD]
AT_OUT = [a + N_IN for a in AT_IN]
AT_GU = AT_OUT[0] + N_OUT
AT_DN = AT_GU + N_GU
AT_MOE = AT_OUT[1] + N_OUT
PER_E = 3 * NCH

PER_LAYER = {
    "conv_done": 1, "conv_in": 16, "conv_out": 16, "cv": 12, "cv_e": 12, "cv_raw": 12, "dat": 3, "dkk": 6, "dlog": 3,
    "dmask": 3, "dmb": 34, "do": 3, "do_mm": 3, "dqd": 3, "dqk": 6, "dqkT": 6, "drow": 3, "drowe": 3, "ds_mm": 2,
    "dsq": 6, "dss_mm": 4, "dtb": 6, "dtr": 9, "dtu": 40, "dtu_mm": 34, "dvm": 4, "dvn": 3, "dvn_mm": 3,
    "dvn_part": 3, "dw": 3, "dw_mm": 3, "dwm": 4, "dy": 34, "dy_mm": 34, "g": 1, "gact": 1, "gam_mm": 1, "gamc": 1,
    "gcols": 1, "gdn_done": 1, "gdn_fin": 1, "gdn_sstate": 4, "gdn_state": 2, "gdn_state_in": 16,
    "gdn_state_out": 32, "gexp": 1, "gla_arg": 3, "gla_at": 3, "gla_at_mm": 3, "gla_exp": 3, "gla_fin": 1,
    "gla_ktr": 3, "gla_o": 3, "gla_o_mm": 3, "gla_ops": 3, "gla_out": 48, "gla_s_mm": 2, "gla_ss_mm": 4,
    "gla_sstate": 2, "gla_state": 2, "gla_state_in": 32, "gla_tok": 6, "gla_tr": 3, "gla_vm": 4, "gx": 1, "la": 1,
    "lr_t": 1, "out_mm": 8, "proj": 28, "proj_mm": 28, "small_mm": 2, "smallw_in": 32, "x_mix": 8, "xp_ready": 1,
    "z_mm": 2, "zb": 1, "zl": 1,
}

SM = {}


def _pack(table, names):
    at = 0
    for name, n in names:
        table[name] = (at, n)
        at += n
    return at


N_SM = _pack(SM, [("c", KD * NC_), ("b_ada", 4 * N_ADA), ("nm0", KD), ("nm1", KD), ("nf0", KD), ("nf1", KD), ("nfin", KD)]
             + [(f"{n}{l}", w) for l in range(DEPTH)
                for n, w in (("bg", 2), ("wconv", CT * CW), ("glan", 1), ("gdnn", 1), ("alog", NH), ("dtb", NH))])
CF = {}
N_CF = _pack(CF, [("ident", P), ("ones", P), ("tri", P), ("tri_s", TS), ("strict", P), ("seq", NSEQ), ("block", TS)])
CB = {}
N_CB = _pack(CB, [("level", len(LEVELS) * P), ("neg_u", P), ("neg_us", TS), ("neg_l", P), ("neg_ls", TS),
                  ("iota", P), ("reset", T), ("before", NE * NE)])


def shape_constants():
    f, b = np.zeros((P, N_CF), np.float32), np.zeros((P, N_CB), np.float32)
    i, j = np.meshgrid(np.arange(P), np.arange(P), indexing="ij")
    si, sj = i[:TS, :TS], j[:TS, :TS]
    same = si // LSEQ == sj // LSEQ

    def put(dst, table, name, v):
        at, n = table[name]
        dst[:v.shape[0], at:at + n] = v

    put(f, CF, "ident", i == j)
    put(f, CF, "ones", np.ones((P, P)))
    put(f, CF, "tri", i <= j)
    put(f, CF, "tri_s", (si <= sj) & same)
    put(f, CF, "strict", i < j)
    put(f, CF, "seq", np.arange(TS)[:, None] // LSEQ == np.arange(NSEQ)[None, :])
    put(f, CF, "block", same)
    put(b, CB, "level", np.concatenate(
        [(i // (2 * w) == j // (2 * w)) & (i % (2 * w) >= w) & (j % (2 * w) < w) for w in LEVELS], 1))
    put(b, CB, "neg_u", np.where(i <= j, 0, BIG))
    put(b, CB, "neg_us", np.where((si <= sj) & same, 0, BIG))
    put(b, CB, "neg_l", np.where(i > j, 0, BIG))
    put(b, CB, "neg_ls", np.where((si > sj) & same, 0, BIG))
    put(b, CB, "iota", j)
    t = np.arange(T)
    put(b, CB, "reset", np.tile(np.where(t < TP, t % P != 0, (t - TP) % LSEQ != 0), (P, 1)))
    e = np.arange(NE)
    put(b, CB, "before", np.tile((e[None, :] < e[:, None]).reshape(-1), (P, 1)))
    return f, b


def mid(ap, n):
    return ap.unsqueeze(1).to_broadcast([ap.shape[0], n, ap.shape[1]])


def last(ap, n):
    return ap.unsqueeze(len(ap.shape)).to_broadcast([*ap.shape, n])


def build(nc, A, O):
    ctx = ExitStack()
    with ctx:
        def sb(name, shape, dt=F32):
            return ctx.enter_context(nc.sbuf_tensor(name, shape, dt))

        def sem(name):
            return ctx.enter_context(nc.semaphore(name))

        B = [ctx.enter_context(nc.psum_tensor(f"bank{i}", [P, 512], F32)) for i in range(8)]

        ring = sb("ring", [P, SLOTS, SLOT])
        xT = sb("xT", [P, KD, T])
        hT = sb("hT", [P, KD, T])
        small = sb("small", [P, N_SM])
        cf = sb("cf", [P, N_CF])
        cb = sb("cb", [P, N_CB], BF16)
        mod = sb("mod", [P, 4 * N_ADA, NC_])
        wsm = sb("wsm", [P, KD, LR + 2 * NH])
        wgate = sb("wgate", [LR, GH * GK])
        wrt = sb("wrt", [P, KD, NE])
        rs = sb("rs", [P, T])
        rv = sb("rv", [P, T])
        csT = rv[:, 0:KD * NC_]
        rt = sb("rt", [P, T])
        rv8, rs8, rt8 = (sb(n, [P, 2 * NH]) for n in ("rv8", "rs8", "rt8"))
        gAB = sb("gate_ab", [P, 3 * 2 * NH])
        gX, gL, gEB, gG, gBE, gGC, gGL, gD, gEG, gDK, gBG = (
            sb(n, [P, 3 * NH]) for n in ("g_x", "g_log", "g_expb", "g_decay", "g_beta", "g_run", "g_end", "g_left",
                                         "g_exprun", "g_expleft", "g_betaexp"))
        gEA = sb("g_expa", [P, NH])
        gEB_ = sb("gla_expend", [P, 2 * NSEQ])
        gEL = sb("g_expend", [P, NH * NSEQ])
        LG = gAB
        lgE, rank, sel, cw = (sb(n, [P, 3 * NE]) for n in ("lg_e", "rank", "sel", "cw"))
        pos, cwp = (sb(n, [P, 3 * (NE + 1)]) for n in ("pos", "cwp"))
        mx = sb("mx", [P, 3])
        flag = sb("flag", [P, 1], I32)
        W = sb("work", [P, WORK])

        def w(at, n):
            return W[:, at:at + n]

        def v3(ap, a):
            return ap.rearrange("p (a b) -> p a b", a=a)

        def col(name):
            at, n = SM[name]
            return small[:, at:at + n]

        def cst(name, rows=P):
            at, n = CF[name]
            return cf[0:rows, at:at + n]

        def cbf(name, rows=P):
            at, n = CB[name]
            return cb[0:rows, at:at + n]

        ident, ones = cst("ident"), cst("ones")
        TL = 4 * T
        QK, V1, G1, ZT = w(0, TL), w(TL, TL), w(2 * TL, TL), w(3 * TL, TL)
        CV = w(4 * TL, 3 * TL)
        R = 7 * TL
        qk3, v13, g13, zt3, cv3 = v3(QK, 4), v3(V1, 4), v3(G1, 4), v3(ZT, 4), v3(CV, CT)
        LA = v3(w(R, 2 * T), 2)
        R1 = R + 2 * T
        XPW, XSW = TP + CW - 1, LSEQ + CW - 1
        at = R1

        def take(n):
            nonlocal at
            at += n
            assert at <= WORK, at
            return w(at - n, n)

        XP = v3(take(4 * XPW), 4)
        XS = take(4 * NSEQ * XSW).rearrange("p (c s u) -> p c s u", c=4, s=NSEQ)
        OC = take(CT * NC_ * 3).rearrange("p (c s u) -> p c s u", c=CT, s=NC_)
        SC = take(CT * NSEQ * 3).rearrange("p (c s u) -> p c s u", c=CT, s=NSEQ)
        CE = v3(take(2 * T), 2)
        LRT = take(T)[0:LR, :]
        LAE = take(2 * T)
        at = R1
        NJ = [P - SUB * j for j in range(P // SUB)]
        GEA = take(2 * sum(NJ))
        GE = [v3(GEA[:, 2 * sum(NJ[:j]):2 * sum(NJ[:j + 1])], 2) for j in range(len(NJ))]
        GKT, GKE, GQD = (v3(take(256), 2) for _ in range(3))
        GVT = take(512)
        GKDT = take(256)
        GAT = take(512)
        GS = v3(take(256), 2)
        GVM = v3(take(1024), NSEQ)
        GSS = [v3(w(TL, 1024), NSEQ), v3(take(1024), NSEQ)]
        DS = w(R, NH * NSEQ * NK).rearrange("p (h s v) -> p h s v", h=NH, s=NSEQ)
        at = R + NH * NSEQ * NK
        DSP = v3(take(NH * NK), NH)
        DVB, DKB, DKD, DM, DMB, DT, DU = (w(512 * i, 512) for i in range(7))
        DY, DX = take(512), take(512)
        DY2, D01, D34 = DY, w(0, 1024), w(3 * 512, 1024)
        FA = v3(w(0, FD * T), FD)
        FSG = [w(FD * T + i * T, T) for i in range(2)]
        at = 0
        HTOK = v3(take(3 * D), 3)
        ONEH, ONEW = v3(take(3 * P), 3), v3(take(3 * P), 3)
        ONEWT = take(T)
        HG = v3(take(D), KD)
        EE, EA, EAT = (v3(take(2 * CH), 2) for _ in range(3))
        YE = take(D)
        CMP, CEQ = (take(3 * NE * NE).rearrange("p (a b) -> p a b", b=NE) for _ in range(2))

        GAB, GOB = (B[4], B[7]), (B[5], B[0])

        sems = {}

        def S(name):
            if name not in sems:
                sems[name] = sem(name)
            return sems[name]

        def after(eng, name, l, v):
            eng.wait_ge(S(name), PER_LAYER[name] * l + v)

        landed = [S(f"landed{s}") for s in range(SLOTS)]

        def piece_in(eng, n):
            eng.wait_ge(landed[n % SLOTS], 16 * (n // SLOTS + 1))

        def slot(n):
            return ring[:, n % SLOTS, :]

        class Own:

            def __init__(self, eng, name):
                self.eng, self.name, self.n = eng, name, {}

            def go(self, ins, name=None):
                name = name or self.name
                self.n[name] = self.n.get(name, 0) + 1
                ins.then_inc(S(name), 1)

            def do(self, ins, name=None):
                self.go(ins, name)
                self.eng.wait_ge(S(name or self.name), self.n[name or self.name])

        block = ctx.enter_context(nc.Block())
        FP = NC_ * KD

        def md(base, n=KD):
            return mod[:, base:base + n, :]

        def freed_by(n):
            if n < AT_IN[0]:
                return S("ada_mm"), n + 1
            for l in range(DEPTH):
                if AT_IN[l] <= n < AT_OUT[l]:
                    return S("proj_mm"), PER_LAYER["proj_mm"] * l + 4 * (n - AT_IN[l] + 1)
                if AT_OUT[l] <= n < AT_OUT[l] + N_OUT:
                    return S("out_mm"), PER_LAYER["out_mm"] * l + 4 * (n - AT_OUT[l] + 1)
            if n < AT_DN:
                return S("gu_mm"), 2 * (n - AT_GU + 1)
            return S("down_mm"), n - AT_DN + 1

        KINDS = ["e_gate_mm", "e_up_mm", "e_down_mm"]

        @block.sync
        def _(sp):
            for dst, src in ((small, A["small"]), (cf, A["cf"]), (W[:, 0:N_CB], A["cb"]), (wrt, A["wrt"])):
                sp.dma_start(dst[:, :] if dst is not wrt else wrt[:, :, :], src).then_inc(S("const_in"), 16)
            sp.dma_start(xT[:], A["xT"]).then_inc(S("x_in"), 16)

            def load(n, dst, src, wait=True):
                if wait and n >= SLOTS:
                    s, v = freed_by(n - SLOTS)
                    sp.wait_ge(s, v)
                sp.dma_start(dst, src).then_inc(landed[n % SLOTS], 16)

            for n in range(SLOTS):
                load(n, slot(n), A["ada"][n, :, :])
            with sp.Fori(1, N_ADA // SLOTS) as turn:
                for s in range(SLOTS):
                    sp.wait_ge(S("ada_mm"), turn * SLOTS + (s + 1 - SLOTS))
                    sp.dma_start(slot(s), A["ada"][turn * SLOTS + s, :, :]).then_inc(landed[s], 16)
            for l in range(DEPTH):
                for i in range(N_IN):
                    load(AT_IN[l] + i, slot(AT_IN[l] + i), A["w_in"][l, i, :, :])
                for i in range(N_OUT):
                    load(AT_OUT[l] + i, slot(AT_OUT[l] + i), A["w_out"][l, i, :, :])
                if l == 0:
                    for i in range(N_GU):
                        load(AT_GU + i, slot(AT_GU + i), A["gu"][i, :, :])
                    for i in range(KD):
                        load(AT_DN + i, slot(AT_DN + i)[:, 0:FD * P], A["down"][i, :, :])
            for q in range(SLOTS):
                load(AT_MOE + q, slot(AT_MOE + q), A["moe"][q, :, :])

            def behind(e, m):
                sp.wait_ge(S(KINDS[m % 3]), e * NCH + (m // 3 + 1))

            with sp.Fori(0, NE - 1) as e:
                for m in range(PER_E):
                    behind(e, m)
                    sp.dma_start(slot(AT_MOE + SLOTS + m), A["moe"][e * PER_E + (SLOTS + m), :, :])\
                        .then_inc(landed[(AT_MOE + SLOTS + m) % SLOTS], 16)
            for m in range(PER_E - SLOTS):
                behind(NE - 1, m)
                sp.dma_start(slot(AT_MOE + SLOTS + m), A["moe"][(NE - 1) * PER_E + SLOTS + m, :, :])\
                    .then_inc(landed[(AT_MOE + SLOTS + m) % SLOTS], 16)
            sp.wait_ge(S("flag_ready"), 1)
            more = sp.value_load(flag[0:1, 0:1], min_val=0, max_val=1)
            with sp.If(more > 0):
                with sp.Fori(1, MAXPASS) as r:
                    with sp.Fori(0, NE) as e:
                        for m in range(PER_E):
                            back = m - SLOTS if m >= SLOTS else m - SLOTS + PER_E
                            sp.wait_ge(S(KINDS[back % 3]),
                                       (r * NE + e) * NCH + (back // 3 + 1 - (NCH if m < SLOTS else 0)))
                            sp.dma_start(slot(AT_MOE + m), A["moe"][e * PER_E + m, :, :])\
                                .then_inc(landed[(AT_MOE + m) % SLOTS], 16)

        @block.gpsimd
        def _(po):
            waits = []

            def store(dst, src, name):
                po.dma_start(dst, src).then_inc(S(name), 16)
                waits.append(name)

            for l in range(DEPTH):
                if l:
                    after(po, "z_mm", 0, 2)
                    after(po, "small_mm", 0, 2)
                    after(po, "gdn_done", 0, 1)
                po.dma_start(wsm[:], A["wsm"][l, :, :, :]).then_inc(S("smallw_in"), 16)
                po.dma_start(wgate[:], A["wgate"][l, :, :]).then_inc(S("smallw_in"), 16)
                if l:
                    after(po, "gdn_state_out", 0, 32)
                po.dma_start(SC, A["s_conv"][l, :, :, :, :]).then_inc(S("conv_in"), 16)
                po.dma_start(GSS[1], A["s_gla"][l, 1, :, :, :]).then_inc(S("gla_state_in"), 16)
                after(po, "conv_done", l, 1)
                store(O["conv"][l, :, :, :, :], OC, "conv_out")
                after(po, "gla_tr", l, 3)
                po.dma_start(GSS[0], A["s_gla"][l, 0, :, :, :]).then_inc(S("gla_state_in"), 16)
                after(po, "gla_state", l, 2)
                store(O["gla_p"][l, :, :, :], GS, "gla_out")
                for p in range(2):
                    after(po, "gla_sstate", l, p + 1)
                    store(O["gla_s"][l, p, :, :, :], GSS[p], "gla_out")
                after(po, "gla_out", l, 48)
                po.dma_start(DS, A["s_gdn"][l, :, :, :, :]).then_inc(S("gdn_state_in"), 16)
                after(po, "gdn_state", l, 2)
                store(O["gdn_p"][l, :, :, :], DSP, "gdn_state_out")
                after(po, "gdn_sstate", l, NH)
                store(O["gdn_s"][l, :, :, :, :], DS, "gdn_state_out")
            po.wait_ge(S("y_done"), 1)
            store(O["y"], hT[:], "y_out")
            for name in dict.fromkeys(waits):
                po.wait_ge(S(name), 16 * waits.count(name))

        @block.tensor
        def _(pe):
            def mm(out, lhsT, rhs, start=True, stop=True, **k):
                return pe.matmul(out, lhsT, rhs, start=start, stop=stop, **k)

            def sum_squares(tag):
                pe.wait_ge(S(f"sq_{tag[0]}"), tag[1])
                for k in range(KD):
                    ins = mm(B[0][:, 0:T], ones, hT[:, k, :], k == 0, k == KD - 1)
                ins.then_inc(S(f"ss_{tag[0]}"), 1)

            def finish_heads(tag):
                pe.wait_ge(S(f"sq_{tag[0]}"), tag[1])
                q = v3(QK, 4)
                for h in range(4):
                    ins = mm(B[0][32 * h:32 * h + 32, 0:T], ones[:, 0:32], q[:, h, :])
                ins.then_inc(S(f"ss_{tag[0]}"), 1)
                pe.wait_ge(S(f"rs_{tag[0]}"), tag[1])
                for h in range(4):
                    ins = mm(B[1 + h][:, 0:T], ident[:, 32 * h:32 * h + 1].to_broadcast([P, P]), rs[:, :])
                ins.then_inc(S(f"rsb_{tag[0]}"), 1)

            pe.wait_ge(S("const_in"), 64)
            pe.wait_ge(S("cs"), 1)
            for name in ("e_tr", "e_sc_mm"):
                pe.sem_inc(S(name), 1)
            with pe.Fori(0, N_ADA // SLOTS) as turn:
                for s in range(SLOTS):
                    pe.wait_ge(landed[s], turn * 16 + 16)
                    if s < 2:
                        pe.wait_ge(S("ada_done"), turn * SLOTS + 1)
                    else:
                        pe.wait_ge(S("ada_done"), turn * SLOTS + s)
                    wv = v3(slot(s), KD)
                    for j in range(4):
                        for k in range(KD):
                            ins = mm(B[s % 2][:, j * NC_:(j + 1) * NC_], wv[:, k, j * P:(j + 1) * P],
                                     csT[:, k * NC_:(k + 1) * NC_], k == 0, k == KD - 1)
                    ins.then_inc(S("ada_mm"), 1)

            for l in range(DEPTH):
                sum_squares(("norm", 2 * l + 1))
                pe.wait_ge(S("h_norm"), 2 * l + 1)
                after(pe, "smallw_in", l, 32)
                for k in range(KD):
                    ins = mm(B[2][0:LR, 0:T], wsm[:, k, 0:LR], hT[:, k, :], k == 0, k == KD - 1)
                ins.then_inc(S("small_mm"), 1)
                for i, (t0, nt) in enumerate(TILES):
                    for k in range(KD):
                        ins = mm(B[3][0:nt, 8 * i:8 * i + 8], hT[:, k, t0:t0 + nt], wsm[:, k, LR:],
                                 k == 0, k == KD - 1)
                ins.then_inc(S("small_mm"), 1)
                for u in range(4 * N_IN):
                    n = AT_IN[l] + u // 4
                    if u % 4 == 0:
                        piece_in(pe, n)
                    if u >= 2:
                        after(pe, "proj", l, u - 1)
                    wv = v3(slot(n), KD)
                    for k in range(KD):
                        ins = mm(B[u % 2][:, 0:T], wv[:, k, (u % 4) * P:(u % 4 + 1) * P], hT[:, k, :],
                                 k == 0, k == KD - 1)
                    ins.then_inc(S("proj_mm"), 1)
                    if u == 3:
                        after(pe, "lr_t", l, 1)
                        for p in range(2):
                            mm(B[4 + p][:, 0:T], wgate[:, p * P:(p + 1) * P], LRT).then_inc(S("z_mm"), 1)
                    if u == 7:
                        after(pe, "g", l, 1)
                        for i, (t0, nt) in enumerate(TILES):
                            tri, blk = (cst("tri"), ones) if i < 2 else (cst("tri_s", TS), cst("block", TS))
                            mm(B[6][0:nt, 4 * i:4 * i + 4], tri, gG[0:nt, 4 * i:4 * i + 4])
                            ins = mm(B[6][0:nt, 16 + 4 * i:20 + 4 * i], blk, gG[0:nt, 4 * i:4 * i + 4])
                        ins.then_inc(S("gam_mm"), 1)

                after(pe, "proj", l, 4 * N_IN)
                after(pe, "la", l, 1)
                after(pe, "gcols", l, 1)
                for i, (t0, nt) in enumerate(TILES):
                    for h in range(GH):
                        ins = pe.transpose(B[2][0:nt, h * P:(h + 1) * P], v13[:, h, t0:t0 + nt], ident)
                    ins.then_inc(S("gla_tr"), 1)
                    after(pe, "gla_ops", l, i + 1)
                    if i:
                        after(pe, "gla_tok", l, 2 * i)
                    for p in range(2):
                        ins = pe.transpose(B[3][0:nt, p * P:(p + 1) * P], GKE[:, p, 0:nt], ident)
                    ins.then_inc(S("gla_ktr"), 1)
                    if i < 2:
                        for h in range(GH):
                            lo, p = 64 * (h % 2), h // 2
                            for j, nj in enumerate(NJ):
                                s0 = SUB * j
                                ins = mm(GAB[h % 2][s0:s0 + SUB, p * P + s0:(p + 1) * P],
                                         GKT[lo:lo + 64, p, s0:s0 + SUB], GE[j][lo:lo + 64, p, :])
                    else:
                        for h in range(GH):
                            lo, p = 64 * (h % 2), h // 2
                            ins = mm(GAB[h % 2][0:TS, p * TS:(p + 1) * TS], GKT[lo:lo + 64, p, 0:TS], GQD[lo:lo + 64, p, 0:TS])
                    ins.then_inc(S("gla_at_mm"), 1)
                    after(pe, "gla_at", l, i + 1)
                    after(pe, "gla_tok", l, 2 * i + 2)
                    if i == 2:
                        after(pe, "gla_state_in", l, 32)
                    for h in range(GH):
                        lo, p = 64 * (h % 2), h // 2
                        o = GOB[h % 2][:, p * nt:(p + 1) * nt]
                        ins = mm(o, GVT[:, h * P:(h + 1) * P], GAT[:, h * nt:(h + 1) * nt], True, i != 1)
                        if i == 1:
                            ins = mm(o, GS[lo:lo + 64, p, :], GQD[lo:lo + 64, p, :], False, True)
                        if i == 2:
                            for s in range(NSEQ):
                                ins = mm(o[:, s * LSEQ:(s + 1) * LSEQ], GSS[p][lo:lo + 64, s, :],
                                         GQD[lo:lo + 64, p, s * LSEQ:(s + 1) * LSEQ], False, s == NSEQ - 1,
                                         skip_group_check=True)
                    ins.then_inc(S("gla_o_mm"), 1)
                    if i < 2:
                        for h in range(GH):
                            lo, p = 64 * (h % 2), h // 2
                            ins = mm(B[6][lo:lo + 64, p * P:(p + 1) * P], GKDT[:, p * P + lo:p * P + lo + 64],
                                     GVT[:, h * P:(h + 1) * P])
                        ins.then_inc(S("gla_s_mm"), 1)
                        after(pe, "gla_state", l, i + 1)
                    else:
                        for h in range(GH):
                            lo, p = 64 * (h % 2), h // 2
                            after(pe, "gla_vm", l, h + 1)
                            if h == 2:
                                after(pe, "gla_sstate", l, 1)
                            for c in range(2):
                                ins = mm(B[6 + c][lo:lo + 64, :], GKDT[0:TS, p * P + lo:p * P + lo + 64],
                                         GVM[0:TS, 4 * c:4 * c + 4, :])
                            ins.then_inc(S("gla_ss_mm"), 1)
                    after(pe, "gla_o", l, i + 1)
                finish_heads(("heads", 2 * l + 1))

                after(pe, "gla_fin", l, 1)
                for i, (t0, nt) in enumerate(TILES):
                    for b in range(3):
                        for h in range(NH):
                            ins = pe.transpose(B[b][0:nt, h * P:(h + 1) * P], cv3[:, 4 * b + h, t0:t0 + nt], ident)
                        ins.then_inc(S("dtr"), 1)
                    tri = cst("tri") if i < 2 else cst("tri_s", TS)
                    for h in range(NH):
                        ins = mm(B[3][:, h * nt:(h + 1) * nt],
                                 gG[0:nt, 4 * i + h:4 * i + h + 1].to_broadcast([nt, P]), tri)
                    ins.then_inc(S("drow"), 1)
                    for b, src in ((4, DT), (5, DU)):
                        after(pe, "dqk", l, 2 * i + b - 3)
                        for h in range(NH):
                            ins = pe.transpose(B[b][:, h * nt:(h + 1) * nt], src[0:nt, h * P:(h + 1) * P], ident[0:nt, 0:nt])
                        ins.then_inc(S("dtb"), 1)
                    after(pe, "dqkT", l, 2 * i + 2)
                    for b, r0 in ((6, 4), (7, 0)):
                        for h in range(NH):
                            kt = cv3[:, 4 + h, t0:t0 + nt]
                            ins = mm(B[b][0:nt, h * nt:(h + 1) * nt], kt, cv3[:, r0 + h, t0:t0 + nt])
                        ins.then_inc(S("dkk"), 1)
                    nlev = 7 if i < 2 else 3
                    base = 14 * i
                    for v in range(nlev):
                        for hs in range(2):
                            after(pe, "dmb", l, base + 2 * v + hs + 1)
                            after(pe, "dtu", l, base + 2 * v + hs + 1 + 2 * i)
                            for h in (2 * hs, 2 * hs + 1):
                                c = slice(h * nt, (h + 1) * nt)
                                ins = mm(B[hs][0:nt, (h % 2) * nt:(h % 2 + 1) * nt], DMB[0:nt, c], DU[0:nt, c])
                            ins.then_inc(S("dy_mm"), 1)
                        for hs in range(2):
                            after(pe, "dy", l, base + 2 * v + hs + 1)
                            for h in (2 * hs, 2 * hs + 1):
                                c = slice(h * nt, (h + 1) * nt)
                                o = (h % 2) * nt
                                ins = mm(B[2 + 2 * hs][0:nt, o:o + nt], DT[0:nt, c], DY[0:nt, c])
                            for h in (2 * hs, 2 * hs + 1):
                                c = slice(h * nt, (h + 1) * nt)
                                o = (h % 2) * nt
                                ins = mm(B[2 + 2 * hs][0:nt, 256 + o:256 + o + nt], DY[0:nt, c], DT[0:nt, c])
                            ins.then_inc(S("dtu_mm"), 1)
                    after(pe, "dtu", l, base + 2 * nlev + 2 * (i + 1))
                    for h in range(NH):
                        ins = mm(B[5][:, h * nt:(h + 1) * nt], DKB[0:nt, h * P:(h + 1) * P], DU[0:nt, h * nt:(h + 1) * nt])
                    ins.then_inc(S("dw_mm"), 1)
                    if i < 2:
                        after(pe, "dw", l, i + 1)
                    else:
                        after(pe, "gdn_state_in", l, 16)
                    for h in range(NH):
                        o = B[6][0:nt, h * P:(h + 1) * P]
                        ins = mm(o, DU[0:nt, h * nt:(h + 1) * nt], DVB[0:nt, h * P:(h + 1) * P], True, i == 0)
                        if i == 1:
                            ins = mm(o, DMB[:, h * nt:(h + 1) * nt], DSP[:, h, :], False, True)
                        if i == 2:
                            after(pe, "dwm", l, h + 1)
                            wm = (DM, DT)[h % 2]
                            for s in range(NSEQ):
                                ins = mm(o, wm[:, s * TS:(s + 1) * TS], DS[:, h, s, :], False, s == NSEQ - 1)
                            if h < NH - 1:
                                ins.then_inc(S("dvn_part"), 1)
                    ins.then_inc(S("dvn_mm"), 1)
                    after(pe, "dvn", l, i + 1)
                    after(pe, "dqd", l, i + 1)
                    for h in range(NH):
                        o = B[7][:, h * nt:(h + 1) * nt]
                        ins = mm(o, DY2[0:nt, h * P:(h + 1) * P], cv3[0:nt, 8 + h, t0:t0 + nt], True, i != 1)
                        if i == 1:
                            ins = mm(o, DSP[:, h, :], cv3[:, h, t0:t0 + nt], False, True)
                        if i == 2:
                            for s in range(NSEQ):
                                ins = mm(o[:, s * LSEQ:(s + 1) * LSEQ], DS[:, h, s, :],
                                         cv3[:, h, t0 + s * LSEQ:t0 + (s + 1) * LSEQ], False, s == NSEQ - 1,
                                         skip_group_check=True)
                    ins.then_inc(S("do_mm"), 1)
                    if i < 2:
                        for h in range(NH):
                            ins = mm(B[3][:, h * P:(h + 1) * P], DKD[:, h * P:(h + 1) * P], DY2[:, h * P:(h + 1) * P])
                        ins.then_inc(S("ds_mm"), 1)
                        after(pe, "gdn_state", l, i + 1)
                    else:
                        for h in range(NH):
                            after(pe, "dvm", l, h + 1)
                            if h >= 1:
                                after(pe, "gdn_sstate", l, h)
                            vm = (D01, D34)[h % 2]
                            for c in range(2):
                                ins = mm(B[3 + c][:, :], DKD[0:TS, h * P:(h + 1) * P], vm[0:TS, 512 * c:512 * c + 512])
                            ins.then_inc(S("dss_mm"), 1)
                    after(pe, "do", l, i + 1)
                finish_heads(("heads", 2 * l + 2))

                after(pe, "gdn_fin", l, 1)
                for j in range(KD):
                    n = AT_OUT[l] + j // 4
                    piece_in(pe, n)
                    if j >= 2:
                        after(pe, "x_mix", l, j - 1)
                    wv = v3(slot(n), KD)
                    for k in range(KD):
                        ins = mm(B[5 + j % 2][:, 0:T], wv[:, k, (j % 4) * P:(j % 4 + 1) * P], hT[:, k, :],
                                 k == 0, k == KD - 1)
                    ins.then_inc(S("out_mm"), 1)
                sum_squares(("norm", 2 * l + 2))
                pe.wait_ge(S("h_norm"), 2 * l + 2)
                if l == 0:
                    for u in range(FD):
                        n = AT_GU + u // 2
                        if u % 2 == 0:
                            piece_in(pe, n)
                        if u >= 2:
                            pe.wait_ge(S("ff_act"), u - 1)
                        wv = v3(slot(n), KD)
                        for b in range(2):
                            c0 = 256 * b + (u % 2) * P
                            for k in range(KD):
                                ins = mm(B[2 * b + u % 2][:, 0:T], wv[:, k, c0:c0 + P], hT[:, k, :], k == 0, k == KD - 1)
                        ins.then_inc(S("gu_mm"), 1)
                    pe.wait_ge(S("ff_act"), FD)
                    for j in range(KD):
                        n = AT_DN + j
                        piece_in(pe, n)
                        if j >= 2:
                            pe.wait_ge(S("x_ff"), j - 1)
                        wv = v3(slot(n)[:, 0:FD * P], FD)
                        for k in range(FD):
                            ins = mm(B[4 + j % 2][:, 0:T], wv[:, k, :], FA[:, k, :], k == 0, k == FD - 1)
                        ins.then_inc(S("down_mm"), 1)

            for i, (t0, nt) in enumerate(TILES):
                for k in range(KD):
                    ins = mm(B[0][0:nt, NE * i:NE * (i + 1)], hT[:, k, t0:t0 + nt], wrt[:, k, :], k == 0, k == KD - 1)
            ins.then_inc(S("logits_mm"), 1)
            for i, (t0, nt) in enumerate(TILES):
                for c in range(2):
                    u = 2 * i + c
                    if u >= 2:
                        pe.wait_ge(S("htok"), u - 1)
                    for k in range(4):
                        ins = pe.transpose(B[2 + u % 2][0:nt, k * P:(k + 1) * P], hT[:, 4 * c + k, t0:t0 + nt], ident)
                    ins.then_inc(S("htok_tr"), 1)
            pe.wait_ge(S("sel"), 1)
            for i in range(3):
                for j in range(i + 1):
                    rows = TILES[j][1]
                    m = TILES[i][1]
                    lhsT = cst("strict", rows)[:, 0:m] if j == i else ones[0:rows, 0:m]
                    mm(B[1][0:m, NE * i:NE * (i + 1)], lhsT, sel[0:rows, NE * j:NE * (j + 1)], j == 0, j == i)
            for j in range(3):
                rows = TILES[j][1]
                ins = mm(B[1][:, 32:32 + NE], ones[0:rows, :], sel[0:rows, NE * j:NE * (j + 1)], j == 0, j == 2)
            ins.then_inc(S("pos_mm"), 1)
            pe.wait_ge(S("htok"), 6)

            def expert(el, r):
                pe.wait_ge(S("onehot"), el + r + 1)
                pe.wait_ge(S("e_scatter"), el * KD + 1)
                for c in range(2):
                    for k in range(4):
                        for i, (t0, nt) in enumerate(TILES):
                            ins = mm(B[4 + c][:, k * P:(k + 1) * P],
                                     HTOK[0:nt, i, (4 * c + k) * P:(4 * c + k + 1) * P], ONEH[0:nt, i, :], i == 0, i == 2)
                    ins.then_inc(S("e_gather_mm"), 1)
                pe.wait_ge(S("e_act"), el * NCH + 1)
                for i, (t0, nt) in enumerate(TILES):
                    ins = pe.transpose(B[0][:, t0:t0 + nt], ONEW[0:nt, i, :], ident[0:nt, 0:nt])
                ins.then_inc(S("e_wT_mm"), 1)
                pe.wait_ge(S("e_in"), el * 3 + 3)

                def turn_act(c):
                    pe.wait_ge(S("e_act"), el * NCH + (c + 2))
                    for a in range(4):
                        ins = pe.transpose(B[4 + c % 2][:, a * P:(a + 1) * P], EA[:, c % 2, a * P:(a + 1) * P], ident)
                    ins.then_inc(S("e_tr"), 1)

                def down(c):
                    m = 3 * c + 2
                    pe.wait_ge(landed[(AT_MOE + m) % SLOTS], el * (16 * PER_E // SLOTS) + 16 * ((AT_MOE + m) // SLOTS + 1))
                    pe.wait_ge(S("e_actT"), el * NCH + (c + 1))
                    if c == 0:
                        pe.wait_ge(S("e_y"), el + 1)
                    wv = v3(slot(AT_MOE + m), 4)
                    for a in range(4):
                        for b in range(2):
                            ins = mm(B[6 + b][:, :], EAT[:, c % 2, a * P:(a + 1) * P], wv[:, a, 512 * b:512 * b + 512],
                                     c == 0 and a == 0, c == NCH - 1 and a == 3)
                    ins.then_inc(S("e_down_mm"), 1)

                for c in range(NCH):
                    for b, name in ((0, "e_gate_mm"), (1, "e_up_mm")):
                        m = 3 * c + b
                        pe.wait_ge(landed[(AT_MOE + m) % SLOTS], el * (16 * PER_E // SLOTS) + 16 * ((AT_MOE + m) // SLOTS + 1))
                        if b == 0 and c >= 2:
                            pe.wait_ge(S("e_act"), el * NCH + c)
                        if b == 1 and c >= 1:
                            turn_act(c - 1)
                        wv = v3(slot(AT_MOE + m), KD)
                        for k in range(KD):
                            ins = mm(B[2 * b + c % 2][:, :], HG[:, k, :], wv[:, k, :], k == 0, k == KD - 1)
                        ins.then_inc(S(name), 1)
                    if c >= 1:
                        down(c - 1)
                turn_act(NCH - 1)
                down(NCH - 1)
                pe.wait_ge(S("e_y"), el + 2)
                for j in range(KD):
                    if j >= 2:
                        pe.wait_ge(S("e_scatter"), el * KD + j)
                    mm(B[4 + j % 2][:, 0:T], YE[:, j * P:(j + 1) * P], ONEWT).then_inc(S("e_sc_mm"), 1)

            with pe.Fori(0, NE) as e:
                expert(e, 0)
            more = pe.value_load(flag[0:1, 0:1], min_val=0, max_val=1)
            with pe.If(more > 0):
                with pe.Fori(1, MAXPASS) as r:
                    with pe.Fori(0, NE) as e:
                        expert(r * NE + e, r)
            sum_squares(("norm", 5))

        @block.scalar
        def _(ac):
            own = Own(ac, "act_own")

            def act(out, in_, func, **k):
                return ac.activation(out, in_, func, **k)

            def rsqrt_seed(tag, x=None, y=None):
                x = rv[:, :] if x is None else x
                y = rs[:, :] if y is None else y
                ac.wait_ge(S(f"var_{tag[0]}"), tag[1])
                own.do(act(y, x, ACT.Ln))
                act(y, y, ACT.Exp, scale=-0.5).then_inc(S(f"rs0_{tag[0]}"), 1)

            def finish_heads(tag, gate):
                rsqrt_seed(tag)
                act(QK, gate, ACT.Exp, scale=-1.0).then_inc(S(f"ge_{tag[0]}"), 1)

            ac.sem_inc(S("e_y"), 1)
            ac.wait_ge(S("const_in"), 64)
            act(csT[:, :], col("c"), ACT.Exp, scale=-1.0).then_inc(S("cs_e"), 1)
            for l in range(DEPTH):
                rsqrt_seed(("norm", 2 * l + 1))
                after(ac, "small_mm", l, 1)
                act(LRT, B[2][0:LR, 0:T], ACT.Copy).then_inc(S("lr_t"), 1)
                after(ac, "gx", l, 1)
                own.do(act(gL[:, :], gX[:, :], ACT.Abs))
                own.do(act(gL[:, :], gL[:, :], ACT.Exp, scale=-1.0))
                act(gL[:, :], gL[:, :], ACT.Ln, bias=1.0)
                act(gEA[:, :], col(f"alog{l}"), ACT.Exp)
                act(v3(gEB[:, :], 3), v3(gAB[:, :], 3)[:, :, NH:2 * NH], ACT.Exp, scale=-1.0).then_inc(S("gact"), 1)
                dest = [None] * CT + [qk3[:, j, :] for j in range(4)] + [v13[:, j, :] for j in range(4)]\
                    + [g13[:, j, :] for j in range(4)] + [zt3[:, j, :] for j in range(4)]

                def conv_exp(c):
                    after(ac, "cv_raw", l, c + 1)
                    if c >= 2:
                        after(ac, "cv", l, c - 1)
                    act(CE[:, c % 2, :], cv3[:, c, :], ACT.Exp, scale=-1.0).then_inc(S("cv_e"), 1)

                for u in range(4 * N_IN):
                    after(ac, "proj_mm", l, u + 1)
                    if u < CT:
                        if u >= 4:
                            after(ac, "cv_raw", l, u - 3)
                        if u == 0:
                            after(ac, "xp_ready", l, 1)
                        act(XP[:, u % 4, CW - 1:], B[u % 2][:, 0:TP], ACT.Copy)
                        act(XS[:, u % 4, :, CW - 1:], v3(B[u % 2][:, TP:T], NSEQ), ACT.Copy).then_inc(S("proj"), 1)
                    else:
                        act(dest[u], B[u % 2][:, 0:T], ACT.Copy).then_inc(S("proj"), 1)
                    if 1 <= u <= CT:
                        conv_exp(u - 1)
                    if u == 5:
                        after(ac, "zb", l, 1)
                        own.do(act(LAE, w(R, 2 * T), ACT.Abs))
                        own.do(act(LAE, LAE, ACT.Exp, scale=-1.0))
                        act(LAE, LAE, ACT.Ln, bias=1.0).then_inc(S("zl"), 1)
                    if u == 9:
                        after(ac, "gamc", l, 1)
                        act(gEG[:, :], gGC[:, :], ACT.Exp)
                        act(gDK[:, :], gD[:, :], ACT.Exp).then_inc(S("gexp"), 1)

                for i, (t0, nt) in enumerate(TILES):
                    la = LA[:, :, t0:t0 + nt]
                    after(ac, "gla_arg", l, i + 1)
                    if i < 2:
                        act(GEA, GEA, ACT.Exp)
                        act(GKT[:, :, 0:nt], GKT[:, :, 0:nt], ACT.Exp)
                    else:
                        act(GKT[:, :, 0:nt], la, ACT.Exp, scale=-1.0)
                    act(GKE[:, :, 0:nt], GKE[:, :, 0:nt], ACT.Exp)
                    act(GQD[:, :, 0:nt], la, ACT.Exp).then_inc(S("gla_exp"), 1)
                    after(ac, "gla_tr", l, i + 1)
                    act(GVT[0:nt, :], B[2][0:nt, :], ACT.Copy).then_inc(S("gla_tok"), 1)
                    after(ac, "gla_ktr", l, i + 1)
                    act(GKDT[0:nt, :], B[3][0:nt, 0:256], ACT.Copy).then_inc(S("gla_tok"), 1)
                    after(ac, "gla_o_mm", l, i + 1)
                    act(hT[:, 0:GH:2, t0:t0 + nt], v3(GOB[0][:, 0:2 * nt], 2), ACT.Copy)
                    act(hT[:, 1:GH:2, t0:t0 + nt], v3(GOB[1][:, 0:2 * nt], 2), ACT.Copy).then_inc(S("gla_o"), 1)
                finish_heads(("heads", 2 * l + 1), G1)

                after(ac, "gla_out", l, 48)
                after(ac, "gla_fin", l, 1)
                for i, (t0, nt) in enumerate(TILES):
                    n4 = 4 * nt
                    for b, dst in ((0, DM), (1, DMB)):
                        after(ac, "dtr", l, 3 * i + b + 1)
                        if i and b == 0:
                            after(ac, "gdn_state", l, i)
                        act(dst[0:nt, :], B[b][0:nt, :], ACT.Square).then_inc(S("dsq"), 1)
                    rsqrt_seed(("qk", 3 * l + i + 1), rv8[0:nt, :], rs8[0:nt, :])
                    after(ac, "dlog", l, i + 1)
                    own.go(act(DX[0:nt, 0:n4], DX[0:nt, 0:n4], ACT.Exp))
                    act(DY[0:nt, 0:n4], DY[0:nt, 0:n4], ACT.Exp).then_inc(S("dmask"), 1)
                    for b, r0 in ((4, 0), (5, 4)):
                        after(ac, "dtb", l, 2 * i + b - 3)
                        act(cv3[:, r0:r0 + 4, t0:t0 + nt], v3(B[b][:, 0:n4], 4), ACT.Copy).then_inc(S("dqkT"), 1)
                    after(ac, "dat", l, i + 1)
                    act(DX[:, 0:n4], B[3][:, 0:n4], ACT.Exp).then_inc(S("drowe"), 1)
                    for v in range(7 if i < 2 else 3):
                        for hs in range(2):
                            after(ac, "dy_mm", l, 14 * i + 2 * v + hs + 1)
                            act(DY[0:nt, 2 * hs * nt:(2 * hs + 2) * nt], B[hs][0:nt, 0:2 * nt], ACT.Copy).then_inc(S("dy"), 1)
                    after(ac, "dw_mm", l, i + 1)
                    act(DMB[:, 0:n4], B[5][:, 0:n4], ACT.Copy, scale=-1.0).then_inc(S("dw"), 1)
                    after(ac, "dvn_mm", l, i + 1)
                    act(DY[0:nt, :], B[6][0:nt, :], ACT.Copy).then_inc(S("dvn"), 1)
                    after(ac, "do_mm", l, i + 1)
                    act(hT[:, GH:, t0:t0 + nt], v3(B[7][:, 0:n4], 4), ACT.Copy).then_inc(S("do"), 1)
                finish_heads(("heads", 2 * l + 2), ZT)
                rsqrt_seed(("norm", 2 * l + 2))
                if l == 0:
                    for u in range(FD):
                        ac.wait_ge(S("gu_mm"), u + 1)
                        if u >= 2:
                            ac.wait_ge(S("ff_act"), u - 1)
                        act(FSG[u % 2], B[u % 2][:, 0:T], ACT.Exp, scale=-1.0).then_inc(S("ff_e"), 1)

            ac.wait_ge(S("lg_shift"), 1)
            act(lgE[:, :], lgE[:, :], ACT.Exp).then_inc(S("lg_exp"), 1)
            for u in range(6):
                i, c = u // 2, u % 2
                nt = TILES[i][1]
                ac.wait_ge(S("htok_tr"), u + 1)
                act(HTOK[0:nt, i, 512 * c:512 * c + 512], B[2 + c][0:nt, :], ACT.Copy).then_inc(S("htok"), 1)

            def expert(el, r):
                for c in range(2):
                    ac.wait_ge(S("e_gather_mm"), el * 2 + (c + 1))
                    act(HG[:, 4 * c:4 * c + 4, :], v3(B[4 + c][:, :], 4), ACT.Copy).then_inc(S("e_in"), 1)
                ac.wait_ge(S("e_wT_mm"), el + 1)
                act(ONEWT, B[0][:, 0:T], ACT.Copy).then_inc(S("e_in"), 1)

                def turned(c):
                    ac.wait_ge(S("e_tr"), el * NCH + (c + 2))
                    act(EAT[:, c % 2, :], B[4 + c % 2][:, :], ACT.Copy).then_inc(S("e_actT"), 1)

                for c in range(NCH):
                    ac.wait_ge(S("e_gate_mm"), el * NCH + (c + 1))
                    ac.wait_ge(S("e_act"), el * NCH + (c if c else 1))
                    act(EE[:, c % 2, :], B[c % 2][:, :], ACT.Exp, scale=-1.0).then_inc(S("e_exp"), 1)
                    if c:
                        turned(c - 1)
                turned(NCH - 1)
                ac.wait_ge(S("e_down_mm"), el * NCH + NCH)
                ac.wait_ge(S("e_sc_mm"), el * KD + 1)
                act(YE[:, 0:512], B[6][:, :], ACT.Copy)
                act(YE[:, 512:], B[7][:, :], ACT.Copy).then_inc(S("e_y"), 1)

            with ac.Fori(0, NE) as e:
                expert(e, 0)
            more = ac.value_load(flag[0:1, 0:1], min_val=0, max_val=1)
            with ac.If(more > 0):
                with ac.Fori(1, MAXPASS) as r:
                    with ac.Fori(0, NE) as e:
                        expert(r * NE + e, r)
            rsqrt_seed(("norm", 5))

        @block.vector
        def _(ve):
            own = Own(ve, "vec_own")
            do, go = own.do, own.go
            tt, ts, stt, cp = ve.tensor_tensor, ve.tensor_scalar, ve.scalar_tensor_tensor, ve.tensor_copy

            def refine(tag, y, v, t):
                ve.wait_ge(S(f"rs0_{tag[0]}"), tag[1])
                do(tt(t, y, y, ALU.mult))
                do(stt(t, t, -0.5, v, ALU.mult, ALU.mult))
                do(stt(y, t, 1.5, y, ALU.add, ALU.mult))

            def norm(tag, shift, scale):
                do(tt(hT[:, :, :], xT[:, :, :], xT[:, :, :], ALU.mult), f"sq_{tag[0]}")
                ve.wait_ge(S(f"ss_{tag[0]}"), tag[1])
                do(ts(rv[:, :], B[0][:, 0:T], 1.0 / D, EPS, ALU.mult, ALU.add), f"var_{tag[0]}")
                refine(tag, rs[:, :], rv[:, :], rt[:, :])
                do(tt(hT[:, :, :], xT[:, :, :], mid(rs[:, :], KD), ALU.mult))
                A_, B_ = md(scale), md(shift)
                for k in range(KD):
                    go(ts(hT[:, k, 0:TP], hT[:, k, 0:TP], A_[:, k, 0:1], B_[:, k, 0:1], ALU.mult, ALU.add))
                hs = hT[:, :, TP:].rearrange("p k (s u) -> p k s u", s=NSEQ)
                do(tt(hs, hs, last(A_[:, :, 1:], LSEQ), ALU.mult))
                do(tt(hs, hs, last(B_[:, :, 1:], LSEQ), ALU.add), f"h_{tag[0]}")

            def finish_heads(tag, h0, gate, weight, done):
                o = hT[:, h0:h0 + 4, :]
                do(tt(v3(QK, 4), o, o, ALU.mult), f"sq_{tag[0]}")
                ve.wait_ge(S(f"ss_{tag[0]}"), tag[1])
                do(ts(rv[:, :], B[0][:, 0:T], 1.0 / GV, EPS, ALU.mult, ALU.add), f"var_{tag[0]}")
                refine(tag, rs[:, :], rv[:, :], rt[:, :])
                go(cp(rt[:, 0:1], rs[:, 0:1]), f"rs_{tag[0]}")
                ve.wait_ge(S(f"ge_{tag[0]}"), tag[1])
                do(ts(QK, QK, 1.0, None, ALU.add))
                do(ve.reciprocal(QK, QK))
                do(stt(gate, gate, weight, QK, ALU.mult, ALU.mult))
                do(tt(o, o, v3(gate, 4), ALU.mult))
                ve.wait_ge(S(f"rsb_{tag[0]}"), tag[1])
                for h in range(3):
                    go(tt(o[:, h, :], o[:, h, :], B[1 + h][:, 0:T], ALU.mult))
                do(tt(o[:, 3, :], o[:, 3, :], B[4][:, 0:T], ALU.mult), done)

            def residual(bank, j, gt, name):
                do(stt(xT[:, j, 0:TP], bank[:, 0:TP], md(gt)[:, j, 0:1], xT[:, j, 0:TP], ALU.mult, ALU.add))
                xs = v3(xT[:, j, TP:], NSEQ)
                do(tt(v3(rt[:, 0:TS], NSEQ), v3(bank[:, TP:T], NSEQ), last(md(gt)[:, j, 1:], LSEQ), ALU.mult))
                do(tt(xs, xs, v3(rt[:, 0:TS], NSEQ), ALU.add), name)

            for name in ("ada_done", "e_act", "e_scatter"):
                ve.sem_inc(S(name), 1)
            ve.memset(gAB[:, :], 0.0)
            ve.wait_ge(S("const_in"), 64)
            ve.tensor_copy(cb[:, :], W[:, 0:N_CB])
            ve.memset(gGC[:, :], 0.0)
            ve.memset(lgE[:, :], 0.0)
            do(ve.memset(gGL[:, :], 0.0))
            ve.wait_ge(S("cs_e"), 1)
            do(ts(csT[:, :], csT[:, :], 1.0, None, ALU.add))
            do(ve.reciprocal(csT[:, :], csT[:, :]))
            do(tt(csT[:, :], csT[:, :], col("c"), ALU.mult), "cs")
            bada = col("b_ada")
            with ve.Fori(0, N_ADA // SLOTS) as turn:
                for s in range(SLOTS):
                    ve.wait_ge(S("ada_mm"), turn * SLOTS + (s + 1))
                    tile = (turn * SLOTS + s) * 4
                    tt(mod[:, bass.ds(tile, 4), :], v3(B[s % 2][:, 0:4 * NC_], 4),
                       last(bada[:, bass.ds(tile, 4)], NC_), ALU.add).then_inc(S("ada_done"), 1)
            ve.wait_ge(S("ada_done"), N_ADA + 1)
            for name, t in (("nm0", 8), ("nf0", 32), ("nm1", 56), ("nf1", 80), ("nfin", 104)):
                go(stt(md(t), md(t), 1.0, last(col(name), NC_), ALU.add, ALU.mult))
            ve.wait_ge(S("x_in"), 16)
            ve.wait_ge(S("vec_own"), own.n["vec_own"])

            for l in range(DEPTH):
                m0 = 48 * l
                norm(("norm", 2 * l + 1), m0, m0 + 8)
                after(ve, "small_mm", l, 2)
                go(cp(gAB[:, 0:16], B[3][:, 0:16]))
                do(cp(gAB[0:TS, 16:24], B[3][0:TS, 16:24]))
                ab = v3(gAB[:, :], 3)
                do(tt(v3(gX[:, :], 3), ab[:, :, 0:NH], mid(col(f"dtb{l}"), 3), ALU.add), "gx")
                after(ve, "gact", l, 1)
                do(stt(gX[:, :], gX[:, :], 0.0, gL[:, :], ALU.max, ALU.add))
                do(stt(v3(gG[:, :], 3), v3(gX[:, :], 3), -1.0, mid(gEA[:, :], 3), ALU.mult, ALU.mult), "g")
                do(ts(gBE[:, :], gEB[:, :], 1.0, None, ALU.add))
                do(ve.reciprocal(gBE[:, :], gBE[:, :]))
                do(ve.memset(XP[:, :, 0:CW - 1], 0.0), "xp_ready")
                after(ve, "conv_in", l, 16)
                wc = v3(col(f"wconv{l}"), CT)

                def silu_tile(c):
                    after(ve, "cv_e", l, c + 1)
                    e = CE[:, c % 2, :]
                    do(ts(e, e, 1.0, None, ALU.add))
                    do(ve.reciprocal(e, e))
                    do(tt(cv3[:, c, :], cv3[:, c, :], e, ALU.mult), "cv")

                for c in range(CT):
                    s = c % 4
                    after(ve, "proj", l, c + 1)
                    do(cp(XS[:, s, :, 0:CW - 1], SC[:, c, :, :]))
                    xs, ys, yp = XS[:, s, :, :], v3(cv3[:, c, TP:], NSEQ), cv3[:, c, 0:TP]
                    go(ts(yp, XP[:, s, 0:TP], wc[:, c, 0:1], None, ALU.mult))
                    do(ts(ys, xs[:, :, 0:LSEQ], wc[:, c, 0:1], None, ALU.mult))
                    for j in range(1, CW):
                        go(stt(yp, XP[:, s, j:j + TP], wc[:, c, j:j + 1], yp, ALU.mult, ALU.add))
                        do(stt(ys, xs[:, :, j:j + LSEQ], wc[:, c, j:j + 1], ys, ALU.mult, ALU.add))
                    go(cp(OC[:, c, 0, :], XP[:, s, TP:TP + 3]))
                    do(cp(OC[:, c, 1:, :], xs[:, :, LSEQ:LSEQ + 3]), "cv_raw")
                    if c >= 1:
                        silu_tile(c - 1)
                    if c == 4:
                        after(ve, "z_mm", l, 2)
                        go(ts(LA[:, 0, :], B[4][:, 0:T], col(f"bg{l}")[:, 0:1], None, ALU.add))
                        do(ts(LA[:, 1, :], B[5][:, 0:T], col(f"bg{l}")[:, 1:2], None, ALU.add), "zb")
                    if c == 6:
                        after(ve, "zl", l, 1)
                        la = w(R, 2 * T)
                        do(stt(la, la, 0.0, LAE, ALU.min, ALU.subtract))
                        do(ts(la, la, 1.0 / GATE_NORM, None, ALU.mult))
                        for p in range(2):
                            go(ve.tensor_tensor_scan(LAE[:, p * T:(p + 1) * T], cbf("reset"), LA[:, p, :], 0.0, ALU.mult, ALU.add))
                        ve.wait_ge(S("vec_own"), own.n["vec_own"])
                        do(cp(la, LAE), "la")
                    if c == 8:
                        after(ve, "gam_mm", l, 1)
                        for i, (t0, nt) in enumerate(TILES):
                            go(cp(gGC[0:nt, 4 * i:4 * i + 4], B[6][0:nt, 4 * i:4 * i + 4]))
                            do(cp(gGL[0:nt, 4 * i:4 * i + 4], B[6][0:nt, 16 + 4 * i:20 + 4 * i]))
                        do(tt(gD[:, :], gGL[:, :], gGC[:, :], ALU.subtract), "gamc")
                    if c == 10:
                        after(ve, "gexp", l, 1)
                        do(tt(gBG[:, :], gBE[:, :], gEG[:, :], ALU.mult), "gcols")
                silu_tile(CT - 1)
                go(cp(rt[:, 0:1], rs[:, 0:1]), "conv_done")

                after(ve, "proj", l, 4 * N_IN)
                after(ve, "conv_out", l, 16)
                for i, (t0, nt) in enumerate(TILES):
                    la = LA[:, :, t0:t0 + nt]
                    q, k = qk3[:, 0:2, t0:t0 + nt], qk3[:, 2:4, t0:t0 + nt]
                    if i:
                        after(ve, "gla_o_mm", l, i)
                        after(ve, "gla_s_mm", l, i)
                    if i < 2:
                        for j, nj in enumerate(NJ):
                            mid_j = LA[:, :, t0 + SUB * j + SUB // 2 - 1]
                            go(tt(GE[j], LA[:, :, t0 + SUB * j:t0 + nt], last(mid_j, nj), ALU.subtract))
                            go(tt(GKT[:, :, SUB * j:SUB * j + SUB], last(mid_j, SUB),
                                  LA[:, :, t0 + SUB * j:t0 + SUB * j + SUB], ALU.subtract))
                        do(tt(GKE, last(LA[:, :, t0 + nt - 1], nt), la, ALU.subtract), "gla_arg")
                    else:
                        for p in range(2):
                            seq = v3(LA[:, p, t0:t0 + nt], NSEQ)
                            ins = tt(v3(GKE[:, p, 0:nt], NSEQ), last(seq[:, :, LSEQ - 1], LSEQ), seq, ALU.subtract)
                            go(ins) if p == 0 else do(ins, "gla_arg")
                    after(ve, "gla_exp", l, i + 1)
                    if i < 2:
                        go(cp(gEB_[:, 0:2], GQD[:, :, P - 1]))
                        for j, nj in enumerate(NJ):
                            go(stt(GE[j], GE[j], GK ** -0.5, qk3[:, 0:2, t0 + SUB * j:t0 + nt], ALU.mult, ALU.mult))
                    else:
                        go(cp(v3(gEB_[:, :], 2), GQD[:, :, LSEQ - 1:TS:LSEQ]))
                    ve.wait_ge(S("vec_own"), own.n["vec_own"])
                    go(tt(GKT[:, :, 0:nt], GKT[:, :, 0:nt], k, ALU.mult))
                    go(tt(GKE[:, :, 0:nt], GKE[:, :, 0:nt], k, ALU.mult))
                    do(stt(GQD[:, :, 0:nt], GQD[:, :, 0:nt], GK ** -0.5, q, ALU.mult, ALU.mult), "gla_ops")
                    after(ve, "gla_at_mm", l, i + 1)
                    if i == 0:
                        do(ve.memset(GAT, 0.0))
                    if i < 2:
                        for j, nj in enumerate(NJ):
                            r0 = SUB * j
                            for e in range(2):
                                ins = tt(v3(GAT, 4)[r0:r0 + SUB, e::2, r0:], v3(GAB[e][:, 0:256], 2)[r0:r0 + SUB, :, r0:],
                                         mid(cst("tri")[r0:r0 + SUB, r0:], 2), ALU.mult)
                                go(ins) if (j, e) != (len(NJ) - 1, 1) else do(ins, "gla_at")
                    else:
                        do(ve.memset(GAT[TS:, 0:4 * TS], 0.0))
                        for e in range(2):
                            ins = tt(v3(GAT[0:TS, 0:4 * TS], 4)[:, e::2, :], v3(GAB[e][0:TS, 0:2 * TS], 2),
                                     mid(cst("tri_s", TS), 2), ALU.mult)
                            go(ins) if e == 0 else do(ins, "gla_at")
                    if i == 0:
                        after(ve, "gla_s_mm", l, 1)
                        do(cp(GS, v3(B[6][:, 0:256], 2)), "gla_state")
                    elif i == 1:
                        after(ve, "gla_s_mm", l, 2)
                        go(stt(GS[:, 0, :], GS[:, 0, :], gEB_[:, 0:1], B[6][:, 0:P], ALU.mult, ALU.add))
                        do(stt(GS[:, 1, :], GS[:, 1, :], gEB_[:, 1:2], B[6][:, P:2 * P], ALU.mult, ALU.add), "gla_state")
                    else:
                        eb = v3(gEB_[:, :], 2)
                        after(ve, "gla_tok", l, 6)
                        for h in range(GH):
                            if h:
                                after(ve, "gla_ss_mm", l, h)
                            if h == 2:
                                for c in range(2):
                                    ins = tt(GSS[0][:, 4 * c:4 * c + 4, :], GSS[0][:, 4 * c:4 * c + 4, :], v3(B[6 + c][:, :], 4), ALU.add)
                                    go(ins) if c == 0 else do(ins, "gla_sstate")
                            do(tt(GVM[0:TS, :, :], mid(GVT[0:TS, h * P:(h + 1) * P], NSEQ), last(cst("seq", TS), GV), ALU.mult), "gla_vm")
                            if h == 0:
                                after(ve, "gla_o_mm", l, 3)
                                for p in range(2):
                                    do(tt(GSS[p], GSS[p], last(eb[:, p, :], GV), ALU.mult))
                        after(ve, "gla_ss_mm", l, GH)
                        for c in range(2):
                            ins = tt(GSS[1][:, 4 * c:4 * c + 4, :], GSS[1][:, 4 * c:4 * c + 4, :], v3(B[6 + c][:, :], 4), ALU.add)
                            go(ins) if c == 0 else do(ins, "gla_sstate")
                after(ve, "gla_o", l, 3)
                finish_heads(("heads", 2 * l + 1), 0, G1, col(f"glan{l}"), "gla_fin")

                after(ve, "gla_out", l, 48)
                for i, (t0, nt) in enumerate(TILES):
                    n4 = 4 * nt
                    gc = gGC[0:nt, 4 * i:4 * i + 4]
                    after(ve, "dsq", l, 2 * i + 2)
                    go(ve.tensor_reduce(rv8[0:nt, 0:4], v3(DM[0:nt, :], 4), AX.X, ALU.add))
                    do(ve.tensor_reduce(rv8[0:nt, 4:8], v3(DMB[0:nt, :], 4), AX.X, ALU.add))
                    do(ts(rv8[0:nt, :], rv8[0:nt, :], EPS, None, ALU.add), "var_qk")
                    after(ve, "drow", l, i + 1)
                    nu, nl = (cbf("neg_u"), cbf("neg_l")) if i < 2 else (cbf("neg_us", TS), cbf("neg_ls", TS))
                    dx, dy = v3(DX[0:nt, 0:n4], 4), v3(DY[0:nt, 0:n4], 4)
                    do(tt(dy, v3(B[3][0:nt, 0:n4], 4), last(gc, nt), ALU.subtract))
                    do(tt(dx, dy, mid(nu, 4), ALU.add))
                    do(tt(dy, mid(nl, 4), dy, ALU.subtract), "dlog")
                    refine(("qk", 3 * l + i + 1), rs8[0:nt, :], rv8[0:nt, :], rt8[0:nt, :])
                    do(ts(rs8[0:nt, 0:4], rs8[0:nt, 0:4], NK ** -0.5, None, ALU.mult))
                    do(tt(v3(DT[0:nt, :], 4), v3(B[0][0:nt, :], 4), last(rs8[0:nt, 0:4], NK), ALU.mult), "dqk")
                    do(tt(v3(DU[0:nt, :], 4), v3(B[1][0:nt, :], 4), last(rs8[0:nt, 4:8], NK), ALU.mult), "dqk")
                    kn = v3(DU[0:nt, :], 4)
                    go(tt(v3(DKD[0:nt, :], 4), kn, last(gDK[0:nt, 4 * i:4 * i + 4], NK), ALU.mult))
                    go(tt(v3(DKB[0:nt, :], 4), kn, last(gBG[0:nt, 4 * i:4 * i + 4], NK), ALU.mult))
                    after(ve, "dtr", l, 3 * i + 3)
                    go(tt(v3(DVB[0:nt, :], 4), v3(B[2][0:nt, :], 4), last(gBE[0:nt, 4 * i:4 * i + 4], NK), ALU.mult))
                    after(ve, "dmask", l, i + 1)
                    after(ve, "dkk", l, 2 * i + 1)
                    do(tt(DM[0:nt, 0:n4], B[6][0:nt, 0:n4], DY[0:nt, 0:n4], ALU.mult))
                    m3 = v3(DM[0:nt, 0:n4], 4)
                    do(tt(m3, m3, last(gBE[0:nt, 4 * i:4 * i + 4], nt), ALU.mult))
                    after(ve, "dkk", l, 2 * i + 2)
                    do(tt(cv3[0:nt, 8:12, t0:t0 + nt], v3(B[7][0:nt, 0:n4], 4), dx, ALU.mult), "dat")
                    lev = v3(cbf("level", nt), 7)

                    def masked(v, hs):
                        if v:
                            after(ve, "dy_mm", l, 14 * i + 2 * (v - 1) + hs + 1)
                        c = slice(2 * hs * nt, (2 * hs + 2) * nt)
                        do(tt(v3(DMB[0:nt, c], 2), v3(DM[0:nt, c], 2), mid(lev[:, v, 0:nt], 2), ALU.mult), "dmb")

                    after(ve, "dtb", l, 2 * i + 2)
                    for hs in range(2):
                        masked(0, hs)
                        c = slice(2 * hs * nt, (2 * hs + 2) * nt)
                        go(cp(v3(DT[0:nt, c], 2), mid(ident[0:nt, 0:nt], 2)))
                        do(cp(v3(DU[0:nt, c], 2), mid(ident[0:nt, 0:nt], 2)), "dtu")
                    after(ve, "drowe", l, i + 1)
                    qd = cv3[:, 0:4, t0:t0 + nt]
                    go(tt(qd, qd, v3(DX[:, 0:n4], 4), ALU.mult), "dqd")
                    if i < 2:
                        do(cp(gEL[:, 0:4], v3(DX[:, :], 4)[:, :, P - 1]))
                    else:
                        do(cp(v3(gEL[:, :], 4), v3(DX[:, 0:n4], 4)[:, :, LSEQ - 1:TS:LSEQ]))
                    nlev = 7 if i < 2 else 3
                    for v in range(nlev):
                        for hs in range(2):
                            if v + 1 < nlev:
                                masked(v + 1, hs)
                            after(ve, "dtu_mm", l, 14 * i + 2 * v + hs + 1)
                            c = slice(2 * hs * nt, (2 * hs + 2) * nt)
                            b = B[2 + 2 * hs]
                            go(tt(DT[0:nt, c], DT[0:nt, c], b[0:nt, 256:256 + 2 * nt], ALU.subtract))
                            do(tt(DU[0:nt, c], DU[0:nt, c], b[0:nt, 0:2 * nt], ALU.subtract), "dtu")
                    if i == 0:
                        after(ve, "ds_mm", l, 1)
                        do(cp(DSP, v3(B[3][:, :], 4)), "gdn_state")
                    elif i == 1:
                        after(ve, "ds_mm", l, 2)
                        for h in range(NH):
                            ins = stt(DSP[:, h, :], DSP[:, h, :], gEL[:, h:h + 1], B[3][:, h * P:(h + 1) * P], ALU.mult, ALU.add)
                            go(ins) if h < NH - 1 else do(ins, "gdn_state")
                    else:
                        after(ve, "dw", l, 3)
                        w3 = v3(DMB[:, 0:n4], 4)
                        for h in range(NH):
                            if h >= 2:
                                after(ve, "dvn_part", l, h - 1)
                            wm = (DM, DT)[h % 2]
                            if h < 2:
                                do(ve.memset(wm, 0.0))
                            base = (3, 5)[h % 2] * 512
                            diag = w(base, NSEQ * (TS + LSEQ)).rearrange("p (s u) -> p s u", s=NSEQ)[:, :, 0:LSEQ]
                            do(cp(diag, v3(w3[:, h, :], NSEQ)), "dwm")
                        after(ve, "do_mm", l, 3)
                        el4 = v3(gEL[:, :], 4)
                        for h in range(NH):
                            if h >= 2:
                                after(ve, "dss_mm", l, h - 1)
                            vm = v3((D01, D34)[h % 2], NSEQ)
                            do(tt(vm[0:TS, :, :], mid(DY[0:TS, h * P:(h + 1) * P], NSEQ), last(cst("seq", TS), NK), ALU.mult), "dvm")
                            do(tt(DS[:, h, :, :], DS[:, h, :, :], last(el4[:, h, :], NK), ALU.mult))
                            after(ve, "dss_mm", l, h + 1)
                            for c in range(2):
                                d = DS[:, h, 4 * c:4 * c + 4, :]
                                ins = tt(d, d, v3(B[3 + c][:, :], 4), ALU.add)
                                go(ins) if c == 0 else do(ins, "gdn_sstate")
                after(ve, "do", l, 3)
                finish_heads(("heads", 2 * l + 2), 4, ZT, col(f"gdnn{l}"), "gdn_fin")
                go(cp(rt[:, 0:1], rs[:, 0:1]), "gdn_done")

                for j in range(KD):
                    after(ve, "out_mm", l, j + 1)
                    residual(B[5 + j % 2], j, m0 + 16, "x_mix")
                norm(("norm", 2 * l + 2), m0 + 24, m0 + 32)
                if l == 0:
                    for u in range(FD):
                        e = FSG[u % 2]
                        ve.wait_ge(S("ff_e"), u + 1)
                        do(ts(e, e, 1.0, None, ALU.add))
                        do(ve.reciprocal(e, e))
                        do(tt(e, e, B[u % 2][:, 0:T], ALU.mult))
                        do(tt(FA[:, u, :], e, B[2 + u % 2][:, 0:T], ALU.mult), "ff_act")
                    for j in range(KD):
                        ve.wait_ge(S("down_mm"), j + 1)
                        residual(B[4 + j % 2], j, m0 + 40, "x_ff")

            ve.wait_ge(S("logits_mm"), 1)
            after(ve, "gdn_state_out", DEPTH - 1, 32)
            go(ve.memset(LG[:, :], 0.0))
            ve.wait_ge(S("vec_own"), own.n["vec_own"])
            go(cp(LG[:, 0:16], B[0][:, 0:16]))
            do(cp(LG[0:TS, 16:24], B[0][0:TS, 16:24]))
            lg3 = v3(LG[:, :], 3)
            do(ve.tensor_reduce(mx[:, :], lg3, AX.X, ALU.max))
            do(tt(v3(lgE[:, :], 3), lg3, last(mx[:, :], NE), ALU.subtract), "lg_shift")
            mine = last(LG[:, :], NE)
            for i in range(3):
                c = slice(NE * i, NE * (i + 1))
                mine = last(LG[:, c], NE)
                other = mid(LG[:, c], NE)
                go(tt(CMP[:, c, :], other, mine, ALU.is_gt))
                do(tt(CEQ[:, c, :], other, mine, ALU.is_equal))
                do(tt(CEQ[:, c, :], CEQ[:, c, :], v3(cbf("before"), NE), ALU.mult))
                do(tt(CMP[:, c, :], CMP[:, c, :], CEQ[:, c, :], ALU.add))
            do(ve.tensor_reduce(rank[:, :], CMP, AX.X, ALU.add))
            do(ts(sel[:, :], rank[:, :], 2.0, None, ALU.is_lt), "sel")
            ve.wait_ge(S("lg_exp"), 1)
            do(tt(cw[:, :], lgE[:, :], sel[:, :], ALU.mult))
            do(ve.tensor_reduce(mx[:, :], v3(cw[:, :], 3), AX.X, ALU.add))
            do(ve.reciprocal(mx[:, :], mx[:, :]))
            do(tt(v3(cw[:, :], 3), v3(cw[:, :], 3), last(mx[:, :], NE), ALU.mult))
            ve.wait_ge(S("pos_mm"), 1)
            do(ve.memset(pos[:, :], FAR))
            pos3 = v3(pos[:, :], 3)
            sel3, cw3 = v3(sel[:, :], 3), v3(cw[:, :], 3)
            for i, (t0, nt) in enumerate(TILES):
                do(stt(pos3[0:nt, i, 0:NE], sel3[0:nt, i, :], -FAR, B[1][0:nt, NE * i:NE * (i + 1)], ALU.mult, ALU.add))
                do(ts(pos3[0:nt, i, 0:NE], pos3[0:nt, i, 0:NE], FAR, None, ALU.add))
            do(ve.tensor_reduce(mx[:, 0:1], B[1][:, 32:32 + NE], AX.X, ALU.max))
            do(ts(flag[:, :], mx[:, 0:1], float(CAP), None, ALU.is_gt))
            ve.wait_ge(S("htok_tr"), 6)
            do(ve.memset(hT[:, :, :], 0.0), "flag_ready")

            def onehot(e, name):
                for i, (t0, nt) in enumerate(TILES):
                    s1 = pos3[0:nt, i, bass.ds(e, 1)]
                    ts(ONEH[0:nt, i, :], cbf("iota", nt), s1, None, ALU.is_equal)
                for i, (t0, nt) in enumerate(TILES):
                    s1 = pos3[0:nt, i, bass.ds(e, 1)]
                    ins = ts(ONEW[0:nt, i, :], cbf("iota", nt), s1, cwp3[0:nt, i, bass.ds(e, 1)], ALU.is_equal, ALU.mult)
                ins.then_inc(S(name), 1)

            do(ve.memset(cwp[:, :], 0.0))
            cwp3 = v3(cwp[:, :], 3)
            do(cp(cwp3[:, :, 0:NE], cw3))
            onehot(0, "onehot")

            def expert(e, el, r):
                for c in range(NCH):
                    if c == 2:
                        ve.wait_ge(S("e_wT_mm"), el + 1)
                        onehot(e + 1, "onehot")
                    ee, n = EE[:, c % 2, :], (el * NCH + c) * 3
                    ve.wait_ge(S("e_exp"), el * NCH + (c + 1))
                    if c >= 2:
                        ve.wait_ge(S("e_tr"), el * NCH + c)
                    elif c == 0:
                        ve.wait_ge(S("e_tr"), el * NCH + 1)
                    ts(ee, ee, 1.0, None, ALU.add).then_inc(S("e_step"), 1)
                    ve.wait_ge(S("e_step"), n + 1)
                    ve.reciprocal(ee, ee).then_inc(S("e_step"), 1)
                    ve.wait_ge(S("e_step"), n + 2)
                    tt(ee, ee, B[c % 2][:, :], ALU.mult).then_inc(S("e_step"), 1)
                    ve.wait_ge(S("e_step"), n + 3)
                    ve.wait_ge(S("e_up_mm"), el * NCH + (c + 1))
                    tt(EA[:, c % 2, :], ee, B[2 + c % 2][:, :], ALU.mult).then_inc(S("e_act"), 1)
                for j in range(KD):
                    ve.wait_ge(S("e_sc_mm"), el * KD + (j + 2))
                    tt(hT[:, j, :], hT[:, j, :], B[4 + j % 2][:, 0:T], ALU.add).then_inc(S("e_scatter"), 1)
                ve.wait_ge(S("e_scatter"), el * KD + KD + 1)

            with ve.Fori(0, NE) as e:
                expert(e, e, 0)
            more = ve.value_load(flag[0:1, 0:1], min_val=0, max_val=1)
            with ve.If(more > 0):
                with ve.Fori(1, MAXPASS) as r:
                    ve.wait_ge(S("onehot"), r * (NE + 1))
                    ts(pos[:, :], pos[:, :], -float(CAP), None, ALU.add).then_inc(S("shifted"), 1)
                    ve.wait_ge(S("shifted"), r)
                    ve.wait_ge(S("e_wT_mm"), r * NE)
                    onehot(0, "onehot")
                    with ve.Fori(0, NE) as e:
                        expert(e, r * NE + e, r)

            for j in range(KD):
                residual(hT[:, j, :], j, 48 + 40, None)
            norm(("norm", 5), 96, 104)
            go(cp(rt[:, 0:1], rs[:, 0:1]), "y_done")
            if len(sems) > 200:
                print(len(sems), "semaphores")


def tiles(a):
    *lead, r, c = a.shape
    return np.moveaxis(a.reshape(*lead, r // P, P, c), -2, -3)


def pieces(a, width=CH):
    r, c = a.shape
    t = tiles(a).reshape(P, r // P, c // width, width)
    return np.ascontiguousarray(t.transpose(2, 0, 1, 3)).reshape(c // width, P, -1)


def columns(v):
    return np.moveaxis(v.reshape(*v.shape[:-1], -1, P), -1, 0)


def lay_out(x):
    f = np.float32
    out = {}
    xs = np.concatenate([x["x_prompt"].reshape(TP, D), x["x_sample"].reshape(TS, D)], 0)
    out["xT"] = tiles(xs.T)
    q, k, v, lr, g, qkv, a, b, z = np.split(x["w_in"], np.cumsum([256, 256, 512, 16, 512, 1536, 4, 4]), axis=-1)
    big = np.concatenate([qkv, q, k, v, g, z], -1)
    out["wsm"] = tiles(np.concatenate([lr, a, b], -1))
    out["w_in"] = np.stack([pieces(big[l]) for l in range(DEPTH)])
    out["w_out"] = np.stack([pieces(x["w_out"][l]) for l in range(DEPTH)])
    out["ada"] = np.concatenate([pieces(x["w_ada"][0]), pieces(x["w_ada"][1]), pieces(x["w_ada_final"])])
    gate, up = tiles(x["w_ff_gate"][0]), tiles(x["w_ff_up"][0])
    gu = np.concatenate([gate.reshape(P, KD, N_GU, 256), up.reshape(P, KD, N_GU, 256)], -1)
    out["gu"] = np.ascontiguousarray(gu.transpose(2, 0, 1, 3)).reshape(N_GU, P, SLOT)
    out["down"] = pieces(x["w_ff_down"][0], P)
    moe = np.empty((NE, NCH, 3, P, SLOT), f)
    for e in range(NE):
        moe[e, :, 0] = pieces(x["w_exp_gate"][0, e])
        moe[e, :, 1] = pieces(x["w_exp_up"][0, e])
        moe[e, :, 2] = tiles(x["w_exp_down"][0, e].reshape(NCH, CH, D)).reshape(NCH, P, SLOT)
    out["moe"] = moe.reshape(NE * PER_E, P, SLOT)
    out["wgate"] = x["w_gla_gate"]
    out["wrt"] = tiles(x["w_router"][0])
    sm = np.zeros((P, N_SM), f)

    def put(name, val):
        at, n = SM[name]
        sm[:, at:at + n] = val.reshape(P, n)

    c = np.concatenate([x["c_prompt"], x["c_sample"]], 0)
    put("c", tiles(c.T))
    put("b_ada", columns(np.concatenate([x["b_ada"][0], x["b_ada"][1], x["b_ada_final"]])))
    for l in range(DEPTH):
        put(f"nm{l}", columns(x["norm_mix"][l]))
        put(f"nf{l}", columns(x["norm_ffn"][l]))
        put(f"bg{l}", columns(x["b_gla_gate"][l]))
        put(f"wconv{l}", columns(x["w_conv"][l]).transpose(0, 2, 1))
        put(f"glan{l}", columns(x["gla_norm"][l]))
        put(f"gdnn{l}", columns(x["gdn_norm"][l]))
        put(f"alog{l}", np.broadcast_to(x["a_log"][l], (P, NH)))
        put(f"dtb{l}", np.broadcast_to(x["dt_bias"][l], (P, NH)))
    put("nfin", columns(x["norm_final"]))
    out["small"] = sm
    out["cf"], out["cb"] = shape_constants()
    out["s_conv"] = columns(x["state_conv"]).transpose(1, 0, 4, 2, 3)
    out["s_gla"] = x["state_gla"].reshape(DEPTH, NSEQ, 2, P, GV).transpose(0, 2, 3, 1, 4)
    out["s_gdn"] = x["state_gdn"].transpose(0, 3, 2, 1, 4)
    return {k: np.ascontiguousarray(v) for k, v in out.items()}


OUTS = {"y": (P, KD, T), "conv": (DEPTH, P, CT, NC_, 3), "gla_p": (DEPTH, P, 2, GV), "gla_s": (DEPTH, 2, P, NSEQ, GV),
        "gdn_p": (DEPTH, P, NH, NK), "gdn_s": (DEPTH, P, NH, NSEQ, NK)}


def kernel(**inputs):
    import concourse.bacc as bacc
    from concourse.bass_utils import run_bass_kernel_spmd as run

    arrays = lay_out({k: np.asarray(v) for k, v in inputs.items()})
    nc = bacc.Bacc("TRN2", target_bir_lowering=False, num_devices=1)
    A = {k: nc.dram_tensor(f"in_{k}", v.shape, mybir.dt.from_np(v.dtype), kind="ExternalInput").ap()
         for k, v in arrays.items()}
    O = {k: nc.dram_tensor(f"out_{k}", s, F32, kind="ExternalOutput").ap() for k, s in OUTS.items()}
    build(nc, A, O)
    got = run(nc, [{f"in_{k}": v for k, v in arrays.items()}], core_ids=[0]).results[0]
    r = {k: got[f"out_{k}"] for k in OUTS}
    y = np.ascontiguousarray(r["y"].transpose(2, 1, 0)).reshape(T, D)
    conv = r["conv"].transpose(0, 3, 4, 2, 1).reshape(DEPTH, NC_, 3, CT * P)
    gla_p = r["gla_p"].transpose(0, 2, 1, 3).reshape(DEPTH, 1, GH, GK, GV)
    gla_s = r["gla_s"].transpose(0, 3, 1, 2, 4).reshape(DEPTH, NSEQ, GH, GK, GV)
    gdn_p = r["gdn_p"].transpose(0, 2, 1, 3).reshape(DEPTH, 1, NH, NK, NK)
    gdn_s = r["gdn_s"].transpose(0, 3, 2, 1, 4)
    full = [y[:TP].reshape(1, TP, D), y[TP:].reshape(NSEQ, LSEQ, D), gla_p, gdn_p, conv[:, 0:1], gla_s, gdn_s, conv[:, 1:]]
    return tuple(np.ascontiguousarray(a) for a in full)
```

```python
from contextlib import ExitStack

import numpy as np

import concourse.bass as bass
from concourse import mybir

ALU = mybir.AluOpType
ACT = mybir.ActivationFunctionType
AX = mybir.AxisListType
F32 = mybir.dt.float32
F32R = mybir.dt.float32r
BF16 = mybir.dt.bfloat16
I32 = mybir.dt.int32

P = 128
D = 1024
KD = D // P
TP, NSEQ, LSEQ = 256, 8, 8
TS = NSEQ * LSEQ
T = TP + TS
DEPTH = 2
NC_ = 1 + NSEQ
GH, GK, GV = 4, 64, 128
NH, NK = 4, 128
CT = 12
CW = 4
LR = 16
GATE_NORM = 16.0
EPS = 1e-6
FD = 2816 // P
NE = 8
FE = 3584
CH = 512
NCH = FE // CH
HALF = KD * CH // 2
SLOTS = 7
PARTS = 3
N_ADA = 28
N_IN = 7
N_GU = FD // 2
N_OUT = 2
SUB = 32
WORK = 14080
BIG = -1.0e30
CAP = P
MAXPASS = -(-T // CAP)
TD = KD * T
FAR = 4096.0
TILES = [(0, P), (P, P), (TP, TS)]
LEVELS = [1, 2, 4, 8, 16, 32, 64]

H_ADA, H_IN, H_OUT, H_GU, H_DN = 2 * N_ADA, 2 * N_IN, 2 * N_OUT, FD, 2 * KD
AT_IN = [H_ADA, H_ADA + H_IN + H_OUT + H_GU + H_DN]
AT_OUT = [a + H_IN for a in AT_IN]
AT_GU = AT_OUT[0] + H_OUT
AT_DN = AT_GU + H_GU
AT_MOE = AT_OUT[1] + H_OUT
GATE, UP, DOWN = range(3)
ORDER = [(GATE, 0), (UP, 0)] + [x for c in range(1, NCH) for x in ((GATE, c), (UP, c), (DOWN, c - 1))] + [(DOWN, NCH - 1)]
PER_E = 2 * len(ORDER)
TURN = 2 * SLOTS

PER_LAYER = {
    "conv_done": 1, "conv_in": 16, "conv_out": 16, "cv_e": 12, "cv_raw": 12, "dat": 3, "dkk": 6, "dlog": 3,
    "dmask": 3, "dmb": 34, "do": 3, "do_mm": 3, "dqd": 3, "dqk": 6, "dqkT": 6, "drow": 3, "drowe": 3, "ds_mm": 2,
    "dsq": 6, "dss_mm": 4, "dtb": 6, "dtr": 9, "dtu": 34, "dtu_mm": 28, "dvm": 4, "dvn": 3, "dvn_mm": 3,
    "dvn_part": 3, "dw": 3, "dw_mm": 3, "dwm": 4, "dy": 28, "dy_mm": 34, "g": 1, "gact": 1, "gam_mm": 1, "gamc": 1,
    "gcols": 1, "gdn_done": 1, "gdn_fin": 1, "gdn_sstate": 4, "gdn_state": 2, "gdn_state_in": 16,
    "gdn_state_out": 32, "gexp": 1, "gla_arg": 3, "gla_at": 3, "gla_at_mm": 3, "gla_exp": 3, "gla_fin": 1,
    "gla_ktr": 3, "gla_o": 3, "gla_o_mm": 3, "gla_ops": 3, "gla_out": 48, "gla_s_mm": 2, "gla_ss_mm": 4,
    "gla_sstate": 2, "gla_state": 2, "gla_state_in": 32, "gla_tok": 6, "gla_tr": 3, "gla_vm": 4, "gx": 1, "hl_in": 1, "hl_out": 1, "la": 1,
    "lr_t": 1, "out_mm": 8, "proj": 28, "proj_mm": 28, "small_mm": 2, "smallw_in": 32, "x_mix": 8, "xp_ready": 1,
    "z_mm": 2, "zb": 1, "zl": 1,
}

SM = {}


def _pack(table, names):
    at = 0
    for name, n in names:
        table[name] = (at, n)
        at += n
    return at


N_SM = _pack(SM, [("c", KD * NC_), ("b_ada", 4 * N_ADA), ("nm0", KD), ("nm1", KD), ("nf0", KD), ("nf1", KD), ("nfin", KD)]
             + [(f"{n}{l}", w) for l in range(DEPTH)
                for n, w in (("bg", 2), ("wconv", CT * CW), ("glan", 1), ("gdnn", 1), ("alog", NH), ("dtb", NH))])
CF = {}
N_CF = _pack(CF, [("ident", P), ("ones", P), ("tri", P), ("tri_s", TS), ("strict", P), ("seq", NSEQ), ("block", TS), ("comb", NC_)])
CB = {}
N_CB = _pack(CB, [("level", len(LEVELS) * P), ("neg_u", P), ("neg_us", TS), ("neg_l", P), ("neg_ls", TS),
                  ("iota", P), ("reset", T), ("before", NE * NE)])


def shape_constants():
    f, b = np.zeros((P, N_CF), np.float32), np.zeros((P, N_CB), np.float32)
    i, j = np.meshgrid(np.arange(P), np.arange(P), indexing="ij")
    si, sj = i[:TS, :TS], j[:TS, :TS]
    same = si // LSEQ == sj // LSEQ

    def put(dst, table, name, v):
        at, n = table[name]
        dst[:v.shape[0], at:at + n] = v

    put(f, CF, "ident", i == j)
    put(f, CF, "ones", np.ones((P, P)))
    put(f, CF, "tri", i <= j)
    put(f, CF, "tri_s", (si <= sj) & same)
    put(f, CF, "strict", i < j)
    put(f, CF, "seq", np.arange(TS)[:, None] // LSEQ == np.arange(NSEQ)[None, :])
    put(f, CF, "block", same)
    put(f, CF, "comb", np.arange(2 * NC_)[:, None] % NC_ == np.arange(NC_)[None, :])
    put(b, CB, "level", np.concatenate(
        [(i // (2 * w) == j // (2 * w)) & (i % (2 * w) >= w) & (j % (2 * w) < w) for w in LEVELS], 1))
    put(b, CB, "neg_u", np.where(i <= j, 0, BIG))
    put(b, CB, "neg_us", np.where((si <= sj) & same, 0, BIG))
    put(b, CB, "neg_l", np.where(i > j, 0, BIG))
    put(b, CB, "neg_ls", np.where((si > sj) & same, 0, BIG))
    put(b, CB, "iota", j)
    t = np.arange(T)
    put(b, CB, "reset", np.tile(np.where(t < TP, t % P != 0, (t - TP) % LSEQ != 0), (P, 1)))
    e = np.arange(NE)
    put(b, CB, "before", np.tile((e[None, :] < e[:, None]).reshape(-1), (P, 1)))
    return f, b


def mid(ap, n):
    return ap.unsqueeze(1).to_broadcast([ap.shape[0], n, ap.shape[1]])


def last(ap, n):
    return ap.unsqueeze(len(ap.shape)).to_broadcast([*ap.shape, n])


def build(nc, A, O):
    ctx = ExitStack()
    with ctx:
        def sb(name, shape, dt=F32):
            return ctx.enter_context(nc.sbuf_tensor(name, shape, dt))

        def sem(name):
            return ctx.enter_context(nc.semaphore(name))

        B = [ctx.enter_context(nc.psum_tensor(f"bank{i}", [P, 512], F32)) for i in range(8)]

        raw = sb("raw", [P, SLOTS, HALF])
        whi = sb("whi", [P, PARTS, HALF], F32R)
        wlo = sb("wlo", [P, PARTS, HALF], F32R)
        xT = sb("xT", [P, KD, T])
        small = sb("small", [P, N_SM])
        cf = sb("cf", [P, N_CF])
        cb = sb("cb", [P, N_CB], BF16)
        mod = sb("mod", [P, 4 * N_ADA, NC_])
        wsm = sb("wsm", [P, KD, LR + 2 * NH])
        wgate = sb("wgate", [LR, GH * GK])
        wrt = sb("wrt", [P, KD, NE])
        rs = sb("rs", [P, T])
        rv = sb("rv", [P, T])
        csT = rv[:, 0:KD * NC_]
        rt = sb("rt", [P, T])
        rv8, rs8, rt8 = (sb(n, [P, 2 * NH]) for n in ("rv8", "rs8", "rt8"))
        gAB = sb("gate_ab", [P, 3 * 2 * NH])
        gX, gL, gEB, gG, gBE, gGC, gGL, gD, gEG, gDK, gBG = (
            sb(n, [P, 3 * NH]) for n in ("g_x", "g_log", "g_expb", "g_decay", "g_beta", "g_run", "g_end", "g_left",
                                         "g_exprun", "g_expleft", "g_betaexp"))
        gEA = sb("g_expa", [P, NH])
        gEB_ = sb("gla_expend", [P, 2 * NSEQ])
        gEL = sb("g_expend", [P, NH * NSEQ])
        LG = gAB
        lgE, sel, cw = (sb(n, [P, 3 * NE]) for n in ("lg_e", "sel", "cw"))
        rank = cw
        pos, cwp = (sb(n, [P, 3 * (NE + 1)]) for n in ("pos", "cwp"))
        mx = sb("mx", [P, 3])
        flag = sb("flag", [P, 1], I32)

        def overlay(*wanted):
            with ExitStack() as over:
                return [over.enter_context(nc.sbuf_tensor(n, [P, size], dt)) for n, size, dt in wanted]

        W, hT_ = overlay(("work", WORK + TD, F32), ("hT", TD, F32))
        _, hh_, hl_ = overlay(("under_h", WORK, F32), ("hh", TD, F32R), ("hl", TD, F32R))
        (cs_r,) = overlay(("cs_parts", KD * P, F32R))
        fah_, fal_ = overlay(("ff_high", FD * T, F32R), ("ff_low", FD * T, F32R))
        hth_, htl_, oneh_, hgh_, hgl_, eath_, eatl_, _ = overlay(
            ("htok_high", 3 * D, F32R), ("htok_low", 3 * D, F32R), ("onehot", 3 * P, F32R), ("hg_high", D, F32R),
            ("hg_low", D, F32R), ("act_high", 2 * CH, F32R), ("act_low", 2 * CH, F32R), ("rest", 16, F32))
        _ = sb("region", [P, WORK + 2 * TD])
        hT, hh, hl = (t[:, :].rearrange("p (k t) -> p k t", k=KD) for t in (hT_, hh_, hl_))

        def w(at, n):
            return W[:, at:at + n]

        def v3(ap, a):
            return ap.rearrange("p (a b) -> p a b", a=a)

        def col(name):
            at, n = SM[name]
            return small[:, at:at + n]

        def cst(name, rows=P):
            at, n = CF[name]
            return cf[0:rows, at:at + n]

        def cbf(name, rows=P):
            at, n = CB[name]
            return cb[0:rows, at:at + n]

        ident, ones = cst("ident"), cst("ones")
        TL = 4 * T
        QK, V1, G1, ZT = w(0, TL), w(TL, TL), w(2 * TL, TL), w(3 * TL, TL)
        CV = w(4 * TL, 3 * TL)
        R = 7 * TL
        qk3, v13, g13, zt3, cv3 = v3(QK, 4), v3(V1, 4), v3(G1, 4), v3(ZT, 4), v3(CV, CT)
        LA = v3(w(R, 2 * T), 2)
        R1 = R + 2 * T
        XPW, XSW = TP + CW - 1, LSEQ + CW - 1
        at = R1

        def take(n):
            nonlocal at
            at += n
            assert at <= WORK + TD, at
            return w(at - n, n)

        XP = v3(take(4 * XPW), 4)
        XS = take(4 * NSEQ * XSW).rearrange("p (c s u) -> p c s u", c=4, s=NSEQ)
        OC = take(CT * NC_ * 3).rearrange("p (c s u) -> p c s u", c=CT, s=NC_)
        SC = take(CT * NSEQ * 3).rearrange("p (c s u) -> p c s u", c=CT, s=NSEQ)
        CE = v3(take(2 * T), 2)
        LRT = take(T)[0:LR, :]
        LAE = take(2 * T)
        at = R1
        NJ = [P - SUB * j for j in range(P // SUB)]
        GEA = take(2 * sum(NJ))
        GE = [v3(GEA[:, 2 * sum(NJ[:j]):2 * sum(NJ[:j + 1])], 2) for j in range(len(NJ))]
        GKT, GKE, GQD = (v3(take(256), 2) for _ in range(3))
        GVT = take(512)
        GKDT = take(256)
        GAT = take(512)
        GS = v3(take(256), 2)
        GVM = v3(take(1024), NSEQ)
        GSS = [v3(w(TL, 1024), NSEQ), v3(take(1024), NSEQ)]
        DS = w(R, NH * NSEQ * NK).rearrange("p (h s v) -> p h s v", h=NH, s=NSEQ)
        at = R + NH * NSEQ * NK
        DSP = v3(take(NH * NK), NH)
        DSET = [[w(512 * i, 512) for i in range(7)] + [take(512), take(512)],
                [w(R + 512 * i, 512) for i in range(8)] + [take(512)]]
        DM, DMB, DT, DY = DSET[0][3], DSET[0][4], DSET[0][5], DSET[0][7]
        D01, D34 = w(0, 1024), w(3 * 512, 1024)
        YBANK, TBANK = ((B[0], B[1]), (B[5], B[6])), ((B[2], B[4]), (B[3], B[7]))
        FAH, FAL = v3(fah_[:, :], FD), v3(fal_[:, :], FD)
        FSG = [rs[:, :], rv[:, :]]
        CSP = v3(cs_r[:, :], KD)
        at = KD * P + N_CB
        AROW = v3(take(2 * CH), 2)
        HTH, HTL, ONEH = (v3(t[:, :], 3) for t in (hth_, htl_, oneh_))
        HGH, HGL = v3(hgh_[:, :], KD), v3(hgl_[:, :], KD)
        EATH, EATL = v3(eath_[:, :], 2), v3(eatl_[:, :], 2)
        at = 2 * 3 * D + 3 * P + 2 * D + 4 * CH
        ONEW = v3(take(3 * P), 3)
        ONEWT = take(T)
        EA = v3(take(2 * CH), 2)
        YE = take(D)
        CMP, CEQ = (take(3 * NE * NE).rearrange("p (a b) -> p a b", b=NE) for _ in range(2))

        GAB, GOB = (B[4], B[7]), (B[5], B[0])

        sems = {}

        def S(name):
            if name not in sems:
                sems[name] = sem(name)
            return sems[name]

        def after(eng, name, l, v):
            eng.wait_ge(S(name), PER_LAYER[name] * l + v)

        landed = [S(f"landed{s}") for s in range(SLOTS)]

        def part(n):
            return (n % TURN) % PARTS if n < H_ADA else (n - H_ADA) % PARTS

        def used(n):
            if n < AT_IN[0]:
                return S("ada_mm"), PARTS + n + 1
            for l in range(DEPTH):
                if AT_IN[l] <= n < AT_OUT[l]:
                    return S("proj_mm"), PER_LAYER["proj_mm"] * l + 2 * (n - AT_IN[l] + 1)
                if AT_OUT[l] <= n < AT_OUT[l] + H_OUT:
                    return S("out_mm"), PER_LAYER["out_mm"] * l + 2 * (n - AT_OUT[l] + 1)
            if n < AT_DN:
                return S("gu_mm"), n - AT_GU + 1
            return S("down_mm"), n - AT_DN + 1

        KINDS = [S("e_gate_mm"), S("e_up_mm"), S("e_down_mm")]

        def split_high(ac, n):
            ac.wait_ge(landed[n % SLOTS], 16 * (n // SLOTS + 1))
            before = [m for m in range(n - 1, max(n - 8, -1), -1) if part(m) == part(n)]
            if before:
                ac.wait_ge(*used(before[0]))
            ac.activation(whi[:, part(n), 0:width(n)], raw[:, n % SLOTS, 0:width(n)], ACT.Copy).then_inc(S("w_high"), 1)

        def split_low(ve, n):
            ve.wait_ge(S("w_high"), n + 1)
            ve.tensor_tensor(wlo[:, part(n), 0:width(n)], raw[:, n % SLOTS, 0:width(n)], whi[:, part(n), 0:width(n)],
                             ALU.subtract).then_inc(S("w_low"), 1)

        def width(n):
            return FD * P // 2 if AT_DN <= n < AT_DN + H_DN else HALF

        def split_in(pe, n):
            pe.wait_ge(S("w_low"), n + 1)

        def levels_of(i):
            return range(7 if i < 2 else 3)

        def at_level(i, v, hs):
            return (4 * v + 2 * i if i < 2 else 28 + 2 * v) + hs + 1

        def at_update(i, v, hs):
            return (4 * (v - 1) + 2 * i if i < 2 else 24 + 2 * (v - 1)) + hs + 1

        class Split:

            def __init__(self, eng, one, first):
                self.eng, self.one, self.next = eng, one, first

            def to(self, n):
                while self.next <= min(n, AT_MOE - 1):
                    self.one(self.eng, self.next)
                    self.next += 1

        def e_used(el, j):
            kind, c = ORDER[j // 2]
            v = 2 * c + j % 2 + 1
            return KINDS[kind], el * (2 * NCH) + v + (PARTS if kind == DOWN else 0)

        def e_split_high(ac, el, j):
            n = AT_MOE + j
            ac.wait_ge(landed[n % SLOTS], el * (16 * PER_E // SLOTS) + 16 * (n // SLOTS + 1))
            if j >= PARTS:
                ac.wait_ge(*e_used(el, j - PARTS))
            else:
                ac.wait_ge(S("e_down_mm"), el * (2 * NCH) + (j + 1))
            ac.activation(whi[:, part(n), :], raw[:, n % SLOTS, :], ACT.Copy).then_inc(S("w_high"), 1)

        def e_split_low(ve, el, j):
            n = AT_MOE + j
            ve.wait_ge(S("w_high"), el * PER_E + (n + 1))
            ve.tensor_tensor(wlo[:, part(n), :], raw[:, n % SLOTS, :], whi[:, part(n), :], ALU.subtract)\
              .then_inc(S("w_low"), 1)

        class Own:

            def __init__(self, eng, name):
                self.eng, self.name, self.n = eng, name, {}

            def go(self, ins, name=None):
                name = name or self.name
                self.n[name] = self.n.get(name, 0) + 1
                ins.then_inc(S(name), 1)

            def do(self, ins, name=None):
                self.go(ins, name)
                self.eng.wait_ge(S(name or self.name), self.n[name or self.name])

        block = ctx.enter_context(nc.Block())
        FP = NC_ * KD

        def md(base, n=KD):
            return mod[:, base:base + n, :]

        @block.sync
        def _(sp):
            for dst, src in ((small, A["small"]), (cf, A["cf"]), (W[:, KD * P:KD * P + N_CB], A["cb"]), (wrt, A["wrt"])):
                sp.dma_start(dst[:, :] if dst is not wrt else wrt[:, :, :], src).then_inc(S("const_in"), 16)
            sp.dma_start(xT[:], A["xT"]).then_inc(S("x_in"), 16)

            def load(n, src):
                if n >= SLOTS:
                    sp.wait_ge(S("w_low"), n - SLOTS + 1)
                sp.dma_start(raw[:, n % SLOTS, 0:width(n)], src).then_inc(landed[n % SLOTS], 16)

            for n in range(TURN):
                load(n, A["ada"][n, :, :])
            with sp.Fori(1, H_ADA // TURN) as turn:
                for j in range(TURN):
                    sp.wait_ge(S("w_low"), turn * TURN + (j - SLOTS + 1))
                    sp.dma_start(raw[:, j % SLOTS, :], A["ada"][turn * TURN + j, :, :]).then_inc(landed[j % SLOTS], 16)
            for l in range(DEPTH):
                for i in range(H_IN):
                    load(AT_IN[l] + i, A["w_in"][l, i, :, :])
                for i in range(H_OUT):
                    load(AT_OUT[l] + i, A["w_out"][l, i, :, :])
                if l == 0:
                    for i in range(H_GU):
                        load(AT_GU + i, A["gu"][i, :, :])
                    for i in range(H_DN):
                        load(AT_DN + i, A["down"][i, :, :])

            def expert(e, el):
                for j in range(PER_E):
                    n = AT_MOE + j
                    sp.wait_ge(S("w_low"), el * PER_E + (n - SLOTS + 1))
                    sp.dma_start(raw[:, n % SLOTS, :], A["moe"][e * PER_E + j, :, :]).then_inc(landed[n % SLOTS], 16)

            with sp.Fori(0, NE) as e:
                expert(e, e)
            sp.wait_ge(S("flag_ready"), 1)
            more = sp.value_load(flag[0:1, 0:1], min_val=0, max_val=1)
            with sp.If(more > 0):
                with sp.Fori(1, MAXPASS) as r:
                    with sp.Fori(0, NE) as e:
                        expert(e, r * NE + e)

        @block.gpsimd
        def _(po):
            waits = []

            def store(dst, src, name):
                po.dma_start(dst, src).then_inc(S(name), 16)
                waits.append(name)

            for l in range(DEPTH):
                if l:
                    after(po, "z_mm", 0, 2)
                    after(po, "small_mm", 0, 2)
                    after(po, "gdn_done", 0, 1)
                po.dma_start(wsm[:], A["wsm"][l, :, :, :]).then_inc(S("smallw_in"), 16)
                po.dma_start(wgate[:], A["wgate"][l, :, :]).then_inc(S("smallw_in"), 16)
                if l:
                    po.wait_ge(S("down_mm"), H_DN)
                po.dma_start(SC, A["s_conv"][l, :, :, :, :]).then_inc(S("conv_in"), 16)
                after(po, "conv_done", l, 1)
                store(O["conv"][l, :, :, :, :], OC, "conv_out")
                after(po, "proj_mm", l, 4 * N_IN)
                po.dma_start(GSS[1], A["s_gla"][l, 1, :, :, :]).then_inc(S("gla_state_in"), 16)
                after(po, "gla_tr", l, 3)
                po.dma_start(GSS[0], A["s_gla"][l, 0, :, :, :]).then_inc(S("gla_state_in"), 16)
                after(po, "gla_state", l, 2)
                store(O["gla_p"][l, :, :, :], GS, "gla_out")
                for p in range(2):
                    after(po, "gla_sstate", l, p + 1)
                    store(O["gla_s"][l, p, :, :, :], GSS[p], "gla_out")
                after(po, "gdn_state", l, 2)
                po.dma_start(DS, A["s_gdn"][l, :, :, :, :]).then_inc(S("gdn_state_in"), 16)
                store(O["gdn_p"][l, :, :, :], DSP, "gdn_state_out")
                after(po, "gdn_sstate", l, NH)
                store(O["gdn_s"][l, :, :, :, :], DS, "gdn_state_out")
            po.wait_ge(S("y_done"), 1)
            store(O["y"], hT[:], "y_out")
            for name in dict.fromkeys(waits):
                po.wait_ge(S(name), 16 * waits.count(name))

        @block.tensor
        def _(pe):
            def mm(out, lhsT, rhs, start=True, stop=True, **k):
                return pe.matmul(out, lhsT, rhs, start=start, stop=stop, **k)

            def sum_squares(tag):
                pe.wait_ge(S(f"sq_{tag[0]}"), tag[1])
                for k in range(KD):
                    ins = mm(B[0][:, 0:T], ones, hT[:, k, :], k == 0, k == KD - 1)
                ins.then_inc(S(f"ss_{tag[0]}"), 1)

            def finish_heads(tag):
                pe.wait_ge(S(f"sq_{tag[0]}"), tag[1])
                q = v3(QK, 4)
                for h in range(4):
                    ins = mm(B[0][32 * h:32 * h + 32, 0:T], ones[:, 0:32], q[:, h, :])
                ins.then_inc(S(f"ss_{tag[0]}"), 1)
                pe.wait_ge(S(f"rs_{tag[0]}"), tag[1])
                for h in range(4):
                    ins = mm(B[1 + h][:, 0:T], ident[:, 32 * h:32 * h + 1].to_broadcast([P, P]), rs[:, :])
                ins.then_inc(S(f"rsb_{tag[0]}"), 1)

            def mm3(out, w_high, w_low, x_high, x_low, first, last):
                mm(out, w_high, x_high, first, False)
                mm(out, w_low, x_high, False, False)
                return mm(out, w_high, x_low, False, last)

            def parts(n):
                return whi[:, part(n), :], wlo[:, part(n), :]

            pe.wait_ge(S("const_in"), 64)
            pe.wait_ge(S("cs"), 1)
            for name, v in (("e_tr", 1), ("e_sc_mm", 1), ("e_wT_mm", 1), ("e_down_mm", PARTS), ("ada_mm", PARTS)):
                pe.sem_inc(S(name), v)
            with pe.Fori(0, H_ADA // TURN) as turn:
                for s in range(TURN // 2):
                    for b in range(2):
                        n = 2 * s + b
                        pe.wait_ge(S("w_low"), turn * TURN + (n + 1))
                        wh, wl = (v3(x, KD // 2) for x in parts(n))
                        for k in range(KD // 2):
                            c = CSP[:, 4 * b + k, :]
                            mm(B[s % 2][:, :], c, wh[:, k, :], n % 2 == 0 and k == 0, False)
                            ins = mm(B[s % 2][:, :], c, wl[:, k, :], False, b == 1 and k == 3)
                        ins.then_inc(S("ada_mm"), 1)
                    pe.wait_ge(S("ada_rows"), turn * (TURN // 2) + (s + 1))
                    pe.wait_ge(S("ada_done"), turn * (TURN // 2) + (1 if s < 2 else s))
                    for j in range(4):
                        ins = mm(B[2 + s % 2][:, j * NC_:(j + 1) * NC_], AROW[0:2 * NC_, s % 2, j * P:(j + 1) * P],
                                 cst("comb", 2 * NC_))
                    ins.then_inc(S("ada_turned"), 1)

            for l in range(DEPTH):
                sum_squares(("norm", 2 * l + 1))
                pe.wait_ge(S("h_norm"), 2 * l + 1)
                after(pe, "smallw_in", l, 32)
                for k in range(KD):
                    ins = mm(B[2][0:LR, 0:T], wsm[:, k, 0:LR], hT[:, k, :], k == 0, k == KD - 1)
                ins.then_inc(S("small_mm"), 1)
                for i, (t0, nt) in enumerate(TILES):
                    for k in range(KD):
                        ins = mm(B[3][0:nt, 8 * i:8 * i + 8], hT[:, k, t0:t0 + nt], wsm[:, k, LR:],
                                 k == 0, k == KD - 1)
                ins.then_inc(S("small_mm"), 1)
                after(pe, "hl_in", l, 1)
                for u in range(4 * N_IN):
                    n = AT_IN[l] + u // 2
                    if u % 2 == 0:
                        split_in(pe, n)
                    if u >= 2:
                        after(pe, "proj", l, u - 1)
                    wh, wl = (v3(x, KD) for x in parts(n))
                    c = slice((u % 2) * P, (u % 2 + 1) * P)
                    for k in range(KD):
                        ins = mm3(B[u % 2][:, 0:T], wh[:, k, c], wl[:, k, c], hh[:, k, :], hl[:, k, :], k == 0, k == KD - 1)
                    ins.then_inc(S("proj_mm"), 1)
                    if u == 3:
                        after(pe, "lr_t", l, 1)
                        for p in range(2):
                            mm(B[4 + p][:, 0:T], wgate[:, p * P:(p + 1) * P], LRT).then_inc(S("z_mm"), 1)
                    if u == 7:
                        after(pe, "g", l, 1)
                        for i, (t0, nt) in enumerate(TILES):
                            tri, blk = (cst("tri"), ones) if i < 2 else (cst("tri_s", TS), cst("block", TS))
                            mm(B[6][0:nt, 4 * i:4 * i + 4], tri, gG[0:nt, 4 * i:4 * i + 4])
                            ins = mm(B[6][0:nt, 16 + 4 * i:20 + 4 * i], blk, gG[0:nt, 4 * i:4 * i + 4])
                        ins.then_inc(S("gam_mm"), 1)

                after(pe, "proj", l, 4 * N_IN)
                after(pe, "la", l, 1)
                after(pe, "gcols", l, 1)
                for i, (t0, nt) in enumerate(TILES):
                    for h in range(GH):
                        ins = pe.transpose(B[2][0:nt, h * P:(h + 1) * P], v13[:, h, t0:t0 + nt], ident)
                    ins.then_inc(S("gla_tr"), 1)
                    after(pe, "gla_ops", l, i + 1)
                    if i:
                        after(pe, "gla_tok", l, 2 * i)
                    for p in range(2):
                        ins = pe.transpose(B[3][0:nt, p * P:(p + 1) * P], GKE[:, p, 0:nt], ident)
                    ins.then_inc(S("gla_ktr"), 1)
                    if i < 2:
                        for h in range(GH):
                            lo, p = 64 * (h % 2), h // 2
                            for j, nj in enumerate(NJ):
                                s0 = SUB * j
                                ins = mm(GAB[h % 2][s0:s0 + SUB, p * P + s0:(p + 1) * P],
                                         GKT[lo:lo + 64, p, s0:s0 + SUB], GE[j][lo:lo + 64, p, :])
                    else:
                        for h in range(GH):
                            lo, p = 64 * (h % 2), h // 2
                            ins = mm(GAB[h % 2][0:TS, p * TS:(p + 1) * TS], GKT[lo:lo + 64, p, 0:TS], GQD[lo:lo + 64, p, 0:TS])
                    ins.then_inc(S("gla_at_mm"), 1)
                    after(pe, "gla_at", l, i + 1)
                    after(pe, "gla_tok", l, 2 * i + 2)
                    if i == 2:
                        after(pe, "gla_state_in", l, 32)
                    for h in range(GH):
                        lo, p = 64 * (h % 2), h // 2
                        o = GOB[h % 2][:, p * nt:(p + 1) * nt]
                        ins = mm(o, GVT[:, h * P:(h + 1) * P], GAT[:, h * nt:(h + 1) * nt], True, i != 1)
                        if i == 1:
                            ins = mm(o, GS[lo:lo + 64, p, :], GQD[lo:lo + 64, p, :], False, True)
                        if i == 2:
                            for s in range(NSEQ):
                                ins = mm(o[:, s * LSEQ:(s + 1) * LSEQ], GSS[p][lo:lo + 64, s, :],
                                         GQD[lo:lo + 64, p, s * LSEQ:(s + 1) * LSEQ], False, s == NSEQ - 1,
                                         skip_group_check=True)
                    ins.then_inc(S("gla_o_mm"), 1)
                    if i < 2:
                        for h in range(GH):
                            lo, p = 64 * (h % 2), h // 2
                            ins = mm(B[6][lo:lo + 64, p * P:(p + 1) * P], GKDT[:, p * P + lo:p * P + lo + 64],
                                     GVT[:, h * P:(h + 1) * P])
                        ins.then_inc(S("gla_s_mm"), 1)
                        after(pe, "gla_state", l, i + 1)
                    else:
                        for h in range(GH):
                            lo, p = 64 * (h % 2), h // 2
                            after(pe, "gla_vm", l, h + 1)
                            if h == 2:
                                after(pe, "gla_sstate", l, 1)
                            for c in range(2):
                                ins = mm(B[6 + c][lo:lo + 64, :], GKDT[0:TS, p * P + lo:p * P + lo + 64],
                                         GVM[0:TS, 4 * c:4 * c + 4, :])
                            ins.then_inc(S("gla_ss_mm"), 1)
                    after(pe, "gla_o", l, i + 1)
                finish_heads(("heads", 2 * l + 1))

                after(pe, "gla_fin", l, 1)
                def prepare(i):
                    (t0, nt), (DVB, DKB, DKD, DM, DMB, DT, DU, DY, DX) = TILES[i], DSET[i % 2]
                    for b in range(3):
                        if i == 1 and b == 2:
                            after(pe, "dat", l, 1)
                            after(pe, "drowe", l, 1)
                        for h in range(NH):
                            ins = pe.transpose(B[b][0:nt, h * P:(h + 1) * P], cv3[:, 4 * b + h, t0:t0 + nt], ident)
                        ins.then_inc(S("dtr"), 1)
                    tri = cst("tri") if i < 2 else cst("tri_s", TS)
                    for h in range(NH):
                        ins = mm(B[3][:, h * nt:(h + 1) * nt],
                                 gG[0:nt, 4 * i + h:4 * i + h + 1].to_broadcast([nt, P]), tri)
                    ins.then_inc(S("drow"), 1)
                    for b, src in ((4, DT), (5, DU)):
                        after(pe, "dqk", l, 2 * i + b - 3)
                        for h in range(NH):
                            ins = pe.transpose(B[b][:, h * nt:(h + 1) * nt], src[0:nt, h * P:(h + 1) * P], ident[0:nt, 0:nt])
                        ins.then_inc(S("dtb"), 1)
                    after(pe, "dqkT", l, 2 * i + 2)
                    for b, r0 in ((6, 4), (7, 0)):
                        for h in range(NH):
                            kt = cv3[:, 4 + h, t0:t0 + nt]
                            ins = mm(B[b][0:nt, h * nt:(h + 1) * nt], kt, cv3[:, r0 + h, t0:t0 + nt])
                        ins.then_inc(S("dkk"), 1)

                def invert(group):
                    if len(group) > 1:
                        after(pe, "drowe", l, 2)
                    for v in levels_of(group[0]):
                        for i in group:
                            nt = TILES[i][1]
                            DMB, DT, DU, DY = DSET[i % 2][4:8]
                            for hs in range(2):
                                after(pe, "dmb", l, at_level(i, v, hs))
                                if v:
                                    after(pe, "dtu", l, at_level(i, v - 1, hs))
                                for h in (2 * hs, 2 * hs + 1):
                                    c = slice(h * nt, (h + 1) * nt)
                                    ins = mm(YBANK[i % 2][hs][0:nt, (h % 2) * nt:(h % 2 + 1) * nt], DMB[0:nt, c],
                                             DU[0:nt, c] if v else ident[0:nt, 0:nt])
                                ins.then_inc(S("dy_mm"), 1)
                        for i in group if v else ():
                            nt = TILES[i][1]
                            DMB, DT, DU, DY = DSET[i % 2][4:8]
                            for hs in range(2):
                                after(pe, "dy", l, at_update(i, v, hs))
                                bank = TBANK[i % 2][hs]
                                for h in (2 * hs, 2 * hs + 1):
                                    c = slice(h * nt, (h + 1) * nt)
                                    o = (h % 2) * nt
                                    ins = mm(bank[0:nt, o:o + nt], DT[0:nt, c], DY[0:nt, c])
                                for h in (2 * hs, 2 * hs + 1) if v < len(levels_of(i)) - 1 else ():
                                    c = slice(h * nt, (h + 1) * nt)
                                    o = (h % 2) * nt
                                    ins = mm(bank[0:nt, 256 + o:256 + o + nt], DY[0:nt, c], DT[0:nt, c])
                                ins.then_inc(S("dtu_mm"), 1)
                    after(pe, "dtu", l, at_level(group[-1], levels_of(group[-1])[-1], 1))

                def finish(i):
                    (t0, nt), (DVB, DKB, DKD, DM, DMB, DT, DU, DY, DX) = TILES[i], DSET[i % 2]
                    for h in range(NH):
                        ins = mm(B[5][:, h * nt:(h + 1) * nt], DKB[0:nt, h * P:(h + 1) * P], DU[0:nt, h * nt:(h + 1) * nt])
                    ins.then_inc(S("dw_mm"), 1)
                    if i < 2:
                        after(pe, "dw", l, i + 1)
                    else:
                        after(pe, "gdn_state_in", l, 16)
                    for h in range(NH):
                        o = B[6][0:nt, h * P:(h + 1) * P]
                        ins = mm(o, DU[0:nt, h * nt:(h + 1) * nt], DVB[0:nt, h * P:(h + 1) * P], True, i == 0)
                        if i == 1:
                            ins = mm(o, DMB[:, h * nt:(h + 1) * nt], DSP[:, h, :], False, True)
                        if i == 2:
                            after(pe, "dwm", l, h + 1)
                            wm = (DM, DT)[h % 2]
                            for s in range(NSEQ):
                                ins = mm(o, wm[:, s * TS:(s + 1) * TS], DS[:, h, s, :], False, s == NSEQ - 1)
                            if h < NH - 1:
                                ins.then_inc(S("dvn_part"), 1)
                    ins.then_inc(S("dvn_mm"), 1)
                    after(pe, "dvn", l, i + 1)
                    after(pe, "dqd", l, i + 1)
                    for h in range(NH):
                        o = B[7][:, h * nt:(h + 1) * nt]
                        ins = mm(o, DY[0:nt, h * P:(h + 1) * P], cv3[0:nt, 8 + h, t0:t0 + nt], True, i != 1)
                        if i == 1:
                            ins = mm(o, DSP[:, h, :], cv3[:, h, t0:t0 + nt], False, True)
                        if i == 2:
                            for s in range(NSEQ):
                                ins = mm(o[:, s * LSEQ:(s + 1) * LSEQ], DS[:, h, s, :],
                                         cv3[:, h, t0 + s * LSEQ:t0 + (s + 1) * LSEQ], False, s == NSEQ - 1,
                                         skip_group_check=True)
                    ins.then_inc(S("do_mm"), 1)
                    if i < 2:
                        for h in range(NH):
                            ins = mm(B[3][:, h * P:(h + 1) * P], DKD[:, h * P:(h + 1) * P], DY[:, h * P:(h + 1) * P])
                        ins.then_inc(S("ds_mm"), 1)
                        after(pe, "gdn_state", l, i + 1)
                    else:
                        for h in range(NH):
                            after(pe, "dvm", l, h + 1)
                            if h >= 1:
                                after(pe, "gdn_sstate", l, h)
                            vm = (D01, D34)[h % 2]
                            for c in range(2):
                                ins = mm(B[3 + c][:, :], DKD[0:TS, h * P:(h + 1) * P], vm[0:TS, 512 * c:512 * c + 512])
                            ins.then_inc(S("dss_mm"), 1)
                    after(pe, "do", l, i + 1)

                for first in (0, 2):
                    group = (0, 1) if first == 0 else (2,)
                    for i in group:
                        prepare(i)
                    invert(group)
                    for i in group:
                        finish(i)
                finish_heads(("heads", 2 * l + 2))

                after(pe, "hl_out", l, 1)
                for j in range(KD):
                    n = AT_OUT[l] + j // 2
                    if j % 2 == 0:
                        split_in(pe, n)
                    if j >= 2:
                        after(pe, "x_mix", l, j - 1)
                    wh, wl = (v3(x, KD) for x in parts(n))
                    c = slice((j % 2) * P, (j % 2 + 1) * P)
                    for k in range(KD):
                        ins = mm3(B[5 + j % 2][:, 0:T], wh[:, k, c], wl[:, k, c], hh[:, k, :], hl[:, k, :], k == 0, k == KD - 1)
                    ins.then_inc(S("out_mm"), 1)
                sum_squares(("norm", 2 * l + 2))
                if l == 0:
                    pe.wait_ge(S("hl_ff"), 1)
                    for u in range(FD):
                        n = AT_GU + u
                        split_in(pe, n)
                        if u >= 2:
                            pe.wait_ge(S("ff_act"), u - 1)
                        wh, wl = (v3(x, KD) for x in parts(n))
                        for b in range(2):
                            c = slice(b * P, (b + 1) * P)
                            for k in range(KD):
                                ins = mm3(B[2 * b + u % 2][:, 0:T], wh[:, k, c], wl[:, k, c], hh[:, k, :], hl[:, k, :],
                                          k == 0, k == KD - 1)
                        ins.then_inc(S("gu_mm"), 1)
                    pe.wait_ge(S("ff_act"), FD)
                    for j in range(KD):
                        if j >= 2:
                            pe.wait_ge(S("x_ff"), j - 1)
                        for b in range(2):
                            n = AT_DN + 2 * j + b
                            split_in(pe, n)
                            wh, wl = (v3(x[:, 0:width(n)], FD // 2) for x in parts(n))
                            for k in range(FD // 2):
                                f = b * (FD // 2) + k
                                ins = mm3(B[4 + j % 2][:, 0:T], wh[:, k, :], wl[:, k, :], FAH[:, f, :], FAL[:, f, :],
                                          f == 0, f == FD - 1)
                            ins.then_inc(S("down_mm"), 1)

            pe.wait_ge(S("h_norm"), 2 * DEPTH)
            for i, (t0, nt) in enumerate(TILES):
                for k in range(KD):
                    ins = mm(B[0][0:nt, NE * i:NE * (i + 1)], hT[:, k, t0:t0 + nt], wrt[:, k, :], k == 0, k == KD - 1)
            ins.then_inc(S("logits_mm"), 1)
            for i, (t0, nt) in enumerate(TILES):
                for c in range(2):
                    u = 2 * i + c
                    if u >= 2:
                        pe.wait_ge(S("htok"), u - 1)
                    for k in range(4):
                        ins = pe.transpose(B[2 + u % 2][0:nt, k * P:(k + 1) * P], hT[:, 4 * c + k, t0:t0 + nt], ident)
                    ins.then_inc(S("htok_tr"), 1)
            pe.wait_ge(S("sel"), 1)
            for i in range(3):
                for j in range(i + 1):
                    rows = TILES[j][1]
                    m = TILES[i][1]
                    lhsT = cst("strict", rows)[:, 0:m] if j == i else ones[0:rows, 0:m]
                    mm(B[1][0:m, NE * i:NE * (i + 1)], lhsT, sel[0:rows, NE * j:NE * (j + 1)], j == 0, j == i)
            for j in range(3):
                rows = TILES[j][1]
                ins = mm(B[1][:, 32:32 + NE], ones[0:rows, :], sel[0:rows, NE * j:NE * (j + 1)], j == 0, j == 2)
            ins.then_inc(S("pos_mm"), 1)
            pe.wait_ge(S("htok"), 6)

            def gather(g):
                pe.wait_ge(S("onehot"), g)
                for c in range(2):
                    bank = B[1 + 2 * c]
                    for k in range(4):
                        f = slice((4 * c + k) * P, (4 * c + k + 1) * P)
                        for i, (t0, nt) in enumerate(TILES):
                            mm(bank[:, k * P:(k + 1) * P], HTH[0:nt, i, f], ONEH[0:nt, i, :], i == 0, False)
                            ins = mm(bank[:, k * P:(k + 1) * P], HTL[0:nt, i, f], ONEH[0:nt, i, :], False, i == 2)
                    ins.then_inc(S("e_gather_mm"), 1)

            def scatter(el, j):
                if j == 0:
                    pe.wait_ge(S("e_y"), el + 1)
                    pe.wait_ge(S("e_wT"), el + 1)
                if j >= 2:
                    pe.wait_ge(S("e_scatter"), el * KD + j)
                mm(B[4 + j % 2][:, 0:T], YE[:, j * P:(j + 1) * P], ONEWT).then_inc(S("e_sc_mm"), 1)

            def expert(el, r):
                pe.wait_ge(S("e_in"), el * 2 + (2 * r + 2))

                def turn_act(c):
                    pe.wait_ge(S("e_act"), el * NCH + (c + 2))
                    if c == 0:
                        pe.wait_ge(S("e_scatter"), el * KD + (KD + 1))
                    for a in range(4):
                        ins = pe.transpose(B[4 + c % 2][:, a * P:(a + 1) * P], EA[:, c % 2, a * P:(a + 1) * P], ident)
                    ins.then_inc(S("e_tr"), 1)

                for j in range(PER_E):
                    kind, c = ORDER[j // 2]
                    b = j % 2
                    if b == 0 and kind == UP and c >= 1:
                        turn_act(c - 1)
                    if 2 <= j < 2 + KD // 2:
                        scatter(el, 2 * (j - 2))
                        scatter(el, 2 * (j - 2) + 1)
                    if b == 0 and (kind, c) == (DOWN, NCH - 2):
                        gather(el + (r + 2))
                        turn_act(NCH - 1)
                    if b == 0 and (kind, c) == (DOWN, NCH - 1):
                        pe.wait_ge(S("onew"), el + 1)
                        for i, (t0, nt) in enumerate(TILES):
                            ins = pe.transpose(B[2][:, t0:t0 + nt], ONEW[0:nt, i, :], ident[0:nt, 0:nt])
                        ins.then_inc(S("e_wT_mm"), 1)
                    n = AT_MOE + j
                    pe.wait_ge(S("w_low"), el * PER_E + (n + 1))
                    if kind == DOWN:
                        if b == 0:
                            pe.wait_ge(S("e_actT"), el * NCH + (c + 1))
                            if c == 0:
                                pe.wait_ge(S("e_y"), el + 1)
                        wh, wl = (v3(x, 2) for x in parts(n))
                        for a in range(2):
                            f = slice((2 * b + a) * P, (2 * b + a + 1) * P)
                            xh, xl = EATH[:, c % 2, f], EATL[:, c % 2, f]
                            for q in range(2):
                                o, m = B[6 + q][:, :], slice(512 * q, 512 * q + 512)
                                mm(o, xh, wh[:, a, m], c == 0 and b == 0 and a == 0, False)
                                mm(o, xh, wl[:, a, m], False, False)
                                ins = mm(o, xl, wh[:, a, m], False, c == NCH - 1 and b == 1 and a == 1)
                    else:
                        if b == 0:
                            pe.wait_ge(S("e_act"), el * NCH + (c if c >= 2 else 1))
                        o = B[2 * kind + c % 2][:, :]
                        wh, wl = (v3(x, 4) for x in parts(n))
                        for a in range(4):
                            k = 4 * b + a
                            mm(o, HGH[:, k, :], wh[:, a, :], k == 0, False)
                            mm(o, HGH[:, k, :], wl[:, a, :], False, False)
                            ins = mm(o, HGL[:, k, :], wh[:, a, :], False, k == KD - 1)
                    ins.then_inc(KINDS[kind], 1)

            def tail(el):
                for j in range(KD):
                    scatter(el, j)

            gather(1)
            with pe.Fori(0, NE) as e:
                expert(e, 0)
            more = pe.value_load(flag[0:1, 0:1], min_val=0, max_val=1)
            with pe.If(more > 0):
                with pe.Fori(1, MAXPASS) as r:
                    pe.wait_ge(S("e_in"), r * (2 * (NE + 1)))
                    gather(r * (NE + 1) + 1)
                    with pe.Fori(0, NE) as e:
                        expert(r * NE + e, r)
                tail(NE * MAXPASS)
            with pe.If(more < 1):
                tail(NE)
            sum_squares(("norm", 5))

        @block.scalar
        def _(ac):
            own = Own(ac, "act_own")

            def act(out, in_, func, **k):
                return ac.activation(out, in_, func, **k)

            def rsqrt_seed(tag, x=None, y=None):
                x = rv[:, :] if x is None else x
                y = rs[:, :] if y is None else y
                ac.wait_ge(S(f"var_{tag[0]}"), tag[1])
                own.do(act(y, x, ACT.Ln))
                act(y, y, ACT.Exp, scale=-0.5).then_inc(S(f"rs0_{tag[0]}"), 1)

            ac.wait_ge(S("const_in"), 64)
            act(csT[:, :], col("c"), ACT.Silu).then_inc(S("cs_e"), 1)
            for n in range(2):
                split_high(ac, n)
            with ac.Fori(0, H_ADA // TURN) as turn:
                for s in range(TURN // 2):
                    for n in (2 * s + 2, 2 * s + 3):
                        j = n % TURN
                        ac.wait_ge(landed[n % SLOTS], turn * (16 * TURN // SLOTS) + 16 * (n // SLOTS + 1))
                        back = (2, 2, 5)[j] if j < PARTS else PARTS
                        ac.wait_ge(S("ada_mm"), turn * TURN + (PARTS + n - back + 1))
                        act(whi[:, j % PARTS, :], raw[:, n % SLOTS, :], ACT.Copy).then_inc(S("w_high"), 1)
                    ac.wait_ge(S("ada_mm"), turn * TURN + (PARTS + 2 * s + 2))
                    act(AROW[0:2 * NC_, s % 2, :], B[s % 2][0:2 * NC_, :], ACT.Copy).then_inc(S("ada_rows"), 1)
            high = Split(ac, split_high, H_ADA + 2)
            for l in range(DEPTH):
                high.to(AT_IN[l] + 2)
                rsqrt_seed(("norm", 2 * l + 1))
                after(ac, "small_mm", l, 1)
                act(LRT, B[2][0:LR, 0:T], ACT.Copy).then_inc(S("lr_t"), 1)
                after(ac, "gx", l, 1)
                own.do(act(gL[:, :], gX[:, :], ACT.Abs))
                own.do(act(gL[:, :], gL[:, :], ACT.Exp, scale=-1.0))
                act(gL[:, :], gL[:, :], ACT.Ln, bias=1.0)
                act(gEA[:, :], col(f"alog{l}"), ACT.Exp)
                act(v3(gEB[:, :], 3), v3(gAB[:, :], 3)[:, :, NH:2 * NH], ACT.Exp, scale=-1.0).then_inc(S("gact"), 1)
                dest = [None] * CT + [qk3[:, j, :] for j in range(4)] + [v13[:, j, :] for j in range(4)]\
                    + [g13[:, j, :] for j in range(4)] + [zt3[:, j, :] for j in range(4)]

                wc = v3(col(f"wconv{l}"), CT)
                for u in range(4 * N_IN):
                    after(ac, "proj_mm", l, u + 1)
                    if u < CT:
                        if u >= 4:
                            after(ac, "cv_raw", l, u - 3)
                        if u == 0:
                            after(ac, "xp_ready", l, 1)
                        act(cv3[:, u, :], B[u % 2][:, 0:T], ACT.Copy, scale=wc[:, u, CW - 1:CW])
                        act(XP[:, u % 4, CW - 1:], B[u % 2][:, 0:TP], ACT.Copy)
                        act(XS[:, u % 4, :, CW - 1:], v3(B[u % 2][:, TP:T], NSEQ), ACT.Copy).then_inc(S("proj"), 1)
                    else:
                        act(dest[u], B[u % 2][:, 0:T], ACT.Silu if u >= 20 else ACT.Copy).then_inc(S("proj"), 1)
                    if u % 2:
                        high.to(AT_IN[l] + u // 2 + PARTS)
                    if 1 <= u <= CT:
                        after(ac, "cv_raw", l, u)
                        act(cv3[:, u - 1, :], cv3[:, u - 1, :], ACT.Silu).then_inc(S("cv_e"), 1)
                    if u == 5:
                        after(ac, "zb", l, 1)
                        own.do(act(LAE, w(R, 2 * T), ACT.Abs))
                        own.do(act(LAE, LAE, ACT.Exp, scale=-1.0))
                        act(LAE, LAE, ACT.Ln, bias=1.0).then_inc(S("zl"), 1)
                    if u == 9:
                        after(ac, "gamc", l, 1)
                        act(gEG[:, :], gGC[:, :], ACT.Exp)
                        act(gDK[:, :], gD[:, :], ACT.Exp).then_inc(S("gexp"), 1)

                for i, (t0, nt) in enumerate(TILES):
                    la = LA[:, :, t0:t0 + nt]
                    after(ac, "gla_arg", l, i + 1)
                    if i < 2:
                        act(GEA, GEA, ACT.Exp)
                        act(GKT[:, :, 0:nt], GKT[:, :, 0:nt], ACT.Exp)
                    else:
                        act(GKT[:, :, 0:nt], la, ACT.Exp, scale=-1.0)
                    act(GKE[:, :, 0:nt], GKE[:, :, 0:nt], ACT.Exp)
                    act(GQD[:, :, 0:nt], la, ACT.Exp).then_inc(S("gla_exp"), 1)
                    after(ac, "gla_tr", l, i + 1)
                    act(GVT[0:nt, :], B[2][0:nt, :], ACT.Copy).then_inc(S("gla_tok"), 1)
                    after(ac, "gla_ktr", l, i + 1)
                    act(GKDT[0:nt, :], B[3][0:nt, 0:256], ACT.Copy).then_inc(S("gla_tok"), 1)
                    after(ac, "gla_o_mm", l, i + 1)
                    act(hT[:, 0:GH:2, t0:t0 + nt], v3(GOB[0][:, 0:2 * nt], 2), ACT.Copy)
                    act(hT[:, 1:GH:2, t0:t0 + nt], v3(GOB[1][:, 0:2 * nt], 2), ACT.Copy).then_inc(S("gla_o"), 1)
                rsqrt_seed(("heads", 2 * l + 1))

                after(ac, "gla_out", l, 48)
                after(ac, "gla_fin", l, 1)
                def prepare(i):
                    (t0, nt), (DVB, DKB, DKD, DM, DMB, DT, DU, DY, DX) = TILES[i], DSET[i % 2]
                    n4 = 4 * nt
                    for b, dst in ((0, DM), (1, DMB)):
                        after(ac, "dtr", l, 3 * i + b + 1)
                        if i == 2 and b == 0:
                            after(ac, "gdn_state", l, i)
                        act(dst[0:nt, :], B[b][0:nt, :], ACT.Square).then_inc(S("dsq"), 1)
                    rsqrt_seed(("qk", 3 * l + i + 1), rv8[0:nt, :], rs8[0:nt, :])
                    after(ac, "dlog", l, i + 1)
                    own.go(act(DX[0:nt, 0:n4], DX[0:nt, 0:n4], ACT.Exp))
                    act(DY[0:nt, 0:n4], DY[0:nt, 0:n4], ACT.Exp).then_inc(S("dmask"), 1)
                    for b, r0 in ((4, 0), (5, 4)):
                        after(ac, "dtb", l, 2 * i + b - 3)
                        act(cv3[:, r0:r0 + 4, t0:t0 + nt], v3(B[b][:, 0:n4], 4), ACT.Copy).then_inc(S("dqkT"), 1)
                    after(ac, "dat", l, i + 1)
                    act(DX[:, 0:n4], B[3][:, 0:n4], ACT.Exp).then_inc(S("drowe"), 1)

                def invert(group):
                    for v in levels_of(group[0])[1:]:
                        for i in group:
                            nt, DY = TILES[i][1], DSET[i % 2][7]
                            for hs in range(2):
                                after(ac, "dy_mm", l, at_level(i, v, hs))
                                act(DY[0:nt, 2 * hs * nt:(2 * hs + 2) * nt], YBANK[i % 2][hs][0:nt, 0:2 * nt],
                                    ACT.Copy).then_inc(S("dy"), 1)

                def finish(i):
                    (t0, nt), (DVB, DKB, DKD, DM, DMB, DT, DU, DY, DX) = TILES[i], DSET[i % 2]
                    n4 = 4 * nt
                    after(ac, "dw_mm", l, i + 1)
                    act(DMB[:, 0:n4], B[5][:, 0:n4], ACT.Copy, scale=-1.0).then_inc(S("dw"), 1)
                    after(ac, "dvn_mm", l, i + 1)
                    act(DY[0:nt, :], B[6][0:nt, :], ACT.Copy).then_inc(S("dvn"), 1)
                    after(ac, "do_mm", l, i + 1)
                    act(hT[:, GH:, t0:t0 + nt], v3(B[7][:, 0:n4], 4), ACT.Copy).then_inc(S("do"), 1)

                for first in (0, 2):
                    group = (0, 1) if first == 0 else (2,)
                    for i in group:
                        prepare(i)
                    invert(group)
                    for i in group:
                        finish(i)
                rsqrt_seed(("heads", 2 * l + 2))
                for i in range(H_OUT):
                    high.to(AT_OUT[l] + i + PARTS)
                rsqrt_seed(("norm", 2 * l + 2))
                if l == 0:
                    for u in range(FD):
                        ac.wait_ge(S("gu_mm"), u + 1)
                        if u >= 2:
                            ac.wait_ge(S("ff_act"), u - 1)
                        act(FSG[u % 2], B[u % 2][:, 0:T], ACT.Silu).then_inc(S("ff_silu"), 1)
                        high.to(AT_GU + u + PARTS)
                    for i in range(H_DN):
                        high.to(AT_DN + i + PARTS)

            ac.wait_ge(S("lg_shift"), 1)
            act(lgE[:, :], lgE[:, :], ACT.Exp).then_inc(S("lg_exp"), 1)
            for u in range(6):
                i, c = u // 2, u % 2
                nt = TILES[i][1]
                ac.wait_ge(S("htok_tr"), u + 1)
                act(HTH[0:nt, i, 512 * c:512 * c + 512], B[2 + c][0:nt, :], ACT.Copy).then_inc(S("htok_high"), 1)

            def gathered(g):
                for c in range(2):
                    ac.wait_ge(S("e_gather_mm"), g + (c - 1))
                    act(HGH[:, 4 * c:4 * c + 4, :], v3(B[1 + 2 * c][:, :], 4), ACT.Copy).then_inc(S("hg_high"), 1)

            def result_weights(el):
                ac.wait_ge(S("e_wT_mm"), el + 1)
                act(ONEWT, B[2][:, 0:T], ACT.Copy).then_inc(S("e_wT"), 1)

            def result(el):
                ac.wait_ge(S("e_down_mm"), el * (2 * NCH) + PARTS)
                ac.wait_ge(S("e_sc_mm"), el * KD + 1)
                act(YE[:, 0:512], B[6][:, :], ACT.Copy)
                act(YE[:, 512:], B[7][:, :], ACT.Copy).then_inc(S("e_y"), 1)

            def expert(el, r):
                def turned(c):
                    ac.wait_ge(S("e_tr"), el * NCH + (c + 2))
                    act(EATH[:, c % 2, :], B[4 + c % 2][:, :], ACT.Copy).then_inc(S("e_turn_high"), 1)

                for j in range(PARTS):
                    if j == PARTS - 1:
                        result_weights(el)
                    e_split_high(ac, el, j)
                result(el)
                for j in range(PER_E - 2):
                    kind, c = ORDER[j // 2]
                    if kind == GATE and j % 2:
                        ac.wait_ge(S("e_gate_mm"), el * (2 * NCH) + (2 * c + 2))
                        ac.wait_ge(S("e_tr"), el * NCH + (c if c else 1))
                        act(EA[:, c % 2, :], B[c % 2][:, :], ACT.Silu).then_inc(S("e_silu"), 1)
                        if c:
                            turned(c - 1)
                    if j == PER_E - 4:
                        gathered(el * 2 + (2 * r + 4))
                        turned(NCH - 1)
                    if j + PARTS < PER_E:
                        e_split_high(ac, el, j + PARTS)

            gathered(2)
            with ac.Fori(0, NE) as e:
                expert(e, 0)
            more = ac.value_load(flag[0:1, 0:1], min_val=0, max_val=1)
            with ac.If(more > 0):
                with ac.Fori(1, MAXPASS) as r:
                    gathered(r * (2 * (NE + 1)) + 2)
                    with ac.Fori(0, NE) as e:
                        expert(r * NE + e, r)
                result_weights(NE * MAXPASS)
                result(NE * MAXPASS)
            with ac.If(more < 1):
                result_weights(NE)
                result(NE)
            rsqrt_seed(("norm", 5))

        @block.vector
        def _(ve):
            own = Own(ve, "vec_own")
            do, go = own.do, own.go
            tt, ts, stt, cp = ve.tensor_tensor, ve.tensor_scalar, ve.scalar_tensor_tensor, ve.tensor_copy

            def refine(tag, y, v, t):
                ve.wait_ge(S(f"rs0_{tag[0]}"), tag[1])
                do(tt(t, y, y, ALU.mult))
                do(stt(t, t, -0.5, v, ALU.mult, ALU.mult))
                do(stt(y, t, 1.5, y, ALU.add, ALU.mult))

            def norm(tag, shift, scale, ahead=None):
                do(tt(hT[:, :, :], xT[:, :, :], xT[:, :, :], ALU.mult), f"sq_{tag[0]}")
                if ahead is not None:
                    low.to(ahead)
                ve.wait_ge(S(f"ss_{tag[0]}"), tag[1])
                do(ts(rv[:, :], B[0][:, 0:T], 1.0 / D, EPS, ALU.mult, ALU.add), f"var_{tag[0]}")
                refine(tag, rs[:, :], rv[:, :], rt[:, :])
                do(tt(hT[:, :, :], xT[:, :, :], mid(rs[:, :], KD), ALU.mult))
                A_, B_ = md(scale), md(shift)
                for k in range(KD):
                    go(ts(hT[:, k, 0:TP], hT[:, k, 0:TP], A_[:, k, 0:1], B_[:, k, 0:1], ALU.mult, ALU.add))
                hs = hT[:, :, TP:].rearrange("p k (s u) -> p k s u", s=NSEQ)
                do(tt(hs, hs, last(A_[:, :, 1:], LSEQ), ALU.mult))
                do(tt(hs, hs, last(B_[:, :, 1:], LSEQ), ALU.add), f"h_{tag[0]}")

            def finish_heads(tag, h0, gate, weight, done):
                o = hT[:, h0:h0 + 4, :]
                do(tt(v3(QK, 4), o, o, ALU.mult), f"sq_{tag[0]}")
                ve.wait_ge(S(f"ss_{tag[0]}"), tag[1])
                do(ts(rv[:, :], B[0][:, 0:T], 1.0 / GV, EPS, ALU.mult, ALU.add), f"var_{tag[0]}")
                refine(tag, rs[:, :], rv[:, :], rt[:, :])
                go(cp(rt[:, 0:1], rs[:, 0:1]), f"rs_{tag[0]}")
                do(stt(o, v3(gate, 4), weight, o, ALU.mult, ALU.mult))
                ve.wait_ge(S(f"rsb_{tag[0]}"), tag[1])
                for h in range(3):
                    go(tt(o[:, h, :], o[:, h, :], B[1 + h][:, 0:T], ALU.mult))
                do(tt(o[:, 3, :], o[:, 3, :], B[4][:, 0:T], ALU.mult), done)

            def two_parts(name):
                do(cp(hh, hT))
                do(tt(hl, hT, hh, ALU.subtract), name)

            def residual(bank, j, gt, name):
                do(stt(xT[:, j, 0:TP], bank[:, 0:TP], md(gt)[:, j, 0:1], xT[:, j, 0:TP], ALU.mult, ALU.add))
                xs = v3(xT[:, j, TP:], NSEQ)
                do(tt(v3(rt[:, 0:TS], NSEQ), v3(bank[:, TP:T], NSEQ), last(md(gt)[:, j, 1:], LSEQ), ALU.mult))
                do(tt(xs, xs, v3(rt[:, 0:TS], NSEQ), ALU.add), name)

            for name in ("ada_done", "e_act", "e_scatter"):
                ve.sem_inc(S(name), 1)
            ve.memset(gAB[:, :], 0.0)
            ve.wait_ge(S("const_in"), 64)
            ve.tensor_copy(cb[:, :], W[:, KD * P:KD * P + N_CB])
            ve.memset(gGC[:, :], 0.0)
            ve.memset(lgE[:, :], 0.0)
            go(ve.memset(gGL[:, :], 0.0))
            do(ve.memset(cs_r[:, :].bitcast(F32), 0.0))
            ve.wait_ge(S("cs_e"), 1)
            cs3 = v3(csT, KD)
            do(cp(CSP[:, :, 0:NC_], cs3))
            do(tt(CSP[:, :, NC_:2 * NC_], cs3, CSP[:, :, 0:NC_], ALU.subtract), "cs")
            bada = col("b_ada")
            for n in range(2):
                split_low(ve, n)
            with ve.Fori(0, H_ADA // TURN) as turn:
                for s in range(TURN // 2):
                    for n in (2 * s + 2, 2 * s + 3):
                        p = (n % TURN) % PARTS
                        ve.wait_ge(S("w_high"), turn * TURN + (n + 1))
                        tt(wlo[:, p, :], raw[:, n % SLOTS, :], whi[:, p, :], ALU.subtract).then_inc(S("w_low"), 1)
                    ve.wait_ge(S("ada_turned"), turn * (TURN // 2) + (s + 1))
                    tile = (turn * (TURN // 2) + s) * 4
                    tt(mod[:, bass.ds(tile, 4), :], v3(B[2 + s % 2][:, 0:4 * NC_], 4),
                       last(bada[:, bass.ds(tile, 4)], NC_), ALU.add).then_inc(S("ada_done"), 1)
            low = Split(ve, split_low, H_ADA + 2)
            ve.wait_ge(S("ada_done"), N_ADA + 1)
            for name, t in (("nm0", 8), ("nf0", 32), ("nm1", 56), ("nf1", 80), ("nfin", 104)):
                go(stt(md(t), md(t), 1.0, last(col(name), NC_), ALU.add, ALU.mult))
            ve.wait_ge(S("x_in"), 16)
            ve.wait_ge(S("vec_own"), own.n["vec_own"])

            for l in range(DEPTH):
                m0 = 48 * l
                norm(("norm", 2 * l + 1), m0, m0 + 8, AT_IN[l] + 2)
                after(ve, "small_mm", l, 2)
                go(cp(gAB[:, 0:16], B[3][:, 0:16]))
                do(cp(gAB[0:TS, 16:24], B[3][0:TS, 16:24]))
                ab = v3(gAB[:, :], 3)
                do(tt(v3(gX[:, :], 3), ab[:, :, 0:NH], mid(col(f"dtb{l}"), 3), ALU.add), "gx")
                after(ve, "gact", l, 1)
                do(stt(gX[:, :], gX[:, :], 0.0, gL[:, :], ALU.max, ALU.add))
                do(stt(v3(gG[:, :], 3), v3(gX[:, :], 3), -1.0, mid(gEA[:, :], 3), ALU.mult, ALU.mult), "g")
                do(ts(gBE[:, :], gEB[:, :], 1.0, None, ALU.add))
                do(ve.reciprocal(gBE[:, :], gBE[:, :]))
                two_parts("hl_in")
                do(ve.memset(XP[:, :, 0:CW - 1], 0.0), "xp_ready")
                after(ve, "conv_in", l, 16)
                wc = v3(col(f"wconv{l}"), CT)

                for c in range(CT):
                    s = c % 4
                    after(ve, "proj", l, c + 1)
                    do(cp(XS[:, s, :, 0:CW - 1], SC[:, c, :, :]))
                    xs, ys, yp = XS[:, s, :, :], v3(cv3[:, c, TP:], NSEQ), cv3[:, c, 0:TP]
                    for j in range(CW - 1):
                        go(stt(yp, XP[:, s, j:j + TP], wc[:, c, j:j + 1], yp, ALU.mult, ALU.add))
                        do(stt(ys, xs[:, :, j:j + LSEQ], wc[:, c, j:j + 1], ys, ALU.mult, ALU.add))
                    go(cp(OC[:, c, 0, :], XP[:, s, TP:TP + 3]))
                    do(cp(OC[:, c, 1:, :], xs[:, :, LSEQ:LSEQ + 3]), "cv_raw")
                    if c % 2:
                        low.to(AT_IN[l] + c // 2 + PARTS)
                    if c == 4:
                        after(ve, "z_mm", l, 2)
                        go(ts(LA[:, 0, :], B[4][:, 0:T], col(f"bg{l}")[:, 0:1], None, ALU.add))
                        do(ts(LA[:, 1, :], B[5][:, 0:T], col(f"bg{l}")[:, 1:2], None, ALU.add), "zb")
                    if c == 6:
                        after(ve, "zl", l, 1)
                        la = w(R, 2 * T)
                        do(stt(la, la, 0.0, LAE, ALU.min, ALU.subtract))
                        do(ts(la, la, 1.0 / GATE_NORM, None, ALU.mult))
                        for p in range(2):
                            go(ve.tensor_tensor_scan(LAE[:, p * T:(p + 1) * T], cbf("reset"), LA[:, p, :], 0.0, ALU.mult, ALU.add))
                        ve.wait_ge(S("vec_own"), own.n["vec_own"])
                        do(cp(la, LAE), "la")
                    if c == 8:
                        after(ve, "gam_mm", l, 1)
                        for i, (t0, nt) in enumerate(TILES):
                            go(cp(gGC[0:nt, 4 * i:4 * i + 4], B[6][0:nt, 4 * i:4 * i + 4]))
                            do(cp(gGL[0:nt, 4 * i:4 * i + 4], B[6][0:nt, 16 + 4 * i:20 + 4 * i]))
                        do(tt(gD[:, :], gGL[:, :], gGC[:, :], ALU.subtract), "gamc")
                    if c == 10:
                        after(ve, "gexp", l, 1)
                        do(tt(gBG[:, :], gBE[:, :], gEG[:, :], ALU.mult), "gcols")
                go(cp(rt[:, 0:1], rs[:, 0:1]), "conv_done")
                low.to(AT_OUT[l] + 2)

                after(ve, "proj", l, 4 * N_IN)
                after(ve, "conv_out", l, 16)
                for i, (t0, nt) in enumerate(TILES):
                    la = LA[:, :, t0:t0 + nt]
                    q, k = qk3[:, 0:2, t0:t0 + nt], qk3[:, 2:4, t0:t0 + nt]
                    if i:
                        after(ve, "gla_o_mm", l, i)
                        after(ve, "gla_s_mm", l, i)
                    if i < 2:
                        for j, nj in enumerate(NJ):
                            mid_j = LA[:, :, t0 + SUB * j + SUB // 2 - 1]
                            go(tt(GE[j], LA[:, :, t0 + SUB * j:t0 + nt], last(mid_j, nj), ALU.subtract))
                            go(tt(GKT[:, :, SUB * j:SUB * j + SUB], last(mid_j, SUB),
                                  LA[:, :, t0 + SUB * j:t0 + SUB * j + SUB], ALU.subtract))
                        do(tt(GKE, last(LA[:, :, t0 + nt - 1], nt), la, ALU.subtract), "gla_arg")
                    else:
                        for p in range(2):
                            seq = v3(LA[:, p, t0:t0 + nt], NSEQ)
                            ins = tt(v3(GKE[:, p, 0:nt], NSEQ), last(seq[:, :, LSEQ - 1], LSEQ), seq, ALU.subtract)
                            go(ins) if p == 0 else do(ins, "gla_arg")
                    after(ve, "gla_exp", l, i + 1)
                    if i < 2:
                        go(cp(gEB_[:, 0:2], GQD[:, :, P - 1]))
                        for j, nj in enumerate(NJ):
                            go(stt(GE[j], GE[j], GK ** -0.5, qk3[:, 0:2, t0 + SUB * j:t0 + nt], ALU.mult, ALU.mult))
                    else:
                        go(cp(v3(gEB_[:, :], 2), GQD[:, :, LSEQ - 1:TS:LSEQ]))
                    ve.wait_ge(S("vec_own"), own.n["vec_own"])
                    go(tt(GKT[:, :, 0:nt], GKT[:, :, 0:nt], k, ALU.mult))
                    go(tt(GKE[:, :, 0:nt], GKE[:, :, 0:nt], k, ALU.mult))
                    do(stt(GQD[:, :, 0:nt], GQD[:, :, 0:nt], GK ** -0.5, q, ALU.mult, ALU.mult), "gla_ops")
                    after(ve, "gla_at_mm", l, i + 1)
                    if i == 0:
                        do(ve.memset(GAT, 0.0))
                    if i < 2:
                        for j, nj in enumerate(NJ):
                            r0 = SUB * j
                            for e in range(2):
                                ins = tt(v3(GAT, 4)[r0:r0 + SUB, e::2, r0:], v3(GAB[e][:, 0:256], 2)[r0:r0 + SUB, :, r0:],
                                         mid(cst("tri")[r0:r0 + SUB, r0:], 2), ALU.mult)
                                go(ins) if (j, e) != (len(NJ) - 1, 1) else do(ins, "gla_at")
                    else:
                        do(ve.memset(GAT[TS:, 0:4 * TS], 0.0))
                        for e in range(2):
                            ins = tt(v3(GAT[0:TS, 0:4 * TS], 4)[:, e::2, :], v3(GAB[e][0:TS, 0:2 * TS], 2),
                                     mid(cst("tri_s", TS), 2), ALU.mult)
                            go(ins) if e == 0 else do(ins, "gla_at")
                    if i == 0:
                        after(ve, "gla_s_mm", l, 1)
                        do(cp(GS, v3(B[6][:, 0:256], 2)), "gla_state")
                    elif i == 1:
                        after(ve, "gla_s_mm", l, 2)
                        go(stt(GS[:, 0, :], GS[:, 0, :], gEB_[:, 0:1], B[6][:, 0:P], ALU.mult, ALU.add))
                        do(stt(GS[:, 1, :], GS[:, 1, :], gEB_[:, 1:2], B[6][:, P:2 * P], ALU.mult, ALU.add), "gla_state")
                    else:
                        eb = v3(gEB_[:, :], 2)
                        after(ve, "gla_tok", l, 6)
                        for h in range(GH):
                            if h:
                                after(ve, "gla_ss_mm", l, h)
                            if h == 2:
                                for c in range(2):
                                    ins = tt(GSS[0][:, 4 * c:4 * c + 4, :], GSS[0][:, 4 * c:4 * c + 4, :], v3(B[6 + c][:, :], 4), ALU.add)
                                    go(ins) if c == 0 else do(ins, "gla_sstate")
                            do(tt(GVM[0:TS, :, :], mid(GVT[0:TS, h * P:(h + 1) * P], NSEQ), last(cst("seq", TS), GV), ALU.mult), "gla_vm")
                            if h == 0:
                                after(ve, "gla_o_mm", l, 3)
                                for p in range(2):
                                    do(tt(GSS[p], GSS[p], last(eb[:, p, :], GV), ALU.mult))
                        after(ve, "gla_ss_mm", l, GH)
                        for c in range(2):
                            ins = tt(GSS[1][:, 4 * c:4 * c + 4, :], GSS[1][:, 4 * c:4 * c + 4, :], v3(B[6 + c][:, :], 4), ALU.add)
                            go(ins) if c == 0 else do(ins, "gla_sstate")
                after(ve, "gla_o", l, 3)
                finish_heads(("heads", 2 * l + 1), 0, G1, col(f"glan{l}"), "gla_fin")

                after(ve, "gla_out", l, 48)
                def masked(i, v, hs):
                    nt, (DM, DMB) = TILES[i][1], DSET[i % 2][3:5]
                    if v:
                        after(ve, "dy_mm", l, at_level(i, v - 1, hs))
                    c = slice(2 * hs * nt, (2 * hs + 2) * nt)
                    lev = v3(cbf("level", nt), 7)
                    do(tt(v3(DMB[0:nt, c], 2), v3(DM[0:nt, c], 2), mid(lev[:, v, 0:nt], 2), ALU.mult), "dmb")

                def prepare(i):
                    (t0, nt), (DVB, DKB, DKD, DM, DMB, DT, DU, DY, DX) = TILES[i], DSET[i % 2]
                    n4 = 4 * nt
                    gc = gGC[0:nt, 4 * i:4 * i + 4]
                    after(ve, "dsq", l, 2 * i + 2)
                    go(ve.tensor_reduce(rv8[0:nt, 0:4], v3(DM[0:nt, :], 4), AX.X, ALU.add))
                    do(ve.tensor_reduce(rv8[0:nt, 4:8], v3(DMB[0:nt, :], 4), AX.X, ALU.add))
                    do(ts(rv8[0:nt, :], rv8[0:nt, :], EPS, None, ALU.add), "var_qk")
                    after(ve, "drow", l, i + 1)
                    nu, nl = (cbf("neg_u"), cbf("neg_l")) if i < 2 else (cbf("neg_us", TS), cbf("neg_ls", TS))
                    dx, dy = v3(DX[0:nt, 0:n4], 4), v3(DY[0:nt, 0:n4], 4)
                    do(tt(dy, v3(B[3][0:nt, 0:n4], 4), last(gc, nt), ALU.subtract))
                    do(tt(dx, dy, mid(nu, 4), ALU.add))
                    do(tt(dy, mid(nl, 4), dy, ALU.subtract), "dlog")
                    refine(("qk", 3 * l + i + 1), rs8[0:nt, :], rv8[0:nt, :], rt8[0:nt, :])
                    do(ts(rs8[0:nt, 0:4], rs8[0:nt, 0:4], NK ** -0.5, None, ALU.mult))
                    do(tt(v3(DT[0:nt, :], 4), v3(B[0][0:nt, :], 4), last(rs8[0:nt, 0:4], NK), ALU.mult), "dqk")
                    do(tt(v3(DU[0:nt, :], 4), v3(B[1][0:nt, :], 4), last(rs8[0:nt, 4:8], NK), ALU.mult), "dqk")
                    kn = v3(DU[0:nt, :], 4)
                    go(tt(v3(DKD[0:nt, :], 4), kn, last(gDK[0:nt, 4 * i:4 * i + 4], NK), ALU.mult))
                    go(tt(v3(DKB[0:nt, :], 4), kn, last(gBG[0:nt, 4 * i:4 * i + 4], NK), ALU.mult))
                    after(ve, "dtr", l, 3 * i + 3)
                    go(tt(v3(DVB[0:nt, :], 4), v3(B[2][0:nt, :], 4), last(gBE[0:nt, 4 * i:4 * i + 4], NK), ALU.mult))
                    after(ve, "dmask", l, i + 1)
                    after(ve, "dkk", l, 2 * i + 1)
                    do(tt(DM[0:nt, 0:n4], B[6][0:nt, 0:n4], DY[0:nt, 0:n4], ALU.mult))
                    m3 = v3(DM[0:nt, 0:n4], 4)
                    do(tt(m3, m3, last(gBE[0:nt, 4 * i:4 * i + 4], nt), ALU.mult))
                    after(ve, "dkk", l, 2 * i + 2)
                    do(tt(cv3[0:nt, 8:12, t0:t0 + nt], v3(B[7][0:nt, 0:n4], 4), dx, ALU.mult), "dat")
                    after(ve, "dtb", l, 2 * i + 2)
                    for hs in range(2):
                        masked(i, 0, hs)
                        c = slice(2 * hs * nt, (2 * hs + 2) * nt)
                        go(tt(v3(DT[0:nt, c], 2), mid(ident[0:nt, 0:nt], 2), v3(DMB[0:nt, c], 2), ALU.subtract))
                    after(ve, "drowe", l, i + 1)
                    qd = cv3[:, 0:4, t0:t0 + nt]
                    go(tt(qd, qd, v3(DX[:, 0:n4], 4), ALU.mult), "dqd")
                    if i < 2:
                        do(cp(gEL[:, 4 * i:4 * i + 4], v3(DX[:, :], 4)[:, :, P - 1]))
                    else:
                        do(cp(v3(gEL[:, :], 4), v3(DX[:, 0:n4], 4)[:, :, LSEQ - 1:TS:LSEQ]))

                def invert(group):
                    nlev = len(levels_of(group[0]))
                    for v in range(nlev):
                        for i in group:
                            nt, (DT, DU) = TILES[i][1], DSET[i % 2][5:7]
                            for hs in range(2):
                                if v + 1 < nlev:
                                    masked(i, v + 1, hs)
                                c = slice(2 * hs * nt, (2 * hs + 2) * nt)
                                if v == 0:
                                    after(ve, "dy_mm", l, at_level(i, v, hs))
                                    do(tt(v3(DU[0:nt, c], 2), mid(ident[0:nt, 0:nt], 2),
                                          v3(YBANK[i % 2][hs][0:nt, 0:2 * nt], 2), ALU.subtract), "dtu")
                                    continue
                                after(ve, "dtu_mm", l, at_update(i, v, hs))
                                b = TBANK[i % 2][hs]
                                if v < nlev - 1:
                                    go(tt(DT[0:nt, c], DT[0:nt, c], b[0:nt, 256:256 + 2 * nt], ALU.subtract))
                                do(tt(DU[0:nt, c], DU[0:nt, c], b[0:nt, 0:2 * nt], ALU.subtract), "dtu")

                def finish(i):
                    (t0, nt), (DVB, DKB, DKD, DM, DMB, DT, DU, DY, DX) = TILES[i], DSET[i % 2]
                    n4 = 4 * nt
                    if i == 0:
                        after(ve, "ds_mm", l, 1)
                        do(cp(DSP, v3(B[3][:, :], 4)), "gdn_state")
                    elif i == 1:
                        after(ve, "ds_mm", l, 2)
                        for h in range(NH):
                            ins = stt(DSP[:, h, :], DSP[:, h, :], gEL[:, 4 + h:5 + h], B[3][:, h * P:(h + 1) * P], ALU.mult, ALU.add)
                            go(ins) if h < NH - 1 else do(ins, "gdn_state")
                    else:
                        after(ve, "dw", l, 3)
                        w3 = v3(DMB[:, 0:n4], 4)
                        for h in range(NH):
                            if h >= 2:
                                after(ve, "dvn_part", l, h - 1)
                            wm = (DM, DT)[h % 2]
                            if h < 2:
                                do(ve.memset(wm, 0.0))
                            base = (3, 5)[h % 2] * 512
                            diag = w(base, NSEQ * (TS + LSEQ)).rearrange("p (s u) -> p s u", s=NSEQ)[:, :, 0:LSEQ]
                            do(cp(diag, v3(w3[:, h, :], NSEQ)), "dwm")
                        after(ve, "do_mm", l, 3)
                        el4 = v3(gEL[:, :], 4)
                        for h in range(NH):
                            if h >= 2:
                                after(ve, "dss_mm", l, h - 1)
                            vm = v3((D01, D34)[h % 2], NSEQ)
                            do(tt(vm[0:TS, :, :], mid(DY[0:TS, h * P:(h + 1) * P], NSEQ), last(cst("seq", TS), NK), ALU.mult), "dvm")
                            do(tt(DS[:, h, :, :], DS[:, h, :, :], last(el4[:, h, :], NK), ALU.mult))
                            after(ve, "dss_mm", l, h + 1)
                            for c in range(2):
                                d = DS[:, h, 4 * c:4 * c + 4, :]
                                ins = tt(d, d, v3(B[3 + c][:, :], 4), ALU.add)
                                go(ins) if c == 0 else do(ins, "gdn_sstate")

                for first in (0, 2):
                    group = (0, 1) if first == 0 else (2,)
                    for i in group:
                        prepare(i)
                    invert(group)
                    for i in group:
                        finish(i)
                after(ve, "do", l, 3)
                finish_heads(("heads", 2 * l + 2), 4, ZT, col(f"gdnn{l}"), "gdn_fin")
                two_parts("hl_out")
                go(cp(rt[:, 0:1], rs[:, 0:1]), "gdn_done")

                for j in range(KD):
                    after(ve, "out_mm", l, j + 1)
                    residual(B[5 + j % 2], j, m0 + 16, "x_mix")
                    if j % 2:
                        low.to(AT_OUT[l] + j // 2 + 2)
                norm(("norm", 2 * l + 2), m0 + 24, m0 + 32, AT_OUT[l] + H_OUT + 2)
                if l == 0:
                    two_parts("hl_ff")
                    after(ve, "gdn_state_out", 0, 32)
                    for u in range(FD):
                        e = FSG[u % 2]
                        ve.wait_ge(S("ff_silu"), u + 1)
                        do(tt(e, e, B[2 + u % 2][:, 0:T], ALU.mult))
                        do(cp(FAH[:, u, :], e))
                        do(tt(FAL[:, u, :], e, FAH[:, u, :], ALU.subtract), "ff_act")
                        low.to(AT_GU + u + PARTS)
                    for j in range(KD):
                        ve.wait_ge(S("down_mm"), 2 * j + 2)
                        residual(B[4 + j % 2], j, m0 + 40, "x_ff")
                        low.to(AT_DN + 2 * j + 1 + PARTS)

            ve.wait_ge(S("logits_mm"), 1)
            after(ve, "gdn_state_out", DEPTH - 1, 32)
            go(ve.memset(LG[:, :], 0.0))
            ve.wait_ge(S("vec_own"), own.n["vec_own"])
            go(cp(LG[:, 0:16], B[0][:, 0:16]))
            do(cp(LG[0:TS, 16:24], B[0][0:TS, 16:24]))
            lg3 = v3(LG[:, :], 3)
            do(ve.tensor_reduce(mx[:, :], lg3, AX.X, ALU.max))
            do(tt(v3(lgE[:, :], 3), lg3, last(mx[:, :], NE), ALU.subtract), "lg_shift")
            mine = last(LG[:, :], NE)
            for i in range(3):
                c = slice(NE * i, NE * (i + 1))
                mine = last(LG[:, c], NE)
                other = mid(LG[:, c], NE)
                go(tt(CMP[:, c, :], other, mine, ALU.is_gt))
                do(tt(CEQ[:, c, :], other, mine, ALU.is_equal))
                do(tt(CEQ[:, c, :], CEQ[:, c, :], v3(cbf("before"), NE), ALU.mult))
                do(tt(CMP[:, c, :], CMP[:, c, :], CEQ[:, c, :], ALU.add))
            do(ve.tensor_reduce(rank[:, :], CMP, AX.X, ALU.add))
            do(ts(sel[:, :], rank[:, :], 2.0, None, ALU.is_lt), "sel")
            ve.wait_ge(S("lg_exp"), 1)
            do(tt(cw[:, :], lgE[:, :], sel[:, :], ALU.mult))
            do(ve.tensor_reduce(mx[:, :], v3(cw[:, :], 3), AX.X, ALU.add))
            do(ve.reciprocal(mx[:, :], mx[:, :]))
            do(tt(v3(cw[:, :], 3), v3(cw[:, :], 3), last(mx[:, :], NE), ALU.mult))
            for u in range(6):
                i, c = u // 2, u % 2
                nt, f = TILES[i][1], slice(512 * c, 512 * c + 512)
                ve.wait_ge(S("htok_high"), u + 1)
                tt(HTL[0:nt, i, f], B[2 + c][0:nt, :], HTH[0:nt, i, f], ALU.subtract).then_inc(S("htok"), 1)
            ve.wait_ge(S("pos_mm"), 1)
            do(ve.memset(pos[:, :], FAR))
            pos3 = v3(pos[:, :], 3)
            sel3, cw3 = v3(sel[:, :], 3), v3(cw[:, :], 3)
            for i, (t0, nt) in enumerate(TILES):
                do(stt(pos3[0:nt, i, 0:NE], sel3[0:nt, i, :], -FAR, B[1][0:nt, NE * i:NE * (i + 1)], ALU.mult, ALU.add))
                do(ts(pos3[0:nt, i, 0:NE], pos3[0:nt, i, 0:NE], FAR, None, ALU.add))
            do(ve.tensor_reduce(mx[:, 0:1], B[1][:, 32:32 + NE], AX.X, ALU.max))
            do(ts(flag[:, :], mx[:, 0:1], float(CAP), None, ALU.is_gt))
            ve.wait_ge(S("htok_tr"), 6)
            do(ve.memset(hT[:, :, :], 0.0), "flag_ready")

            def onehot(e):
                for i, (t0, nt) in enumerate(TILES):
                    ins = ts(ONEH[0:nt, i, :], cbf("iota", nt), pos3[0:nt, i, bass.ds(e, 1)], None, ALU.is_equal)
                ins.then_inc(S("onehot"), 1)

            def onehot_weights(e):
                for i, (t0, nt) in enumerate(TILES):
                    ins = ts(ONEW[0:nt, i, :], cbf("iota", nt), pos3[0:nt, i, bass.ds(e, 1)],
                             cwp3[0:nt, i, bass.ds(e, 1)], ALU.is_equal, ALU.mult)
                ins.then_inc(S("onew"), 1)

            def gathered(g):
                for c in range(2):
                    ve.wait_ge(S("hg_high"), g + (c - 1))
                    tt(HGL[:, 4 * c:4 * c + 4, :], v3(B[1 + 2 * c][:, :], 4), HGH[:, 4 * c:4 * c + 4, :], ALU.subtract)\
                        .then_inc(S("e_in"), 1)

            def scattered(el, j):
                ve.wait_ge(S("e_sc_mm"), el * KD + (j + 2))
                tt(hT[:, j, :], hT[:, j, :], B[4 + j % 2][:, 0:T], ALU.add).then_inc(S("e_scatter"), 1)

            for z in (B[2], B[6], B[7]):
                go(ve.memset(z[:, :], 0.0))
            do(ve.memset(cwp[:, :], 0.0))
            cwp3 = v3(cwp[:, :], 3)
            do(cp(cwp3[:, :, 0:NE], cw3))
            onehot(0)
            gathered(2)

            def expert(e, el, r):
                def turned(c):
                    ve.wait_ge(S("e_turn_high"), el * NCH + (c + 1))
                    tt(EATL[:, c % 2, :], B[4 + c % 2][:, :], EATH[:, c % 2, :], ALU.subtract).then_inc(S("e_actT"), 1)

                for j in range(PARTS):
                    e_split_low(ve, el, j)
                for j in range(PER_E - 2):
                    kind, c = ORDER[j // 2]
                    if 2 <= j < 2 + KD // 2:
                        scattered(el, 2 * (j - 2))
                        scattered(el, 2 * (j - 2) + 1)
                    if kind == GATE and j % 2 and c:
                        turned(c - 1)
                    if kind == UP and j % 2:
                        ve.wait_ge(S("e_silu"), el * NCH + (c + 1))
                        ve.wait_ge(S("e_up_mm"), el * (2 * NCH) + (2 * c + 2))
                        tt(EA[:, c % 2, :], EA[:, c % 2, :], B[2 + c % 2][:, :], ALU.mult).then_inc(S("e_act"), 1)
                    if j == PER_E - 4:
                        gathered(el * 2 + (2 * r + 4))
                        turned(NCH - 1)
                    if j + PARTS < PER_E:
                        e_split_low(ve, el, j + PARTS)
                    if j == 10:
                        ve.wait_ge(S("e_wT_mm"), el + 1)
                        onehot_weights(e)
                    if j == 14:
                        ve.wait_ge(S("e_gather_mm"), el * 2 + (2 * r + 2))
                        onehot(e + 1)

            def tail(el):
                for j in range(KD):
                    scattered(el, j)
                ve.wait_ge(S("e_scatter"), el * KD + (KD + 1))

            with ve.Fori(0, NE) as e:
                expert(e, e, 0)
            more = ve.value_load(flag[0:1, 0:1], min_val=0, max_val=1)
            with ve.If(more > 0):
                with ve.Fori(1, MAXPASS) as r:
                    ve.wait_ge(S("onew"), r * NE)
                    ve.wait_ge(S("onehot"), r * (NE + 1))
                    ts(pos[:, :], pos[:, :], -float(CAP), None, ALU.add).then_inc(S("shifted"), 1)
                    ve.wait_ge(S("shifted"), r)
                    ve.wait_ge(S("e_gather_mm"), r * (2 * (NE + 1)))
                    onehot(0)
                    gathered(r * (2 * (NE + 1)) + 2)
                    with ve.Fori(0, NE) as e:
                        expert(e, r * NE + e, r)
                tail(NE * MAXPASS)
            with ve.If(more < 1):
                tail(NE)

            for j in range(KD):
                residual(hT[:, j, :], j, 48 + 40, None)
            norm(("norm", 5), 96, 104)
            go(cp(rt[:, 0:1], rs[:, 0:1]), "y_done")
            if len(sems) > 200:
                print(len(sems), "semaphores")


def tiles(a):
    *lead, r, c = a.shape
    return np.moveaxis(a.reshape(*lead, r // P, P, c), -2, -3)


def halves(a, width=CH, rows=KD // 2):
    r, c = a.shape
    t = a.reshape(r // P // rows, rows, P, c // width, width).transpose(3, 0, 2, 1, 4)
    return np.ascontiguousarray(t).reshape(-1, P, rows * width)


def columns(v):
    return np.moveaxis(v.reshape(*v.shape[:-1], -1, P), -1, 0)


def lay_out(x):
    f = np.float32
    out = {}
    xs = np.concatenate([x["x_prompt"].reshape(TP, D), x["x_sample"].reshape(TS, D)], 0)
    out["xT"] = tiles(xs.T)
    q, k, v, lr, g, qkv, a, b, z = np.split(x["w_in"], np.cumsum([256, 256, 512, 16, 512, 1536, 4, 4]), axis=-1)
    big = np.concatenate([qkv, q, k, v, g, z], -1)
    out["wsm"] = tiles(np.concatenate([lr, a, b], -1))
    out["w_in"] = np.stack([halves(big[l], 2 * P, KD) for l in range(DEPTH)])
    out["w_out"] = np.stack([halves(x["w_out"][l], 2 * P, KD) for l in range(DEPTH)])
    out["ada"] = np.concatenate([halves(w) for w in (x["w_ada"][0], x["w_ada"][1], x["w_ada_final"])])
    gate, up = x["w_ff_gate"][0].reshape(D, FD, 1, P), x["w_ff_up"][0].reshape(D, FD, 1, P)
    out["gu"] = halves(np.concatenate([gate, up], 2).reshape(D, 2 * FD * P), 2 * P, KD)
    out["down"] = halves(x["w_ff_down"][0], P, FD // 2)
    moe = np.empty((NE, len(ORDER), 2, P, HALF), f)
    for e in range(NE):
        by_kind = [halves(x["w_exp_gate"][0, e]), halves(x["w_exp_up"][0, e]), halves(x["w_exp_down"][0, e], D, 2)]
        for i, (kind, c) in enumerate(ORDER):
            moe[e, i] = by_kind[kind][2 * c:2 * c + 2]
    out["moe"] = moe.reshape(NE * PER_E, P, HALF)
    out["wgate"] = x["w_gla_gate"]
    out["wrt"] = tiles(x["w_router"][0])
    sm = np.zeros((P, N_SM), f)

    def put(name, val):
        at, n = SM[name]
        sm[:, at:at + n] = val.reshape(P, n)

    c = np.concatenate([x["c_prompt"], x["c_sample"]], 0)
    put("c", tiles(c.T))
    put("b_ada", columns(np.concatenate([x["b_ada"][0], x["b_ada"][1], x["b_ada_final"]])))
    for l in range(DEPTH):
        put(f"nm{l}", columns(x["norm_mix"][l]))
        put(f"nf{l}", columns(x["norm_ffn"][l]))
        put(f"bg{l}", columns(x["b_gla_gate"][l]))
        put(f"wconv{l}", columns(x["w_conv"][l]).transpose(0, 2, 1))
        put(f"glan{l}", columns(x["gla_norm"][l]))
        put(f"gdnn{l}", columns(x["gdn_norm"][l]))
        put(f"alog{l}", np.broadcast_to(x["a_log"][l], (P, NH)))
        put(f"dtb{l}", np.broadcast_to(x["dt_bias"][l], (P, NH)))
    put("nfin", columns(x["norm_final"]))
    out["small"] = sm
    out["cf"], out["cb"] = shape_constants()
    out["s_conv"] = columns(x["state_conv"]).transpose(1, 0, 4, 2, 3)
    out["s_gla"] = x["state_gla"].reshape(DEPTH, NSEQ, 2, P, GV).transpose(0, 2, 3, 1, 4)
    out["s_gdn"] = x["state_gdn"].transpose(0, 3, 2, 1, 4)
    return {k: np.ascontiguousarray(v) for k, v in out.items()}


OUTS = {"y": (P, KD, T), "conv": (DEPTH, P, CT, NC_, 3), "gla_p": (DEPTH, P, 2, GV), "gla_s": (DEPTH, 2, P, NSEQ, GV),
        "gdn_p": (DEPTH, P, NH, NK), "gdn_s": (DEPTH, P, NH, NSEQ, NK)}


def kernel(**inputs):
    import concourse.bacc as bacc
    from concourse.bass_utils import run_bass_kernel_spmd as run

    arrays = lay_out({k: np.asarray(v) for k, v in inputs.items()})
    nc = bacc.Bacc("TRN2", target_bir_lowering=False, num_devices=1)
    A = {k: nc.dram_tensor(f"in_{k}", v.shape, mybir.dt.from_np(v.dtype), kind="ExternalInput").ap()
         for k, v in arrays.items()}
    O = {k: nc.dram_tensor(f"out_{k}", s, F32, kind="ExternalOutput").ap() for k, s in OUTS.items()}
    build(nc, A, O)
    got = run(nc, [{f"in_{k}": v for k, v in arrays.items()}], core_ids=[0]).results[0]
    r = {k: got[f"out_{k}"] for k in OUTS}
    y = np.ascontiguousarray(r["y"].transpose(2, 1, 0)).reshape(T, D)
    conv = r["conv"].transpose(0, 3, 4, 2, 1).reshape(DEPTH, NC_, 3, CT * P)
    gla_p = r["gla_p"].transpose(0, 2, 1, 3).reshape(DEPTH, 1, GH, GK, GV)
    gla_s = r["gla_s"].transpose(0, 3, 1, 2, 4).reshape(DEPTH, NSEQ, GH, GK, GV)
    gdn_p = r["gdn_p"].transpose(0, 2, 1, 3).reshape(DEPTH, 1, NH, NK, NK)
    gdn_s = r["gdn_s"].transpose(0, 3, 2, 1, 4)
    full = [y[:TP].reshape(1, TP, D), y[TP:].reshape(NSEQ, LSEQ, D), gla_p, gdn_p, conv[:, 0:1], gla_s, gdn_s, conv[:, 1:]]
    return tuple(np.ascontiguousarray(a) for a in full)
```

```python
from contextlib import ExitStack

import numpy as np

import concourse.bass as bass
from concourse import mybir

ALU = mybir.AluOpType
ACT = mybir.ActivationFunctionType
AX = mybir.AxisListType
F32 = mybir.dt.float32
F32R = mybir.dt.float32r
BF16 = mybir.dt.bfloat16
I32 = mybir.dt.int32

P = 128
D = 1024
KD = D // P
TP, NSEQ, LSEQ = 256, 8, 8
TS = NSEQ * LSEQ
T = TP + TS
DEPTH = 2
NC_ = 1 + NSEQ
GH, GK, GV = 4, 64, 128
NH, NK = 4, 128
CT = 12
CW = 4
LR = 16
GATE_NORM = 16.0
EPS = 1e-6
FD = 2816 // P
NE = 8
FE = 3584
CH = 512
NCH = FE // CH
HALF = KD * CH // 2
SLOTS = 7
PARTS = 3
N_ADA = 28
UNITS = 29
AB = 32
N_OUT = 2
SUB = 32
WORK = 14080
BIG = -1.0e30
CAP = P
MAXPASS = -(-T // CAP)
TD = KD * T
FAR = 4096.0
TILES = [(0, P), (P, P), (TP, TS)]
LEVELS = [1, 2, 4, 8, 16, 32, 64]

H_ADA, H_IN, H_OUT, H_GU, H_DN = 2 * N_ADA, (UNITS + 1) // 2, 2 * N_OUT, FD, 2 * KD
AT_IN = [H_ADA, H_ADA + H_IN + H_OUT + H_GU + H_DN]
AT_OUT = [a + H_IN for a in AT_IN]
AT_GU = AT_OUT[0] + H_OUT
AT_DN = AT_GU + H_GU
AT_MOE = AT_OUT[1] + H_OUT
GATE, UP, DOWN = range(3)
ORDER = [(GATE, 0), (UP, 0)] + [x for c in range(1, NCH) for x in ((GATE, c), (UP, c), (DOWN, c - 1))] + [(DOWN, NCH - 1)]
PER_E = 2 * len(ORDER)
TURN = 2 * SLOTS

PER_LAYER = {
    "conv_done": 1, "conv_in": 16, "conv_out": 16, "cv_e": 12, "cv_raw": 12, "dat": 3, "dkk": 6, "dlog": 3,
    "dmask": 3, "dmb": 34, "do": 3, "do_mm": 3, "dqd": 3, "dqk": 6, "dqkT": 6, "drow": 3, "drowe": 3, "ds_mm": 2,
    "dsq": 6, "dss_mm": 4, "dtb": 6, "dtr": 9, "dtu": 34, "dtu_mm": 28, "dvm": 4, "dvn": 3, "dvn_mm": 3,
    "dvn_part": 3, "dw": 3, "dw_mm": 3, "dwm": 4, "dy": 28, "dy_mm": 34, "g": 1, "gact": 1, "gam_mm": 1, "gamc": 1,
    "gcols": 1, "gdn_done": 1, "gdn_fin": 4, "gdn_sstate": 4, "gdn_state": 2, "gdn_state_in": 16,
    "gdn_state_out": 32, "gexp": 1, "gla_arg": 3, "gla_at": 3, "gla_at_mm": 3, "gla_exp": 3, "gla_fin": 1,
    "gla_ktr": 3, "gla_o": 3, "gla_o_mm": 3, "gla_ops": 3, "gla_out": 48, "gla_s_mm": 2, "gla_ss_mm": 4,
    "gla_sstate": 2, "gla_state": 2, "gla_state_in": 32, "gla_tok": 6, "gla_tr": 3, "gla_vm": 4, "gx": 1, "hl_in": KD, "hl_out": KD, "la": 1,
    "out_mm": 8, "proj": 29, "proj_mm": 29, "small_mm": 1, "smallw_in": 16, "x_mix": 8, "xp_ready": 1,
    "z_mm": 2, "zb": 1, "zl": 1,
}

SM = {}


def _pack(table, names):
    at = 0
    for name, n in names:
        table[name] = (at, n)
        at += n
    return at


N_SM = _pack(SM, [("c", KD * NC_), ("b_ada", 4 * N_ADA), ("nm0", KD), ("nm1", KD), ("nf0", KD), ("nf1", KD), ("nfin", KD)]
             + [(f"{n}{l}", w) for l in range(DEPTH)
                for n, w in (("bg", 2), ("wconv", CT * CW), ("glan", 1), ("gdnn", 1), ("alog", NH), ("dtb", NH))])
CF = {}
N_CF = _pack(CF, [("ident", P), ("ones", P), ("tri", P), ("tri_s", TS), ("strict", P), ("seq", NSEQ), ("block", TS), ("comb", NC_)])
CB = {}
N_CB = _pack(CB, [("level", len(LEVELS) * P), ("neg_u", P), ("neg_us", TS), ("neg_l", P), ("neg_ls", TS),
                  ("iota", P), ("reset", T), ("before", NE * NE)])


def shape_constants():
    f, b = np.zeros((P, N_CF), np.float32), np.zeros((P, N_CB), np.float32)
    i, j = np.meshgrid(np.arange(P), np.arange(P), indexing="ij")
    si, sj = i[:TS, :TS], j[:TS, :TS]
    same = si // LSEQ == sj // LSEQ

    def put(dst, table, name, v):
        at, n = table[name]
        dst[:v.shape[0], at:at + n] = v

    put(f, CF, "ident", i == j)
    put(f, CF, "ones", np.ones((P, P)))
    put(f, CF, "tri", i <= j)
    put(f, CF, "tri_s", (si <= sj) & same)
    put(f, CF, "strict", i < j)
    put(f, CF, "seq", np.arange(TS)[:, None] // LSEQ == np.arange(NSEQ)[None, :])
    put(f, CF, "block", same)
    put(f, CF, "comb", np.arange(2 * NC_)[:, None] % NC_ == np.arange(NC_)[None, :])
    put(b, CB, "level", np.concatenate(
        [(i // (2 * w) == j // (2 * w)) & (i % (2 * w) >= w) & (j % (2 * w) < w) for w in LEVELS], 1))
    put(b, CB, "neg_u", np.where(i <= j, 0, BIG))
    put(b, CB, "neg_us", np.where((si <= sj) & same, 0, BIG))
    put(b, CB, "neg_l", np.where(i > j, 0, BIG))
    put(b, CB, "neg_ls", np.where((si > sj) & same, 0, BIG))
    put(b, CB, "iota", j)
    t = np.arange(T)
    put(b, CB, "reset", np.tile(np.where(t < TP, t % P != 0, (t - TP) % LSEQ != 0), (P, 1)))
    e = np.arange(NE)
    put(b, CB, "before", np.tile((e[None, :] < e[:, None]).reshape(-1), (P, 1)))
    return f, b


def mid(ap, n):
    return ap.unsqueeze(1).to_broadcast([ap.shape[0], n, ap.shape[1]])


def last(ap, n):
    return ap.unsqueeze(len(ap.shape)).to_broadcast([*ap.shape, n])


def build(nc, A, O):
    ctx = ExitStack()
    with ctx:
        def sb(name, shape, dt=F32):
            return ctx.enter_context(nc.sbuf_tensor(name, shape, dt))

        def sem(name):
            return ctx.enter_context(nc.semaphore(name))

        B = [ctx.enter_context(nc.psum_tensor(f"bank{i}", [P, 512], F32)) for i in range(8)]

        raw = sb("raw", [P, SLOTS, HALF])
        whi = sb("whi", [P, PARTS, HALF], F32R)
        wlo = sb("wlo", [P, PARTS, HALF], F32R)
        xT = sb("xT", [P, KD, T])
        small = sb("small", [P, N_SM])
        cf = sb("cf", [P, N_CF])
        cb = sb("cb", [P, N_CB], BF16)
        mod = sb("mod", [P, 4 * N_ADA, NC_])
        wgate = sb("wgate", [LR, GH * GK])
        wrt = sb("wrt", [P, KD, NE])
        rs = sb("rs", [P, T])
        rv = sb("rv", [P, T])
        csT = rv[:, 0:KD * NC_]
        rt = sb("rt", [P, T])
        rv8, rs8, rt8 = (sb(n, [P, 2 * NH]) for n in ("rv8", "rs8", "rt8"))
        gAB = sb("gate_ab", [P, 3 * 2 * NH])
        gX, gL, gEB, gG, gBE, gGC, gGL, gD, gEG, gDK, gBG = (
            sb(n, [P, 3 * NH]) for n in ("g_x", "g_log", "g_expb", "g_decay", "g_beta", "g_run", "g_end", "g_left",
                                         "g_exprun", "g_expleft", "g_betaexp"))
        gEA = sb("g_expa", [P, NH])
        gEB_ = sb("gla_expend", [P, 2 * NSEQ])
        gEL = sb("g_expend", [P, NH * NSEQ])
        LG = gAB
        lgE, sel, cw = (sb(n, [P, 3 * NE]) for n in ("lg_e", "sel", "cw"))
        rank = cw
        pos, cwp = (sb(n, [P, 3 * (NE + 1)]) for n in ("pos", "cwp"))
        mx = sb("mx", [P, 3])
        warm = sb("warm", [P, 1])
        flag = sb("flag", [P, 1], I32)

        def overlay(*wanted):
            with ExitStack() as over:
                return [over.enter_context(nc.sbuf_tensor(n, [P, size], dt)) for n, size, dt in wanted]

        W, hT_ = overlay(("work", WORK + TD, F32), ("hT", TD, F32))
        _, hh_, hl_ = overlay(("under_h", WORK, F32), ("hh", TD, F32R), ("hl", TD, F32R))
        (cs_r,) = overlay(("cs_parts", KD * P, F32R))
        fah_, fal_ = overlay(("ff_high", FD * T, F32R), ("ff_low", FD * T, F32R))
        hth_, htl_, oneh_, hgh_, hgl_, eath_, eatl_, _ = overlay(
            ("htok_high", 3 * D, F32R), ("htok_low", 3 * D, F32R), ("onehot", 3 * P, F32R), ("hg_high", D, F32R),
            ("hg_low", D, F32R), ("act_high", 2 * CH, F32R), ("act_low", 2 * CH, F32R), ("rest", 16, F32))
        _ = sb("region", [P, WORK + 2 * TD])
        hT, hh, hl = (t[:, :].rearrange("p (k t) -> p k t", k=KD) for t in (hT_, hh_, hl_))

        def w(at, n):
            return W[:, at:at + n]

        def v3(ap, a):
            return ap.rearrange("p (a b) -> p a b", a=a)

        def col(name):
            at, n = SM[name]
            return small[:, at:at + n]

        def cst(name, rows=P):
            at, n = CF[name]
            return cf[0:rows, at:at + n]

        def cbf(name, rows=P):
            at, n = CB[name]
            return cb[0:rows, at:at + n]

        ident, ones = cst("ident"), cst("ones")
        TL = 4 * T
        QK, V1, G1, ZT = w(0, TL), w(TL, TL), w(2 * TL, TL), w(3 * TL, TL)
        CV = w(4 * TL, 3 * TL)
        R = 7 * TL
        qk3, v13, g13, zt3, cv3 = v3(QK, 4), v3(V1, 4), v3(G1, 4), v3(ZT, 4), v3(CV, CT)
        LA = v3(w(R, 2 * T), 2)
        R1 = R + 2 * T
        XPW, XSW = TP + CW - 1, LSEQ + CW - 1
        at = R1

        def take(n):
            nonlocal at
            at += n
            assert at <= WORK + TD, at
            return w(at - n, n)

        XP = v3(take(4 * XPW), 4)
        XS = take(4 * NSEQ * XSW).rearrange("p (c s u) -> p c s u", c=4, s=NSEQ)
        OC = take(CT * NC_ * 3).rearrange("p (c s u) -> p c s u", c=CT, s=NC_)
        SC = take(CT * NSEQ * 3).rearrange("p (c s u) -> p c s u", c=CT, s=NSEQ)
        AR = AB + 2 * NH
        LRT = take(T)[0:AB + 2 * NH, :]
        LAE = take(2 * T)
        at = R1
        NJ = [P - SUB * j for j in range(P // SUB)]

        def gla_set():
            gea = take(2 * sum(NJ))
            return [gea, [v3(gea[:, 2 * sum(NJ[:j]):2 * sum(NJ[:j + 1])], 2) for j in range(len(NJ))]]\
                + [v3(take(256), 2) for _ in range(3)]

        GSET = [gla_set()]
        GVT = take(512)
        GKDT = take(256)
        GAT = take(512)
        GS = v3(take(256), 2)
        GVM = v3(take(1024), NSEQ)
        GSS = [v3(w(TL, 1024), NSEQ), v3(take(1024), NSEQ)]
        GSET.append(gla_set())
        GQ2 = GSET[1][4]
        DS = w(R, NH * NSEQ * NK).rearrange("p (h s v) -> p h s v", h=NH, s=NSEQ)
        at = R + NH * NSEQ * NK
        DSP = v3(take(NH * NK), NH)
        DSET = [[w(512 * i, 512) for i in range(7)] + [take(512), take(512)],
                [w(R + 512 * i, 512) for i in range(8)] + [take(512)]]
        DM, DMB, DT, DY = DSET[0][3], DSET[0][4], DSET[0][5], DSET[0][7]
        D01, D34 = w(0, 1024), w(3 * 512, 1024)
        WQ_AT = (WORK, WORK + NSEQ * P)
        SBANK = ((B[3], B[4]), (B[1], B[2]))
        STATE_AT = (0, 1, 3, 4)
        YBANK, TBANK = ((B[0], B[1]), (B[5], B[6])), ((B[2], B[4]), (B[3], B[7]))
        SQ = v3(w(4 * TL, TD), KD)
        FAH, FAL = v3(fah_[:, :], FD), v3(fal_[:, :], FD)
        FSG = [rs[:, :], rv[:, :]]
        CSP = v3(cs_r[:, :], KD)
        at = KD * P + N_CB
        AROW = v3(take(2 * CH), 2)
        HTH, HTL, ONEH = (v3(t[:, :], 3) for t in (hth_, htl_, oneh_))
        HGH, HGL = v3(hgh_[:, :], KD), v3(hgl_[:, :], KD)
        EATH, EATL = v3(eath_[:, :], 2), v3(eatl_[:, :], 2)
        at = 2 * 3 * D + 3 * P + 2 * D + 4 * CH
        ONEW = v3(take(3 * P), 3)
        ONEWT = take(T)
        EA = v3(take(2 * CH), 2)
        YE = take(D)
        CMP, CEQ = (take(3 * NE * NE).rearrange("p (a b) -> p a b", b=NE) for _ in range(2))

        GAB, GOB = (B[4], B[7]), (B[5], B[0])

        sems = {}

        def S(name):
            if name not in sems:
                sems[name] = sem(name)
            return sems[name]

        def after(eng, name, l, v):
            eng.wait_ge(S(name), PER_LAYER[name] * l + v)

        landed = [S(f"landed{s}") for s in range(SLOTS)]

        def part(n):
            return (n % TURN) % PARTS if n < H_ADA else (n - H_ADA) % PARTS

        def used(n):
            if n < AT_IN[0]:
                return S("ada_mm"), PARTS + n + 1
            for l in range(DEPTH):
                if AT_IN[l] <= n < AT_OUT[l]:
                    return S("proj_mm"), PER_LAYER["proj_mm"] * l + min(2 * (n - AT_IN[l] + 1), UNITS)
                if AT_OUT[l] <= n < AT_OUT[l] + H_OUT:
                    return S("out_mm"), PER_LAYER["out_mm"] * l + 2 * (n - AT_OUT[l] + 1)
            if n < AT_DN:
                return S("gu_mm"), n - AT_GU + 1
            return S("down_mm"), n - AT_DN + 1

        KINDS = [S("e_gate_mm"), S("e_up_mm"), S("e_down_mm")]

        def split_high(ac, n):
            ac.wait_ge(landed[n % SLOTS], 16 * (n // SLOTS + 1))
            before = [m for m in range(n - 1, max(n - 8, -1), -1) if part(m) == part(n)]
            if before:
                ac.wait_ge(*used(before[0]))
            ac.activation(whi[:, part(n), 0:width(n)], raw[:, n % SLOTS, 0:width(n)], ACT.Copy).then_inc(S("w_high"), 1)

        def split_low(ve, n):
            ve.wait_ge(S("w_high"), n + 1)
            ve.tensor_tensor(wlo[:, part(n), 0:width(n)], raw[:, n % SLOTS, 0:width(n)], whi[:, part(n), 0:width(n)],
                             ALU.subtract).then_inc(S("w_low"), 1)

        def width(n):
            return FD * P // 2 if AT_DN <= n < AT_DN + H_DN else HALF

        def split_in(pe, n):
            pe.wait_ge(S("w_low"), n + 1)

        def levels_of(i):
            return range(7 if i < 2 else 3)

        def at_level(i, v, hs):
            return (4 * v + 2 * i if i < 2 else 28 + 2 * v) + hs + 1

        def at_update(i, v, hs):
            return (4 * (v - 1) + 2 * i if i < 2 else 24 + 2 * (v - 1)) + hs + 1

        class Split:

            def __init__(self, eng, one, first):
                self.eng, self.one, self.next = eng, one, first

            def to(self, n):
                while self.next <= min(n, AT_MOE - 1):
                    self.one(self.eng, self.next)
                    self.next += 1

        def e_used(el, j):
            kind, c = ORDER[j // 2]
            v = 2 * c + j % 2 + 1
            return KINDS[kind], el * (2 * NCH) + v + (PARTS if kind == DOWN else 0)

        def e_split_high(ac, el, j):
            n = AT_MOE + j
            ac.wait_ge(landed[n % SLOTS], el * (16 * PER_E // SLOTS) + 16 * (n // SLOTS + 1))
            if j >= PARTS:
                ac.wait_ge(*e_used(el, j - PARTS))
            else:
                ac.wait_ge(S("e_down_mm"), el * (2 * NCH) + (j + 1))
            ac.activation(whi[:, part(n), :], raw[:, n % SLOTS, :], ACT.Copy).then_inc(S("w_high"), 1)

        def e_split_low(ve, el, j):
            n = AT_MOE + j
            ve.wait_ge(S("w_high"), el * PER_E + (n + 1))
            ve.tensor_tensor(wlo[:, part(n), :], raw[:, n % SLOTS, :], whi[:, part(n), :], ALU.subtract)\
              .then_inc(S("w_low"), 1)

        class Own:

            def __init__(self, eng, name):
                self.eng, self.name, self.n = eng, name, {}

            def go(self, ins, name=None):
                name = name or self.name
                self.n[name] = self.n.get(name, 0) + 1
                ins.then_inc(S(name), 1)

            def do(self, ins, name=None):
                self.go(ins, name)
                self.eng.wait_ge(S(name or self.name), self.n[name or self.name])

        block = ctx.enter_context(nc.Block())

        def md(base, n=KD):
            return mod[:, base:base + n, :]

        @block.sync
        def _(sp):
            for dst, src in ((small, A["small"]), (cf, A["cf"]), (W[:, KD * P:KD * P + N_CB], A["cb"]), (wrt, A["wrt"])):
                sp.dma_start(dst[:, :] if dst is not wrt else wrt[:, :, :], src).then_inc(S("const_in"), 16)
            sp.dma_start(xT[:], A["xT"]).then_inc(S("x_in"), 16)

            def load(n, src):
                if n >= SLOTS:
                    sp.wait_ge(S("w_low"), n - SLOTS + 1)
                sp.dma_start(raw[:, n % SLOTS, 0:width(n)], src).then_inc(landed[n % SLOTS], 16)

            for n in range(TURN):
                load(n, A["ada"][n, :, :])
            with sp.Fori(1, H_ADA // TURN) as turn:
                for j in range(TURN):
                    sp.wait_ge(S("w_low"), turn * TURN + (j - SLOTS + 1))
                    sp.dma_start(raw[:, j % SLOTS, :], A["ada"][turn * TURN + j, :, :]).then_inc(landed[j % SLOTS], 16)
            for l in range(DEPTH):
                for i in range(H_IN):
                    load(AT_IN[l] + i, A["w_in"][l, i, :, :])
                for i in range(H_OUT):
                    load(AT_OUT[l] + i, A["w_out"][l, i, :, :])
                if l == 0:
                    for i in range(H_GU):
                        load(AT_GU + i, A["gu"][i, :, :])
                    for i in range(H_DN):
                        load(AT_DN + i, A["down"][i, :, :])

            def expert(e, el):
                for j in range(PER_E):
                    n = AT_MOE + j
                    sp.wait_ge(S("w_low"), el * PER_E + (n - SLOTS + 1))
                    sp.dma_start(raw[:, n % SLOTS, :], A["moe"][e * PER_E + j, :, :]).then_inc(landed[n % SLOTS], 16)

            with sp.Fori(0, NE) as e:
                expert(e, e)
            sp.wait_ge(S("flag_ready"), 1)
            more = sp.value_load(flag[0:1, 0:1], min_val=0, max_val=1)
            with sp.If(more > 0):
                with sp.Fori(1, MAXPASS) as r:
                    with sp.Fori(0, NE) as e:
                        expert(e, r * NE + e)

        @block.gpsimd
        def _(po):
            waits = []

            def store(dst, src, name):
                po.dma_start(dst, src).then_inc(S(name), 16)
                waits.append(name)

            for l in range(DEPTH):
                if l:
                    after(po, "z_mm", 0, 2)
                    after(po, "small_mm", 0, 1)
                    after(po, "gdn_done", 0, 1)
                po.dma_start(wgate[:], A["wgate"][l, :, :]).then_inc(S("smallw_in"), 16)
                if l:
                    po.wait_ge(S("down_mm"), H_DN)
                po.dma_start(SC, A["s_conv"][l, :, :, :, :]).then_inc(S("conv_in"), 16)
                after(po, "conv_done", l, 1)
                store(O["conv"][l, :, :, :, :], OC, "conv_out")
                after(po, "proj_mm", l, UNITS)
                po.dma_start(GSS[1], A["s_gla"][l, 1, :, :, :]).then_inc(S("gla_state_in"), 16)
                after(po, "gla_tr", l, 3)
                po.dma_start(GSS[0], A["s_gla"][l, 0, :, :, :]).then_inc(S("gla_state_in"), 16)
                after(po, "gla_state", l, 2)
                store(O["gla_p"][l, :, :, :], GS, "gla_out")
                for p in range(2):
                    after(po, "gla_sstate", l, p + 1)
                    store(O["gla_s"][l, p, :, :, :], GSS[p], "gla_out")
                after(po, "gdn_state", l, 2)
                po.dma_start(DS, A["s_gdn"][l, :, :, :, :]).then_inc(S("gdn_state_in"), 16)
                store(O["gdn_p"][l, :, :, :], DSP, "gdn_state_out")
                after(po, "gdn_sstate", l, NH)
                store(O["gdn_s"][l, :, :, :, :], DS, "gdn_state_out")
            po.wait_ge(S("y_done"), 1)
            store(O["y"], hT[:], "y_out")
            for name in dict.fromkeys(waits):
                po.wait_ge(S(name), 16 * waits.count(name))

        @block.tensor
        def _(pe):
            def mm(out, lhsT, rhs, start=True, stop=True, **k):
                return pe.matmul(out, lhsT, rhs, start=start, stop=stop, **k)

            def sum_squares(t, sq, j):
                pe.wait_ge(S("sq_norm"), KD * (t - 1) + (j + 1))
                ins = mm(B[0][:, 0:T], ones, sq[:, j, :], j == 0, j == KD - 1)
                if j == KD - 1:
                    ins.then_inc(S("ss_norm"), 1)

            def finish_heads(tag, sq):
                pe.wait_ge(S(f"sq_{tag[0]}"), tag[1])
                q = v3(sq, 4)
                for h in range(4):
                    ins = mm(B[0][32 * h:32 * h + 32, 0:T], ones[:, 0:32], q[:, h, :])
                ins.then_inc(S(f"ss_{tag[0]}"), 1)
                pe.wait_ge(S(f"rs_{tag[0]}"), tag[1])
                for h in range(4):
                    ins = mm(B[1 + h][:, 0:T], ident[:, 32 * h:32 * h + 1].to_broadcast([P, P]), rs[:, :])
                ins.then_inc(S(f"rsb_{tag[0]}"), 1)

            def mm3(out, w_high, w_low, x_high, x_low, first, last):
                mm(out, w_high, x_high, first, False)
                mm(out, w_low, x_high, False, False)
                return mm(out, w_high, x_low, False, last)

            def parts(n):
                return whi[:, part(n), :], wlo[:, part(n), :]

            pe.wait_ge(S("const_in"), 64)
            pe.wait_ge(S("cs"), 1)
            for name, v in (("e_tr", 1), ("e_sc_mm", 1), ("e_wT_mm", 1), ("e_down_mm", PARTS), ("ada_mm", PARTS)):
                pe.sem_inc(S(name), v)
            with pe.Fori(0, H_ADA // TURN) as turn:
                for s in range(TURN // 2):
                    for b in range(2):
                        n = 2 * s + b
                        pe.wait_ge(S("w_low"), turn * TURN + (n + 1))
                        wh, wl = (v3(x, KD // 2) for x in parts(n))
                        for k in range(KD // 2):
                            c = CSP[:, 4 * b + k, :]
                            mm(B[s % 2][:, :], c, wh[:, k, :], n % 2 == 0 and k == 0, False)
                            ins = mm(B[s % 2][:, :], c, wl[:, k, :], False, b == 1 and k == 3)
                        ins.then_inc(S("ada_mm"), 1)
                    pe.wait_ge(S("ada_rows"), turn * (TURN // 2) + (s + 1))
                    pe.wait_ge(S("ada_done"), turn * (TURN // 2) + (1 if s < 2 else s))
                    for j in range(4):
                        ins = mm(B[2 + s % 2][:, j * NC_:(j + 1) * NC_], AROW[0:2 * NC_, s % 2, j * P:(j + 1) * P],
                                 cst("comb", 2 * NC_))
                    ins.then_inc(S("ada_turned"), 1)

            for l in range(DEPTH):
                if l == 0:
                    for j in range(KD):
                        sum_squares(1, hT, j)
                for u in range(UNITS):
                    n = AT_IN[l] + u // 2
                    if u % 2 == 0:
                        split_in(pe, n)
                    if u >= 2:
                        after(pe, "proj", l, u - 1)
                    wh, wl = (v3(x, KD) for x in parts(n))
                    c = slice((u % 2) * P, (u % 2 + 1) * P)
                    for k in range(KD):
                        if u == 0:
                            after(pe, "hl_in", l, k + 1)
                        ins = mm3(B[u % 2][:, 0:T], wh[:, k, c], wl[:, k, c], hh[:, k, :], hl[:, k, :], k == 0, k == KD - 1)
                    ins.then_inc(S("proj_mm"), 1)
                    if u == 1:
                        after(pe, "proj", l, 1)
                        for i, (t0, nt) in enumerate(TILES):
                            ins = pe.transpose(B[3][0:nt, AR * i:AR * (i + 1)], LRT[:, t0:t0 + nt], ident[0:AR, 0:AR])
                        ins.then_inc(S("small_mm"), 1)
                    if u == 2:
                        after(pe, "smallw_in", l, 16)
                        for p in range(2):
                            mm(B[4 + p][:, 0:T], wgate[:, p * P:(p + 1) * P], LRT[0:LR, :]).then_inc(S("z_mm"), 1)
                    if u == 8:
                        after(pe, "g", l, 1)
                        for i, (t0, nt) in enumerate(TILES):
                            tri, blk = (cst("tri"), ones) if i < 2 else (cst("tri_s", TS), cst("block", TS))
                            mm(B[6][0:nt, 4 * i:4 * i + 4], tri, gG[0:nt, 4 * i:4 * i + 4])
                            ins = mm(B[6][0:nt, 16 + 4 * i:20 + 4 * i], blk, gG[0:nt, 4 * i:4 * i + 4])
                        ins.then_inc(S("gam_mm"), 1)

                after(pe, "proj", l, UNITS)
                after(pe, "la", l, 1)
                after(pe, "gcols", l, 1)
                for i, (t0, nt) in enumerate(TILES):
                    _, GE, GKT, GKE, GQD = GSET[i % 2]
                    for h in range(GH):
                        ins = pe.transpose(B[2][0:nt, h * P:(h + 1) * P], v13[:, h, t0:t0 + nt], ident)
                    ins.then_inc(S("gla_tr"), 1)
                    after(pe, "gla_ops", l, i + 1)
                    if i:
                        after(pe, "gla_tok", l, 2 * i)
                    for p in range(2):
                        ins = pe.transpose(B[3][0:nt, p * P:(p + 1) * P], GKE[:, p, 0:nt], ident)
                    ins.then_inc(S("gla_ktr"), 1)
                    if i < 2:
                        for h in range(GH):
                            lo, p = 64 * (h % 2), h // 2
                            for j, nj in enumerate(NJ):
                                s0 = SUB * j
                                ins = mm(GAB[h % 2][s0:s0 + SUB, p * P + s0:(p + 1) * P],
                                         GKT[lo:lo + 64, p, s0:s0 + SUB], GE[j][lo:lo + 64, p, :])
                    else:
                        for h in range(GH):
                            lo, p = 64 * (h % 2), h // 2
                            ins = mm(GAB[h % 2][0:TS, p * TS:(p + 1) * TS], GKT[lo:lo + 64, p, 0:TS], GQD[lo:lo + 64, p, 0:TS])
                    ins.then_inc(S("gla_at_mm"), 1)
                    after(pe, "gla_at", l, i + 1)
                    after(pe, "gla_tok", l, 2 * i + 2)
                    if i == 2:
                        after(pe, "gla_state_in", l, 32)
                    for h in range(GH):
                        lo, p = 64 * (h % 2), h // 2
                        o = GOB[h % 2][:, p * nt:(p + 1) * nt] if i < 2 else B[5][:, h * nt:(h + 1) * nt]
                        ins = mm(o, GVT[:, h * P:(h + 1) * P], GAT[:, h * nt:(h + 1) * nt], i < 2 or h % 2 == 0, i == 0,
                                 skip_group_check=i == 2)
                        if i == 1:
                            ins = mm(o, GS[lo:lo + 64, p, :], GQD[lo:lo + 64, p, :], False, True)
                        if i == 2 and h % 2:
                            pair = v3(B[5][:, 2 * p * TS:2 * (p + 1) * TS], 2)
                            for q in range(NSEQ):
                                c = slice(q * LSEQ, (q + 1) * LSEQ)
                                ins = mm(pair[:, :, c], GSS[p][:, q, :], v3(GQ2[:, p, :], 2)[:, :, c], False, q == NSEQ - 1,
                                         skip_group_check=True)
                    ins.then_inc(S("gla_o_mm"), 1)
                    if i < 2:
                        for h in range(GH):
                            lo, p = 64 * (h % 2), h // 2
                            ins = mm(B[6][lo:lo + 64, p * P:(p + 1) * P], GKDT[:, p * P + lo:p * P + lo + 64],
                                     GVT[:, h * P:(h + 1) * P])
                        ins.then_inc(S("gla_s_mm"), 1)
                        after(pe, "gla_state", l, i + 1)
                    else:
                        for h in range(GH):
                            lo, p = 64 * (h % 2), h // 2
                            after(pe, "gla_vm", l, h + 1)
                            if h == 2:
                                after(pe, "gla_sstate", l, 1)
                            for c in range(2):
                                ins = mm(B[6 + c][lo:lo + 64, :], GKDT[0:TS, p * P + lo:p * P + lo + 64],
                                         GVM[0:TS, 4 * c:4 * c + 4, :])
                            ins.then_inc(S("gla_ss_mm"), 1)
                    after(pe, "gla_o", l, i + 1)
                finish_heads(("heads", 2 * l + 1), QK)

                after(pe, "gla_fin", l, 1)
                def prepare(i):
                    (t0, nt), (DVB, DKB, DKD, DM, DMB, DT, DU, DY, DX) = TILES[i], DSET[i % 2]
                    for b in range(3):
                        if i == 1 and b == 2:
                            after(pe, "dat", l, 1)
                            after(pe, "drowe", l, 1)
                        for h in range(NH):
                            ins = pe.transpose(B[b][0:nt, h * P:(h + 1) * P], cv3[:, 4 * b + h, t0:t0 + nt], ident)
                        ins.then_inc(S("dtr"), 1)
                    tri = cst("tri") if i < 2 else cst("tri_s", TS)
                    for h in range(NH):
                        ins = mm(B[3][:, h * nt:(h + 1) * nt],
                                 gG[0:nt, 4 * i + h:4 * i + h + 1].to_broadcast([nt, P]), tri)
                    ins.then_inc(S("drow"), 1)
                    for b, src in ((4, DT), (5, DU)):
                        after(pe, "dqk", l, 2 * i + b - 3)
                        for h in range(NH):
                            ins = pe.transpose(B[b][:, h * nt:(h + 1) * nt], src[0:nt, h * P:(h + 1) * P], ident[0:nt, 0:nt])
                        ins.then_inc(S("dtb"), 1)
                    after(pe, "dqkT", l, 2 * i + 2)
                    for b, r0 in ((6, 4), (7, 0)):
                        for h in range(NH):
                            kt = cv3[:, 4 + h, t0:t0 + nt]
                            ins = mm(B[b][0:nt, h * nt:(h + 1) * nt], kt, cv3[:, r0 + h, t0:t0 + nt])
                        ins.then_inc(S("dkk"), 1)

                def invert(group):
                    if len(group) > 1:
                        after(pe, "drowe", l, 2)
                    for v in levels_of(group[0]):
                        for i in group:
                            nt = TILES[i][1]
                            DMB, DT, DU, DY = DSET[i % 2][4:8]
                            for hs in range(2):
                                after(pe, "dmb", l, at_level(i, v, hs))
                                if v:
                                    after(pe, "dtu", l, at_level(i, v - 1, hs))
                                for h in (2 * hs, 2 * hs + 1):
                                    c = slice(h * nt, (h + 1) * nt)
                                    ins = mm(YBANK[i % 2][hs][0:nt, (h % 2) * nt:(h % 2 + 1) * nt], DMB[0:nt, c],
                                             DU[0:nt, c] if v else ident[0:nt, 0:nt])
                                ins.then_inc(S("dy_mm"), 1)
                        for i in group if v else ():
                            nt = TILES[i][1]
                            DMB, DT, DU, DY = DSET[i % 2][4:8]
                            for hs in range(2):
                                after(pe, "dy", l, at_update(i, v, hs))
                                bank = TBANK[i % 2][hs]
                                for h in (2 * hs, 2 * hs + 1):
                                    c = slice(h * nt, (h + 1) * nt)
                                    o = (h % 2) * nt
                                    ins = mm(bank[0:nt, o:o + nt], DT[0:nt, c], DY[0:nt, c])
                                for h in (2 * hs, 2 * hs + 1) if v < len(levels_of(i)) - 1 else ():
                                    c = slice(h * nt, (h + 1) * nt)
                                    o = (h % 2) * nt
                                    ins = mm(bank[0:nt, 256 + o:256 + o + nt], DY[0:nt, c], DT[0:nt, c])
                                ins.then_inc(S("dtu_mm"), 1)
                    after(pe, "dtu", l, at_level(group[-1], levels_of(group[-1])[-1], 1))

                def finish(i):
                    (t0, nt), (DVB, DKB, DKD, DM, DMB, DT, DU, DY, DX) = TILES[i], DSET[i % 2]
                    for h in range(NH):
                        ins = mm(B[5][:, h * nt:(h + 1) * nt], DKB[0:nt, h * P:(h + 1) * P], DU[0:nt, h * nt:(h + 1) * nt])
                    ins.then_inc(S("dw_mm"), 1)
                    if i < 2:
                        after(pe, "dw", l, i + 1)
                    else:
                        after(pe, "gdn_state_in", l, 16)
                    for h in range(NH):
                        o = B[6][0:nt, h * P:(h + 1) * P]
                        if i < 2:
                            ins = mm(o, DU[0:nt, h * nt:(h + 1) * nt], DVB[0:nt, h * P:(h + 1) * P], True, i == 0)
                        if i == 1:
                            ins = mm(o, DMB[:, h * nt:(h + 1) * nt], DSP[:, h, :], False, True)
                        if i == 2:
                            after(pe, "dwm", l, h + 1)
                            for q in range(NSEQ):
                                mm(B[6][:, h * P:(h + 1) * P], w(WQ_AT[h % 2] + q * P, P), DS[:, h, q, :], q == 0, q == NSEQ - 1)
                            ins = mm(o, DU[0:nt, h * nt:(h + 1) * nt], DVB[0:nt, h * P:(h + 1) * P], False, True,
                                     skip_group_check=True)
                            if h < NH - 1:
                                ins.then_inc(S("dvn_part"), 1)
                    ins.then_inc(S("dvn_mm"), 1)
                    after(pe, "dvn", l, i + 1)
                    after(pe, "dqd", l, i + 1)
                    for h in range(NH):
                        o = B[7][:, h * nt:(h + 1) * nt]
                        ins = mm(o, DY[0:nt, h * P:(h + 1) * P], cv3[0:nt, 8 + h, t0:t0 + nt], True, i == 0)
                        if i == 1:
                            ins = mm(o, DSP[:, h, :], cv3[:, h, t0:t0 + nt], False, True)
                        if i == 2:
                            ins = mm(o, DY[:, h * P:(h + 1) * P], ident[:, TS:], False, True)
                    ins.then_inc(S("do_mm"), 1)
                    if i < 2:
                        for h in range(NH):
                            ins = mm(B[3][:, h * P:(h + 1) * P], DKD[:, h * P:(h + 1) * P], DY[:, h * P:(h + 1) * P])
                        ins.then_inc(S("ds_mm"), 1)
                        after(pe, "gdn_state", l, i + 1)
                    after(pe, "do", l, i + 1)

                for first in (0, 2):
                    group = (0, 1) if first == 0 else (2,)
                    for i in group:
                        prepare(i)
                    invert(group)
                    for i in group:
                        finish(i)
                finish_heads(("heads", 2 * l + 2), w(4 * TL, TL))

                def sample_state(h):
                    after(pe, "dvm", l, h + 1)
                    if h >= 2:
                        after(pe, "gdn_sstate", l, h - 1)
                    vm = (D01, D34)[h % 2]
                    for c in range(2):
                        ins = mm(SBANK[h % 2][c][:, :], DSET[0][2][0:TS, h * P:(h + 1) * P], vm[0:TS, 512 * c:512 * c + 512])
                    ins.then_inc(S("dss_mm"), 1)

                for j in range(KD):
                    n = AT_OUT[l] + j // 2
                    if j % 2 == 0:
                        split_in(pe, n)
                    if j >= 2:
                        after(pe, "x_mix", l, j - 1)
                    wh, wl = (v3(x, KD) for x in parts(n))
                    c = slice((j % 2) * P, (j % 2 + 1) * P)
                    for k in range(KD):
                        if j == 0:
                            after(pe, "hl_out", l, k + 1)
                        ins = mm3(B[5 + j % 2][:, 0:T], wh[:, k, c], wl[:, k, c], hh[:, k, :], hl[:, k, :], k == 0, k == KD - 1)
                    ins.then_inc(S("out_mm"), 1)
                    if j in STATE_AT:
                        sample_state(STATE_AT.index(j))
                    if j >= 2:
                        sum_squares(2 * l + 2, SQ, j - 2)
                for j in (KD - 2, KD - 1):
                    sum_squares(2 * l + 2, SQ, j)
                if l == 0:
                    for u in range(FD):
                        n = AT_GU + u
                        split_in(pe, n)
                        if u >= 2:
                            pe.wait_ge(S("ff_act"), u - 1)
                        wh, wl = (v3(x, KD) for x in parts(n))
                        for b in range(2):
                            c = slice(b * P, (b + 1) * P)
                            for k in range(KD):
                                if (u, b) == (0, 0):
                                    pe.wait_ge(S("hl_ff"), k + 1)
                                ins = mm3(B[2 * b + u % 2][:, 0:T], wh[:, k, c], wl[:, k, c], hh[:, k, :], hl[:, k, :],
                                          k == 0, k == KD - 1)
                        ins.then_inc(S("gu_mm"), 1)
                    pe.wait_ge(S("ff_act"), FD)
                    for j in range(KD):
                        if j >= 2:
                            pe.wait_ge(S("x_ff"), j - 1)
                        for b in range(2):
                            n = AT_DN + 2 * j + b
                            split_in(pe, n)
                            wh, wl = (v3(x[:, 0:width(n)], FD // 2) for x in parts(n))
                            for k in range(FD // 2):
                                f = b * (FD // 2) + k
                                ins = mm3(B[4 + j % 2][:, 0:T], wh[:, k, :], wl[:, k, :], FAH[:, f, :], FAL[:, f, :],
                                          f == 0, f == FD - 1)
                            ins.then_inc(S("down_mm"), 1)
                        if j >= 2:
                            sum_squares(3, hT, j - 2)
                    for j in (KD - 2, KD - 1):
                        sum_squares(3, hT, j)

            pe.wait_ge(S("h_norm"), KD * 2 * DEPTH)
            for i, (t0, nt) in enumerate(TILES):
                for k in range(KD):
                    ins = mm(B[0][0:nt, NE * i:NE * (i + 1)], hT[:, k, t0:t0 + nt], wrt[:, k, :], k == 0, k == KD - 1)
            ins.then_inc(S("logits_mm"), 1)
            for i, (t0, nt) in enumerate(TILES):
                for c in range(2):
                    u = 2 * i + c
                    if u >= 2:
                        pe.wait_ge(S("htok"), u - 1)
                    for k in range(4):
                        ins = pe.transpose(B[2 + u % 2][0:nt, k * P:(k + 1) * P], hT[:, 4 * c + k, t0:t0 + nt], ident)
                    ins.then_inc(S("htok_tr"), 1)
            pe.wait_ge(S("sel"), 1)
            for i in range(3):
                for j in range(i + 1):
                    rows = TILES[j][1]
                    m = TILES[i][1]
                    lhsT = cst("strict", rows)[:, 0:m] if j == i else ones[0:rows, 0:m]
                    mm(B[1][0:m, NE * i:NE * (i + 1)], lhsT, sel[0:rows, NE * j:NE * (j + 1)], j == 0, j == i)
            for j in range(3):
                rows = TILES[j][1]
                ins = mm(B[1][:, 32:32 + NE], ones[0:rows, :], sel[0:rows, NE * j:NE * (j + 1)], j == 0, j == 2)
            ins.then_inc(S("pos_mm"), 1)
            pe.wait_ge(S("htok"), 6)

            def gather(g):
                pe.wait_ge(S("onehot"), g)
                for c in range(2):
                    bank = B[1 + 2 * c]
                    for k in range(4):
                        f = slice((4 * c + k) * P, (4 * c + k + 1) * P)
                        for i, (t0, nt) in enumerate(TILES):
                            mm(bank[:, k * P:(k + 1) * P], HTH[0:nt, i, f], ONEH[0:nt, i, :], i == 0, False)
                            ins = mm(bank[:, k * P:(k + 1) * P], HTL[0:nt, i, f], ONEH[0:nt, i, :], False, i == 2)
                    ins.then_inc(S("e_gather_mm"), 1)

            def scatter(el, j):
                if j == 0:
                    pe.wait_ge(S("e_y"), el + 1)
                    pe.wait_ge(S("e_wT"), el + 1)
                if j >= 2:
                    pe.wait_ge(S("e_scatter"), el * KD + j)
                mm(B[4 + j % 2][:, 0:T], YE[:, j * P:(j + 1) * P], ONEWT).then_inc(S("e_sc_mm"), 1)

            def expert(el, r):
                pe.wait_ge(S("e_in"), el * 2 + (2 * r + 2))

                def turn_act(c):
                    pe.wait_ge(S("e_act"), el * NCH + (c + 2))
                    if c == 0:
                        pe.wait_ge(S("e_scatter"), el * KD + (KD + 1))
                    for a in range(4):
                        ins = pe.transpose(B[4 + c % 2][:, a * P:(a + 1) * P], EA[:, c % 2, a * P:(a + 1) * P], ident)
                    ins.then_inc(S("e_tr"), 1)

                for j in range(PER_E):
                    kind, c = ORDER[j // 2]
                    b = j % 2
                    if b == 0 and kind == UP and c >= 1:
                        turn_act(c - 1)
                    if 2 <= j < 2 + KD // 2:
                        scatter(el, 2 * (j - 2))
                        scatter(el, 2 * (j - 2) + 1)
                    if b == 0 and (kind, c) == (DOWN, NCH - 2):
                        gather(el + (r + 2))
                        turn_act(NCH - 1)
                    if b == 0 and (kind, c) == (DOWN, NCH - 1):
                        pe.wait_ge(S("onew"), el + 1)
                        for i, (t0, nt) in enumerate(TILES):
                            ins = pe.transpose(B[2][:, t0:t0 + nt], ONEW[0:nt, i, :], ident[0:nt, 0:nt])
                        ins.then_inc(S("e_wT_mm"), 1)
                    n = AT_MOE + j
                    pe.wait_ge(S("w_low"), el * PER_E + (n + 1))
                    if kind == DOWN:
                        if b == 0:
                            pe.wait_ge(S("e_actT"), el * NCH + (c + 1))
                            if c == 0:
                                pe.wait_ge(S("e_y"), el + 1)
                        wh, wl = (v3(x, 2) for x in parts(n))
                        for a in range(2):
                            f = slice((2 * b + a) * P, (2 * b + a + 1) * P)
                            xh, xl = EATH[:, c % 2, f], EATL[:, c % 2, f]
                            for q in range(2):
                                o, m = B[6 + q][:, :], slice(512 * q, 512 * q + 512)
                                mm(o, xh, wh[:, a, m], c == 0 and b == 0 and a == 0, False)
                                mm(o, xh, wl[:, a, m], False, False)
                                ins = mm(o, xl, wh[:, a, m], False, c == NCH - 1 and b == 1 and a == 1)
                    else:
                        if b == 0:
                            pe.wait_ge(S("e_act"), el * NCH + (c if c >= 2 else 1))
                        o = B[2 * kind + c % 2][:, :]
                        wh, wl = (v3(x, 4) for x in parts(n))
                        for a in range(4):
                            k = 4 * b + a
                            mm(o, HGH[:, k, :], wh[:, a, :], k == 0, False)
                            mm(o, HGH[:, k, :], wl[:, a, :], False, False)
                            ins = mm(o, HGL[:, k, :], wh[:, a, :], False, k == KD - 1)
                    ins.then_inc(KINDS[kind], 1)

            def tail(el):
                for j in range(KD):
                    scatter(el, j)

            gather(1)
            with pe.Fori(0, NE) as e:
                expert(e, 0)
            more = pe.value_load(flag[0:1, 0:1], min_val=0, max_val=1)
            with pe.If(more > 0):
                with pe.Fori(1, MAXPASS) as r:
                    pe.wait_ge(S("e_in"), r * (2 * (NE + 1)))
                    gather(r * (NE + 1) + 1)
                    with pe.Fori(0, NE) as e:
                        expert(r * NE + e, r)
                tail(NE * MAXPASS)
            with pe.If(more < 1):
                tail(NE)
            for j in range(KD):
                sum_squares(5, SQ, j)

        @block.scalar
        def _(ac):
            own = Own(ac, "act_own")

            def act(out, in_, func, **k):
                return ac.activation(out, in_, func, **k)

            def rsqrt_seed(tag, x=None, y=None):
                x = rv[:, :] if x is None else x
                y = rs[:, :] if y is None else y
                act(warm[:, :], warm[:, :], ACT.Ln, bias=1.0)
                ac.wait_ge(S(f"var_{tag[0]}"), tag[1])
                own.do(act(y, x, ACT.Ln))
                act(y, y, ACT.Exp, scale=-0.5).then_inc(S(f"rs0_{tag[0]}"), 1)

            ac.wait_ge(S("const_in"), 64)
            own.do(act(warm[:, :], small[:, 0:1], ACT.Square))
            act(csT[:, :], col("c"), ACT.Silu).then_inc(S("cs_e"), 1)
            for n in range(2):
                split_high(ac, n)
            with ac.Fori(0, H_ADA // TURN) as turn:
                for s in range(TURN // 2):
                    for n in (2 * s + 2, 2 * s + 3):
                        j = n % TURN
                        ac.wait_ge(landed[n % SLOTS], turn * (16 * TURN // SLOTS) + 16 * (n // SLOTS + 1))
                        back = (2, 2, 5)[j] if j < PARTS else PARTS
                        ac.wait_ge(S("ada_mm"), turn * TURN + (PARTS + n - back + 1))
                        act(whi[:, j % PARTS, :], raw[:, n % SLOTS, :], ACT.Copy).then_inc(S("w_high"), 1)
                    ac.wait_ge(S("ada_mm"), turn * TURN + (PARTS + 2 * s + 2))
                    act(AROW[0:2 * NC_, s % 2, :], B[s % 2][0:2 * NC_, :], ACT.Copy).then_inc(S("ada_rows"), 1)
            high = Split(ac, split_high, H_ADA + 2)

            def squares(sq, j, ready, v):
                ac.wait_ge(S(ready), v)
                act(sq[:, j, :], xT[:, j, :], ACT.Square).then_inc(S("sq_norm"), 1)

            def norm(t, shift, parts):
                rsqrt_seed(("norm", t))
                ac.wait_ge(S("hs_norm"), t)
                if parts:
                    act(hh[:, :, TP:], hT[:, :, TP:], ACT.Copy)
                for k in range(KD):
                    ac.wait_ge(S("hx_norm"), KD * (t - 1) + (k + 1))
                    b = md(shift)[:, k, 0:1]
                    if parts:
                        act(hh[:, k, 0:TP], hT[:, k, 0:TP], ACT.Identity, bias=b).then_inc(S("hh"), 1)
                    act(hT[:, k, 0:TP], hT[:, k, 0:TP], ACT.Identity, bias=b).then_inc(S("h_norm"), 1)

            for j in range(KD):
                squares(hT, j, "x_in", 16)
            for l in range(DEPTH):
                high.to(AT_IN[l] + 2)
                norm(2 * l + 1, 48 * l, True)
                dest = [None] * CT + [qk3[:, j, :] for j in range(4)] + [v13[:, j, :] for j in range(4)]\
                    + [g13[:, j, :] for j in range(4)] + [zt3[:, j, :] for j in range(4)]

                wc = v3(col(f"wconv{l}"), CT)
                after(ac, "proj_mm", l, 1)
                act(LRT, B[0][0:AR, 0:T], ACT.Copy).then_inc(S("proj"), 1)
                def exponentials(i):
                    (t0, nt), (GEA, GE, GKT, GKE, GQD) = TILES[i], GSET[i % 2]
                    la = LA[:, :, t0:t0 + nt]
                    after(ac, "gla_arg", l, i + 1)
                    if i < 2:
                        act(GEA, GEA, ACT.Exp)
                        act(GKT[:, :, 0:nt], GKT[:, :, 0:nt], ACT.Exp)
                    else:
                        act(GKT[:, :, 0:nt], la, ACT.Exp, scale=-1.0)
                    act(GKE[:, :, 0:nt], GKE[:, :, 0:nt], ACT.Exp)
                    act(GQD[:, :, 0:nt], la, ACT.Exp).then_inc(S("gla_exp"), 1)

                for u in range(UNITS - 1):
                    bank = B[(u + 1) % 2]
                    after(ac, "proj_mm", l, u + 2)
                    if u < CT:
                        if u >= 4:
                            after(ac, "cv_raw", l, u - 3)
                        if u == 0:
                            after(ac, "xp_ready", l, 1)
                        act(cv3[:, u, :], bank[:, 0:T], ACT.Copy, scale=wc[:, u, CW - 1:CW])
                        act(XP[:, u % 4, CW - 1:], bank[:, 0:TP], ACT.Copy)
                        act(XS[:, u % 4, :, CW - 1:], v3(bank[:, TP:T], NSEQ), ACT.Copy).then_inc(S("proj"), 1)
                    else:
                        act(dest[u], bank[:, 0:T], ACT.Silu if u >= 20 else ACT.Copy).then_inc(S("proj"), 1)
                    if u % 2 == 0:
                        high.to(AT_IN[l] + u // 2 + PARTS)
                    if 1 <= u <= CT:
                        after(ac, "cv_raw", l, u)
                        act(cv3[:, u - 1, :], cv3[:, u - 1, :], ACT.Silu).then_inc(S("cv_e"), 1)
                    if u == 3:
                        after(ac, "gx", l, 1)
                        own.do(act(gL[:, :], gX[:, :], ACT.Abs))
                        own.do(act(gL[:, :], gL[:, :], ACT.Exp, scale=-1.0))
                        act(gL[:, :], gL[:, :], ACT.Ln, bias=1.0)
                        act(gEA[:, :], col(f"alog{l}"), ACT.Exp)
                        act(v3(gEB[:, :], 3), v3(gAB[:, :], 3)[:, :, NH:2 * NH], ACT.Exp, scale=-1.0).then_inc(S("gact"), 1)
                    if u == 7:
                        after(ac, "zb", l, 1)
                        own.do(act(LAE, w(R, 2 * T), ACT.Abs))
                        own.do(act(LAE, LAE, ACT.Exp, scale=-1.0))
                        act(LAE, LAE, ACT.Ln, bias=1.0).then_inc(S("zl"), 1)
                    if u == 11:
                        after(ac, "gamc", l, 1)
                        act(gEG[:, :], gGC[:, :], ACT.Exp)
                        act(gDK[:, :], gD[:, :], ACT.Exp).then_inc(S("gexp"), 1)
                    if u == 17:
                        exponentials(0)

                for i, (t0, nt) in enumerate(TILES):
                    after(ac, "gla_tr", l, i + 1)
                    act(GVT[0:nt, :], B[2][0:nt, :], ACT.Copy).then_inc(S("gla_tok"), 1)
                    after(ac, "gla_ktr", l, i + 1)
                    act(GKDT[0:nt, :], B[3][0:nt, 0:256], ACT.Copy).then_inc(S("gla_tok"), 1)
                    if i < 2:
                        exponentials(i + 1)
                    after(ac, "gla_o_mm", l, i + 1)
                    if i < 2:
                        act(hT[:, 0:GH:2, t0:t0 + nt], v3(GOB[0][:, 0:2 * nt], 2), ACT.Copy)
                        act(hT[:, 1:GH:2, t0:t0 + nt], v3(GOB[1][:, 0:2 * nt], 2), ACT.Copy).then_inc(S("gla_o"), 1)
                    else:
                        act(hT[:, 0:GH, t0:t0 + nt], v3(B[5][:, 0:GH * nt], 4), ACT.Copy).then_inc(S("gla_o"), 1)
                rsqrt_seed(("heads", 2 * l + 1))

                after(ac, "gla_out", l, 48)
                after(ac, "gla_fin", l, 1)
                def prepare(i):
                    (t0, nt), (DVB, DKB, DKD, DM, DMB, DT, DU, DY, DX) = TILES[i], DSET[i % 2]
                    n4 = 4 * nt
                    for b, dst in ((0, DM), (1, DMB)):
                        after(ac, "dtr", l, 3 * i + b + 1)
                        if i == 2 and b == 0:
                            after(ac, "gdn_state", l, i)
                        act(dst[0:nt, :], B[b][0:nt, :], ACT.Square).then_inc(S("dsq"), 1)
                    rsqrt_seed(("qk", 3 * l + i + 1), rv8[0:nt, :], rs8[0:nt, :])
                    after(ac, "dlog", l, i + 1)
                    own.go(act(DX[0:nt, 0:n4], DX[0:nt, 0:n4], ACT.Exp))
                    act(DY[0:nt, 0:n4], DY[0:nt, 0:n4], ACT.Exp).then_inc(S("dmask"), 1)
                    for b, r0 in ((4, 0), (5, 4)):
                        after(ac, "dtb", l, 2 * i + b - 3)
                        act(cv3[:, r0:r0 + 4, t0:t0 + nt], v3(B[b][:, 0:n4], 4), ACT.Copy).then_inc(S("dqkT"), 1)
                    after(ac, "dat", l, i + 1)
                    act(DX[:, 0:n4], B[3][:, 0:n4], ACT.Exp).then_inc(S("drowe"), 1)

                def invert(group):
                    for v in levels_of(group[0])[1:]:
                        for i in group:
                            nt, DY = TILES[i][1], DSET[i % 2][7]
                            for hs in range(2):
                                after(ac, "dy_mm", l, at_level(i, v, hs))
                                act(DY[0:nt, 2 * hs * nt:(2 * hs + 2) * nt], YBANK[i % 2][hs][0:nt, 0:2 * nt],
                                    ACT.Copy).then_inc(S("dy"), 1)

                def finish(i):
                    (t0, nt), (DVB, DKB, DKD, DM, DMB, DT, DU, DY, DX) = TILES[i], DSET[i % 2]
                    n4 = 4 * nt
                    after(ac, "dw_mm", l, i + 1)
                    act(DMB[:, 0:n4], B[5][:, 0:n4], ACT.Copy, scale=-1.0).then_inc(S("dw"), 1)
                    after(ac, "dvn_mm", l, i + 1)
                    act(DY, B[6][:, :], ACT.Copy).then_inc(S("dvn"), 1)
                    after(ac, "do_mm", l, i + 1)
                    act(hT[:, GH:, t0:t0 + nt], v3(B[7][:, 0:n4], 4), ACT.Copy).then_inc(S("do"), 1)

                for first in (0, 2):
                    group = (0, 1) if first == 0 else (2,)
                    for i in group:
                        prepare(i)
                    invert(group)
                    high.to(AT_OUT[l] + 2)
                    for i in group:
                        finish(i)
                for k in range(GH):
                    act(hh[:, k, :], hT[:, k, :], ACT.Copy).then_inc(S("hh"), 1)
                rsqrt_seed(("heads", 2 * l + 2))
                for h in range(NH):
                    after(ac, "gdn_fin", l, h + 1)
                    act(hh[:, GH + h, :], hT[:, GH + h, :], ACT.Copy).then_inc(S("hh"), 1)
                for j in range(KD):
                    if j % 2:
                        high.to(AT_OUT[l] + j // 2 + PARTS)
                    squares(SQ, j, "x_mix", KD * l + (j + 1))
                norm(2 * l + 2, 48 * l + 24, l == 0)
                if l == 0:
                    for u in range(FD):
                        ac.wait_ge(S("gu_mm"), u + 1)
                        if u >= 2:
                            ac.wait_ge(S("ff_act"), u - 1)
                        act(FSG[u % 2], B[u % 2][:, 0:T], ACT.Silu).then_inc(S("ff_silu"), 1)
                        high.to(AT_GU + u + PARTS)
                    for j in range(KD):
                        high.to(AT_DN + 2 * j + 1 + PARTS)
                        squares(hT, j, "x_ff", j + 1)

            ac.wait_ge(S("lg_shift"), 1)
            act(lgE[:, :], lgE[:, :], ACT.Exp).then_inc(S("lg_exp"), 1)
            for u in range(6):
                i, c = u // 2, u % 2
                nt = TILES[i][1]
                ac.wait_ge(S("htok_tr"), u + 1)
                act(HTH[0:nt, i, 512 * c:512 * c + 512], B[2 + c][0:nt, :], ACT.Copy).then_inc(S("htok_high"), 1)

            def gathered(g):
                for c in range(2):
                    ac.wait_ge(S("e_gather_mm"), g + (c - 1))
                    act(HGH[:, 4 * c:4 * c + 4, :], v3(B[1 + 2 * c][:, :], 4), ACT.Copy).then_inc(S("hg_high"), 1)

            def result_weights(el):
                ac.wait_ge(S("e_wT_mm"), el + 1)
                act(ONEWT, B[2][:, 0:T], ACT.Copy).then_inc(S("e_wT"), 1)

            def result(el):
                ac.wait_ge(S("e_down_mm"), el * (2 * NCH) + PARTS)
                ac.wait_ge(S("e_sc_mm"), el * KD + 1)
                act(YE[:, 0:512], B[6][:, :], ACT.Copy)
                act(YE[:, 512:], B[7][:, :], ACT.Copy).then_inc(S("e_y"), 1)

            def expert(el, r):
                def turned(c):
                    ac.wait_ge(S("e_tr"), el * NCH + (c + 2))
                    act(EATH[:, c % 2, :], B[4 + c % 2][:, :], ACT.Copy).then_inc(S("e_turn_high"), 1)

                for j in range(PARTS):
                    if j == PARTS - 1:
                        result_weights(el)
                    e_split_high(ac, el, j)
                result(el)
                for j in range(PER_E - 2):
                    kind, c = ORDER[j // 2]
                    if kind == GATE and j % 2:
                        ac.wait_ge(S("e_gate_mm"), el * (2 * NCH) + (2 * c + 2))
                        ac.wait_ge(S("e_tr"), el * NCH + (c if c else 1))
                        act(EA[:, c % 2, :], B[c % 2][:, :], ACT.Silu).then_inc(S("e_silu"), 1)
                        if c:
                            turned(c - 1)
                    if j == PER_E - 4:
                        gathered(el * 2 + (2 * r + 4))
                        turned(NCH - 1)
                    if j + PARTS < PER_E:
                        e_split_high(ac, el, j + PARTS)

            gathered(2)
            with ac.Fori(0, NE) as e:
                expert(e, 0)
            more = ac.value_load(flag[0:1, 0:1], min_val=0, max_val=1)
            with ac.If(more > 0):
                with ac.Fori(1, MAXPASS) as r:
                    gathered(r * (2 * (NE + 1)) + 2)
                    with ac.Fori(0, NE) as e:
                        expert(r * NE + e, r)
                result_weights(NE * MAXPASS)
                result(NE * MAXPASS)
            with ac.If(more < 1):
                result_weights(NE)
                result(NE)
            for j in range(KD):
                squares(SQ, j, "x_moe", j + 1)
            norm(5, 96, False)

        @block.vector
        def _(ve):
            own = Own(ve, "vec_own")
            do, go = own.do, own.go
            tt, ts, stt, cp = ve.tensor_tensor, ve.tensor_scalar, ve.scalar_tensor_tensor, ve.tensor_copy

            def refine(tag, y, v, t):
                ve.wait_ge(S(f"rs0_{tag[0]}"), tag[1])
                do(tt(t, y, y, ALU.mult))
                do(stt(t, t, -0.5, v, ALU.mult, ALU.mult))
                do(stt(y, t, 1.5, y, ALU.add, ALU.mult))

            def norm(t, shift, scale, ahead=None):
                ve.wait_ge(S("ss_norm"), t)
                do(ts(rv[:, :], B[0][:, 0:T], 1.0 / D, EPS, ALU.mult, ALU.add), "var_norm")
                refine(("norm", t), rs[:, :], rv[:, :], rt[:, :])
                A_, B_ = md(scale), md(shift)
                hs, xs = (v[:, :, TP:].rearrange("p k (s u) -> p k s u", s=NSEQ) for v in (hT, xT))
                do(tt(hT[:, :, TP:], xT[:, :, TP:], mid(rs[:, TP:], KD), ALU.mult))
                do(tt(hs, hs, last(A_[:, :, 1:], LSEQ), ALU.mult))
                go(tt(hs, hs, last(B_[:, :, 1:], LSEQ), ALU.add), "hs_norm")
                for k in range(KD):
                    go(stt(hT[:, k, 0:TP], xT[:, k, 0:TP], A_[:, k, 0:1], rs[:, 0:TP], ALU.mult, ALU.mult), "hx_norm")
                if ahead is not None:
                    low.to(ahead)

            def low_parts(phase, name, tiles=range(KD)):
                for k in tiles:
                    ve.wait_ge(S("hh"), KD * phase + (k + 1))
                    go(tt(hl[:, k, :], hT[:, k, :], hh[:, k, :], ALU.subtract), name)

            def finish_heads(tag, h0, gate, weight, done, sq, each, meanwhile=None):
                o = hT[:, h0:h0 + 4, :]
                do(tt(v3(sq, 4), o, o, ALU.mult), f"sq_{tag[0]}")
                if meanwhile:
                    meanwhile()
                ve.wait_ge(S(f"ss_{tag[0]}"), tag[1])
                do(ts(rv[:, :], B[0][:, 0:T], 1.0 / GV, EPS, ALU.mult, ALU.add), f"var_{tag[0]}")
                refine(tag, rs[:, :], rv[:, :], rt[:, :])
                go(cp(rt[:, 0:1], rs[:, 0:1]), f"rs_{tag[0]}")
                do(stt(o, v3(gate, 4), weight, o, ALU.mult, ALU.mult))
                ve.wait_ge(S(f"rsb_{tag[0]}"), tag[1])
                for h in range(4):
                    go(tt(o[:, h, :], o[:, h, :], B[1 + h][:, 0:T], ALU.mult), done if each or h == 3 else None)

            def residual(bank, j, gt, name):
                do(stt(xT[:, j, 0:TP], bank[:, 0:TP], md(gt)[:, j, 0:1], xT[:, j, 0:TP], ALU.mult, ALU.add))
                xs = v3(xT[:, j, TP:], NSEQ)
                do(tt(v3(rt[:, 0:TS], NSEQ), v3(bank[:, TP:T], NSEQ), last(md(gt)[:, j, 1:], LSEQ), ALU.mult))
                do(tt(xs, xs, v3(rt[:, 0:TS], NSEQ), ALU.add), name)

            for name in ("ada_done", "e_act", "e_scatter"):
                ve.sem_inc(S(name), 1)
            ve.memset(gAB[:, :], 0.0)
            ve.wait_ge(S("const_in"), 64)
            ve.tensor_copy(cb[:, :], W[:, KD * P:KD * P + N_CB])
            ve.memset(gGC[:, :], 0.0)
            ve.memset(lgE[:, :], 0.0)
            go(ve.memset(gGL[:, :], 0.0))
            do(ve.memset(cs_r[:, :].bitcast(F32), 0.0))
            ve.wait_ge(S("cs_e"), 1)
            cs3 = v3(csT, KD)
            do(cp(CSP[:, :, 0:NC_], cs3))
            do(tt(CSP[:, :, NC_:2 * NC_], cs3, CSP[:, :, 0:NC_], ALU.subtract), "cs")
            bada = col("b_ada")
            for n in range(2):
                split_low(ve, n)
            with ve.Fori(0, H_ADA // TURN) as turn:
                for s in range(TURN // 2):
                    for n in (2 * s + 2, 2 * s + 3):
                        p = (n % TURN) % PARTS
                        ve.wait_ge(S("w_high"), turn * TURN + (n + 1))
                        tt(wlo[:, p, :], raw[:, n % SLOTS, :], whi[:, p, :], ALU.subtract).then_inc(S("w_low"), 1)
                    ve.wait_ge(S("ada_turned"), turn * (TURN // 2) + (s + 1))
                    tile = (turn * (TURN // 2) + s) * 4
                    tt(mod[:, bass.ds(tile, 4), :], v3(B[2 + s % 2][:, 0:4 * NC_], 4),
                       last(bada[:, bass.ds(tile, 4)], NC_), ALU.add).then_inc(S("ada_done"), 1)
            low = Split(ve, split_low, H_ADA + 2)
            ve.wait_ge(S("ada_done"), N_ADA + 1)
            for name, t in (("nm0", 8), ("nf0", 32), ("nm1", 56), ("nf1", 80), ("nfin", 104)):
                go(stt(md(t), md(t), 1.0, last(col(name), NC_), ALU.add, ALU.mult))
            ve.wait_ge(S("x_in"), 16)
            ve.wait_ge(S("vec_own"), own.n["vec_own"])

            for l in range(DEPTH):
                m0 = 48 * l
                norm(2 * l + 1, m0, m0 + 8, AT_IN[l] + 2)
                for k in range(KD):
                    ve.wait_ge(S("h_norm"), KD * 2 * l + (k + 1))
                    low_parts(3 * l, "hl_in", (k,))
                do(ve.memset(XP[:, :, 0:CW - 1], 0.0), "xp_ready")
                after(ve, "conv_in", l, 16)
                wc = v3(col(f"wconv{l}"), CT)

                for c in range(CT):
                    s = c % 4
                    after(ve, "proj", l, c + 2)
                    do(cp(XS[:, s, :, 0:CW - 1], SC[:, c, :, :]))
                    xs, ys, yp = XS[:, s, :, :], v3(cv3[:, c, TP:], NSEQ), cv3[:, c, 0:TP]
                    for j in range(CW - 1):
                        go(stt(yp, XP[:, s, j:j + TP], wc[:, c, j:j + 1], yp, ALU.mult, ALU.add))
                        do(stt(ys, xs[:, :, j:j + LSEQ], wc[:, c, j:j + 1], ys, ALU.mult, ALU.add))
                    go(cp(OC[:, c, 0, :], XP[:, s, TP:TP + 3]))
                    do(cp(OC[:, c, 1:, :], xs[:, :, LSEQ:LSEQ + 3]), "cv_raw")
                    if c % 2 == 0:
                        low.to(AT_IN[l] + c // 2 + PARTS)
                    if c == 1:
                        after(ve, "small_mm", l, 1)
                        go(cp(v3(gAB[:, 0:16], 2), v3(B[3][:, 0:2 * AR], 2)[:, :, AB:]))
                        do(cp(gAB[0:TS, 16:24], B[3][0:TS, 2 * AR + AB:3 * AR]))
                        ab = v3(gAB[:, :], 3)
                        do(tt(v3(gX[:, :], 3), ab[:, :, 0:NH], mid(col(f"dtb{l}"), 3), ALU.add), "gx")
                    if c == 3:
                        after(ve, "gact", l, 1)
                        do(stt(gX[:, :], gX[:, :], 0.0, gL[:, :], ALU.max, ALU.add))
                        do(stt(v3(gG[:, :], 3), v3(gX[:, :], 3), -1.0, mid(gEA[:, :], 3), ALU.mult, ALU.mult), "g")
                        do(ts(gBE[:, :], gEB[:, :], 1.0, None, ALU.add))
                        do(ve.reciprocal(gBE[:, :], gBE[:, :]))
                    if c == 4:
                        after(ve, "z_mm", l, 2)
                        go(ts(LA[:, 0, :], B[4][:, 0:T], col(f"bg{l}")[:, 0:1], None, ALU.add))
                        do(ts(LA[:, 1, :], B[5][:, 0:T], col(f"bg{l}")[:, 1:2], None, ALU.add), "zb")
                    if c == 8:
                        after(ve, "zl", l, 1)
                        la = w(R, 2 * T)
                        do(stt(la, la, 0.0, LAE, ALU.min, ALU.subtract))
                        do(ts(la, la, 1.0 / GATE_NORM, None, ALU.mult))
                        for p in range(2):
                            go(ve.tensor_tensor_scan(LAE[:, p * T:(p + 1) * T], cbf("reset"), LA[:, p, :], 0.0, ALU.mult, ALU.add))
                        ve.wait_ge(S("vec_own"), own.n["vec_own"])
                        do(cp(la, LAE), "la")
                    if c == 9:
                        after(ve, "gam_mm", l, 1)
                        for i, (t0, nt) in enumerate(TILES):
                            go(cp(gGC[0:nt, 4 * i:4 * i + 4], B[6][0:nt, 4 * i:4 * i + 4]))
                            do(cp(gGL[0:nt, 4 * i:4 * i + 4], B[6][0:nt, 16 + 4 * i:20 + 4 * i]))
                        do(tt(gD[:, :], gGL[:, :], gGC[:, :], ALU.subtract), "gamc")
                    if c == 11:
                        after(ve, "gexp", l, 1)
                        do(tt(gBG[:, :], gBE[:, :], gEG[:, :], ALU.mult), "gcols")
                go(cp(rt[:, 0:1], rs[:, 0:1]), "conv_done")
                def arguments(i):
                    (t0, nt), (GEA, GE, GKT, GKE, GQD) = TILES[i], GSET[i % 2]
                    la = LA[:, :, t0:t0 + nt]
                    if i == 2:
                        after(ve, "gla_o_mm", l, 1)
                        after(ve, "gla_s_mm", l, 1)
                    if i < 2:
                        for j, nj in enumerate(NJ):
                            mid_j = LA[:, :, t0 + SUB * j + SUB // 2 - 1]
                            go(tt(GE[j], LA[:, :, t0 + SUB * j:t0 + nt], last(mid_j, nj), ALU.subtract))
                            go(tt(GKT[:, :, SUB * j:SUB * j + SUB], last(mid_j, SUB),
                                  LA[:, :, t0 + SUB * j:t0 + SUB * j + SUB], ALU.subtract))
                        do(tt(GKE, last(LA[:, :, t0 + nt - 1], nt), la, ALU.subtract), "gla_arg")
                    else:
                        for p in range(2):
                            seq = v3(LA[:, p, t0:t0 + nt], NSEQ)
                            ins = tt(v3(GKE[:, p, 0:nt], NSEQ), last(seq[:, :, LSEQ - 1], LSEQ), seq, ALU.subtract)
                            go(ins) if p == 0 else do(ins, "gla_arg")

                def operands(i):
                    (t0, nt), (GEA, GE, GKT, GKE, GQD) = TILES[i], GSET[i % 2]
                    q, k = qk3[:, 0:2, t0:t0 + nt], qk3[:, 2:4, t0:t0 + nt]
                    after(ve, "gla_exp", l, i + 1)
                    if i < 2:
                        go(cp(gEB_[:, 0:2], GQD[:, :, P - 1]))
                        for j, nj in enumerate(NJ):
                            go(stt(GE[j], GE[j], GK ** -0.5, qk3[:, 0:2, t0 + SUB * j:t0 + nt], ALU.mult, ALU.mult))
                    else:
                        go(cp(v3(gEB_[:, :], 2), GQD[:, :, LSEQ - 1:TS:LSEQ]))
                    ve.wait_ge(S("vec_own"), own.n["vec_own"])
                    go(tt(GKT[:, :, 0:nt], GKT[:, :, 0:nt], k, ALU.mult))
                    go(tt(GKE[:, :, 0:nt], GKE[:, :, 0:nt], k, ALU.mult))
                    do(stt(GQD[:, :, 0:nt], GQD[:, :, 0:nt], GK ** -0.5, q, ALU.mult, ALU.mult), "gla_ops" if i < 2 else None)
                    if i == 2:
                        do(ve.memset(GQ2, 0.0))
                        go(cp(GQ2[0:64, :, 0:TS], GQD[0:64, :, 0:TS]))
                        go(cp(GQ2[64:, :, TS:], GQD[64:, :, 0:TS]), "gla_ops")

                def scores_and_state(i):
                    t0, nt = TILES[i]
                    after(ve, "gla_at_mm", l, i + 1)
                    if i == 0:
                        do(ve.memset(GAT, 0.0))
                    if i < 2:
                        for j, nj in enumerate(NJ):
                            r0 = SUB * j
                            for e in range(2):
                                ins = tt(v3(GAT, 4)[r0:r0 + SUB, e::2, r0:], v3(GAB[e][:, 0:256], 2)[r0:r0 + SUB, :, r0:],
                                         mid(cst("tri")[r0:r0 + SUB, r0:], 2), ALU.mult)
                                go(ins) if (j, e) != (len(NJ) - 1, 1) else do(ins, "gla_at")
                    else:
                        do(ve.memset(GAT[TS:, 0:4 * TS], 0.0))
                        for e in range(2):
                            ins = tt(v3(GAT[0:TS, 0:4 * TS], 4)[:, e::2, :], v3(GAB[e][0:TS, 0:2 * TS], 2),
                                     mid(cst("tri_s", TS), 2), ALU.mult)
                            go(ins) if e == 0 else do(ins, "gla_at")
                    if i == 0:
                        after(ve, "gla_s_mm", l, 1)
                        do(cp(GS, v3(B[6][:, 0:256], 2)), "gla_state")
                    elif i == 1:
                        after(ve, "gla_s_mm", l, 2)
                        go(stt(GS[:, 0, :], GS[:, 0, :], gEB_[:, 0:1], B[6][:, 0:P], ALU.mult, ALU.add))
                        do(stt(GS[:, 1, :], GS[:, 1, :], gEB_[:, 1:2], B[6][:, P:2 * P], ALU.mult, ALU.add), "gla_state")
                    else:
                        eb = v3(gEB_[:, :], 2)
                        after(ve, "gla_tok", l, 6)
                        for h in range(GH):
                            if h:
                                after(ve, "gla_ss_mm", l, h)
                            if h == 2:
                                for c in range(2):
                                    ins = tt(GSS[0][:, 4 * c:4 * c + 4, :], GSS[0][:, 4 * c:4 * c + 4, :], v3(B[6 + c][:, :], 4), ALU.add)
                                    go(ins) if c == 0 else do(ins, "gla_sstate")
                            do(tt(GVM[0:TS, :, :], mid(GVT[0:TS, h * P:(h + 1) * P], NSEQ), last(cst("seq", TS), GV), ALU.mult), "gla_vm")
                            if h == 0:
                                after(ve, "gla_o_mm", l, 3)
                                for p in range(2):
                                    do(tt(GSS[p], GSS[p], last(eb[:, p, :], GV), ALU.mult))
                        after(ve, "gla_ss_mm", l, GH)
                        for c in range(2):
                            ins = tt(GSS[1][:, 4 * c:4 * c + 4, :], GSS[1][:, 4 * c:4 * c + 4, :], v3(B[6 + c][:, :], 4), ALU.add)
                            go(ins) if c == 0 else do(ins, "gla_sstate")

                low.to(AT_IN[l] + 10)
                after(ve, "conv_out", l, 16)
                after(ve, "proj", l, 17)
                arguments(0)
                low.to(AT_IN[l] + 12)
                operands(0)
                low.to(AT_OUT[l] - 1)
                after(ve, "proj", l, UNITS)
                for step, i in ((arguments, 1), (scores_and_state, 0), (operands, 1), (arguments, 2), (scores_and_state, 1),
                                (operands, 2), (scores_and_state, 2)):
                    step(i)
                after(ve, "gla_o", l, 3)
                finish_heads(("heads", 2 * l + 1), 0, G1, col(f"glan{l}"), "gla_fin", QK, False)

                after(ve, "gla_out", l, 48)
                def masked(i, v, hs):
                    nt, (DM, DMB) = TILES[i][1], DSET[i % 2][3:5]
                    if v:
                        after(ve, "dy_mm", l, at_level(i, v - 1, hs))
                    c = slice(2 * hs * nt, (2 * hs + 2) * nt)
                    lev = v3(cbf("level", nt), 7)
                    do(tt(v3(DMB[0:nt, c], 2), v3(DM[0:nt, c], 2), mid(lev[:, v, 0:nt], 2), ALU.mult), "dmb")

                def prepare(i):
                    (t0, nt), (DVB, DKB, DKD, DM, DMB, DT, DU, DY, DX) = TILES[i], DSET[i % 2]
                    n4 = 4 * nt
                    gc = gGC[0:nt, 4 * i:4 * i + 4]
                    after(ve, "dsq", l, 2 * i + 2)
                    go(ve.tensor_reduce(rv8[0:nt, 0:4], v3(DM[0:nt, :], 4), AX.X, ALU.add))
                    do(ve.tensor_reduce(rv8[0:nt, 4:8], v3(DMB[0:nt, :], 4), AX.X, ALU.add))
                    do(ts(rv8[0:nt, :], rv8[0:nt, :], EPS, None, ALU.add), "var_qk")
                    after(ve, "drow", l, i + 1)
                    nu, nl = (cbf("neg_u"), cbf("neg_l")) if i < 2 else (cbf("neg_us", TS), cbf("neg_ls", TS))
                    dx, dy = v3(DX[0:nt, 0:n4], 4), v3(DY[0:nt, 0:n4], 4)
                    do(tt(dy, v3(B[3][0:nt, 0:n4], 4), last(gc, nt), ALU.subtract))
                    do(tt(dx, dy, mid(nu, 4), ALU.add))
                    do(tt(dy, mid(nl, 4), dy, ALU.subtract), "dlog")
                    refine(("qk", 3 * l + i + 1), rs8[0:nt, :], rv8[0:nt, :], rt8[0:nt, :])
                    do(ts(rs8[0:nt, 0:4], rs8[0:nt, 0:4], NK ** -0.5, None, ALU.mult))
                    do(tt(v3(DT[0:nt, :], 4), v3(B[0][0:nt, :], 4), last(rs8[0:nt, 0:4], NK), ALU.mult), "dqk")
                    do(tt(v3(DU[0:nt, :], 4), v3(B[1][0:nt, :], 4), last(rs8[0:nt, 4:8], NK), ALU.mult), "dqk")
                    kn = v3(DU[0:nt, :], 4)
                    go(tt(v3(DKD[0:nt, :], 4), kn, last(gDK[0:nt, 4 * i:4 * i + 4], NK), ALU.mult))
                    go(tt(v3(DKB[0:nt, :], 4), kn, last(gBG[0:nt, 4 * i:4 * i + 4], NK), ALU.mult))
                    after(ve, "dtr", l, 3 * i + 3)
                    go(tt(v3(DVB[0:nt, :], 4), v3(B[2][0:nt, :], 4), last(gBE[0:nt, 4 * i:4 * i + 4], NK), ALU.mult))
                    after(ve, "dmask", l, i + 1)
                    after(ve, "dkk", l, 2 * i + 1)
                    do(tt(DM[0:nt, 0:n4], B[6][0:nt, 0:n4], DY[0:nt, 0:n4], ALU.mult))
                    m3 = v3(DM[0:nt, 0:n4], 4)
                    do(tt(m3, m3, last(gBE[0:nt, 4 * i:4 * i + 4], nt), ALU.mult))
                    after(ve, "dkk", l, 2 * i + 2)
                    do(tt(cv3[0:nt, 8:12, t0:t0 + nt], v3(B[7][0:nt, 0:n4], 4), dx, ALU.mult), "dat")
                    after(ve, "dtb", l, 2 * i + 2)
                    for hs in range(2):
                        masked(i, 0, hs)
                        c = slice(2 * hs * nt, (2 * hs + 2) * nt)
                        go(tt(v3(DT[0:nt, c], 2), mid(ident[0:nt, 0:nt], 2), v3(DMB[0:nt, c], 2), ALU.subtract))
                    after(ve, "drowe", l, i + 1)
                    qd = cv3[:, 0:4, t0:t0 + nt]
                    go(tt(qd, qd, v3(DX[:, 0:n4], 4), ALU.mult), "dqd")
                    if i < 2:
                        do(cp(gEL[:, 4 * i:4 * i + 4], v3(DX[:, :], 4)[:, :, P - 1]))
                    else:
                        do(cp(v3(gEL[:, :], 4), v3(DX[:, 0:n4], 4)[:, :, LSEQ - 1:TS:LSEQ]))

                def invert(group):
                    nlev = len(levels_of(group[0]))
                    for v in range(nlev):
                        for i in group:
                            nt, (DT, DU) = TILES[i][1], DSET[i % 2][5:7]
                            for hs in range(2):
                                if v + 1 < nlev:
                                    masked(i, v + 1, hs)
                                c = slice(2 * hs * nt, (2 * hs + 2) * nt)
                                if v == 0:
                                    after(ve, "dy_mm", l, at_level(i, v, hs))
                                    do(tt(v3(DU[0:nt, c], 2), mid(ident[0:nt, 0:nt], 2),
                                          v3(YBANK[i % 2][hs][0:nt, 0:2 * nt], 2), ALU.subtract), "dtu")
                                    continue
                                after(ve, "dtu_mm", l, at_update(i, v, hs))
                                b = TBANK[i % 2][hs]
                                if v < nlev - 1:
                                    go(tt(DT[0:nt, c], DT[0:nt, c], b[0:nt, 256:256 + 2 * nt], ALU.subtract))
                                do(tt(DU[0:nt, c], DU[0:nt, c], b[0:nt, 0:2 * nt], ALU.subtract), "dtu")

                def finish(i):
                    (t0, nt), (DVB, DKB, DKD, DM, DMB, DT, DU, DY, DX) = TILES[i], DSET[i % 2]
                    n4 = 4 * nt
                    if i == 0:
                        after(ve, "ds_mm", l, 1)
                        do(cp(DSP, v3(B[3][:, :], 4)), "gdn_state")
                    elif i == 1:
                        after(ve, "ds_mm", l, 2)
                        for h in range(NH):
                            ins = stt(DSP[:, h, :], DSP[:, h, :], gEL[:, 4 + h:5 + h], B[3][:, h * P:(h + 1) * P], ALU.mult, ALU.add)
                            go(ins) if h < NH - 1 else do(ins, "gdn_state")
                    else:
                        after(ve, "dw", l, 3)
                        w3 = v3(DMB[:, 0:n4], 4)
                        for h in range(NH):
                            if h >= 2:
                                after(ve, "dvn_part", l, h - 1)
                            if h < 2:
                                do(ve.memset(w(WQ_AT[h], NSEQ * P), 0.0))
                            own_w, own_q = (w(WQ_AT[h % 2] + x, NSEQ * (P + LSEQ)).rearrange("p (s u) -> p s u", s=NSEQ)[:, :, 0:LSEQ]
                                            for x in (0, TS))
                            go(cp(own_q, v3(cv3[:, h, t0:t0 + TS], NSEQ)))
                            go(cp(own_w, v3(w3[:, h, :], NSEQ)), "dwm")

                for first in (0, 2):
                    group = (0, 1) if first == 0 else (2,)
                    for i in group:
                        prepare(i)
                    invert(group)
                    low.to(AT_OUT[l] + 2)
                    for i in group:
                        finish(i)
                after(ve, "do", l, 3)

                def sample_values(h):
                    vm = v3((D01, D34)[h % 2], NSEQ)
                    go(tt(vm[0:TS, :, :], mid(DY[0:TS, h * P:(h + 1) * P], NSEQ), last(cst("seq", TS), NK), ALU.mult), "dvm")
                    do(tt(DS[:, h, :, :], DS[:, h, :, :], last(v3(gEL[:, :], 4)[:, h, :], NK), ALU.mult))

                def sample_state(h):
                    after(ve, "dss_mm", l, h + 1)
                    for c in range(2):
                        d = DS[:, h, 4 * c:4 * c + 4, :]
                        go(tt(d, d, v3(SBANK[h % 2][c][:, :], 4), ALU.add), "gdn_sstate" if c else None)

                finish_heads(("heads", 2 * l + 2), 4, ZT, col(f"gdnn{l}"), "gdn_fin", w(4 * TL, TL), True,
                             lambda: low_parts(3 * l + 1, "hl_out", range(GH)))
                low_parts(3 * l + 1, "hl_out", range(GH, KD))
                sample_values(0)
                sample_values(1)
                go(cp(rt[:, 0:1], rs[:, 0:1]), "gdn_done")

                for j in range(KD):
                    after(ve, "out_mm", l, j + 1)
                    residual(B[5 + j % 2], j, m0 + 16, "x_mix")
                    if j % 2:
                        low.to(AT_OUT[l] + j // 2 + 2)
                    if j - 1 in STATE_AT:
                        h = STATE_AT.index(j - 1)
                        sample_state(h)
                        if h < 2:
                            sample_values(h + 2)
                norm(2 * l + 2, m0 + 24, m0 + 32, AT_OUT[l] + H_OUT + 2)
                if l == 0:
                    for k in range(KD):
                        ve.wait_ge(S("h_norm"), KD + (k + 1))
                        low_parts(2, "hl_ff", (k,))
                    after(ve, "gdn_state_out", 0, 32)
                    for u in range(FD):
                        e = FSG[u % 2]
                        ve.wait_ge(S("ff_silu"), u + 1)
                        do(tt(e, e, B[2 + u % 2][:, 0:T], ALU.mult))
                        do(cp(FAH[:, u, :], e))
                        do(tt(FAL[:, u, :], e, FAH[:, u, :], ALU.subtract), "ff_act")
                        low.to(AT_GU + u + PARTS)
                    for j in range(KD):
                        ve.wait_ge(S("down_mm"), 2 * j + 2)
                        residual(B[4 + j % 2], j, m0 + 40, "x_ff")
                        if j < KD - 1:
                            low.to(AT_DN + 2 * j + 1 + PARTS)

            ve.wait_ge(S("logits_mm"), 1)
            after(ve, "gdn_state_out", DEPTH - 1, 32)
            go(ve.memset(LG[:, :], 0.0))
            ve.wait_ge(S("vec_own"), own.n["vec_own"])
            go(cp(LG[:, 0:16], B[0][:, 0:16]))
            do(cp(LG[0:TS, 16:24], B[0][0:TS, 16:24]))
            lg3 = v3(LG[:, :], 3)
            do(ve.tensor_reduce(mx[:, :], lg3, AX.X, ALU.max))
            do(tt(v3(lgE[:, :], 3), lg3, last(mx[:, :], NE), ALU.subtract), "lg_shift")
            mine = last(LG[:, :], NE)
            for i in range(3):
                c = slice(NE * i, NE * (i + 1))
                mine = last(LG[:, c], NE)
                other = mid(LG[:, c], NE)
                go(tt(CMP[:, c, :], other, mine, ALU.is_gt))
                do(tt(CEQ[:, c, :], other, mine, ALU.is_equal))
                do(tt(CEQ[:, c, :], CEQ[:, c, :], v3(cbf("before"), NE), ALU.mult))
                do(tt(CMP[:, c, :], CMP[:, c, :], CEQ[:, c, :], ALU.add))
            do(ve.tensor_reduce(rank[:, :], CMP, AX.X, ALU.add))
            do(ts(sel[:, :], rank[:, :], 2.0, None, ALU.is_lt), "sel")
            ve.wait_ge(S("lg_exp"), 1)
            do(tt(cw[:, :], lgE[:, :], sel[:, :], ALU.mult))
            do(ve.tensor_reduce(mx[:, :], v3(cw[:, :], 3), AX.X, ALU.add))
            do(ve.reciprocal(mx[:, :], mx[:, :]))
            do(tt(v3(cw[:, :], 3), v3(cw[:, :], 3), last(mx[:, :], NE), ALU.mult))
            for u in range(6):
                i, c = u // 2, u % 2
                nt, f = TILES[i][1], slice(512 * c, 512 * c + 512)
                ve.wait_ge(S("htok_high"), u + 1)
                tt(HTL[0:nt, i, f], B[2 + c][0:nt, :], HTH[0:nt, i, f], ALU.subtract).then_inc(S("htok"), 1)
            ve.wait_ge(S("pos_mm"), 1)
            do(ve.memset(pos[:, :], FAR))
            pos3 = v3(pos[:, :], 3)
            sel3, cw3 = v3(sel[:, :], 3), v3(cw[:, :], 3)
            for i, (t0, nt) in enumerate(TILES):
                do(stt(pos3[0:nt, i, 0:NE], sel3[0:nt, i, :], -FAR, B[1][0:nt, NE * i:NE * (i + 1)], ALU.mult, ALU.add))
                do(ts(pos3[0:nt, i, 0:NE], pos3[0:nt, i, 0:NE], FAR, None, ALU.add))
            do(ve.tensor_reduce(mx[:, 0:1], B[1][:, 32:32 + NE], AX.X, ALU.max))
            do(ts(flag[:, :], mx[:, 0:1], float(CAP), None, ALU.is_gt))
            ve.wait_ge(S("htok_tr"), 6)
            do(ve.memset(hT[:, :, :], 0.0), "flag_ready")

            def onehot(e):
                for i, (t0, nt) in enumerate(TILES):
                    ins = ts(ONEH[0:nt, i, :], cbf("iota", nt), pos3[0:nt, i, bass.ds(e, 1)], None, ALU.is_equal)
                ins.then_inc(S("onehot"), 1)

            def onehot_weights(e):
                for i, (t0, nt) in enumerate(TILES):
                    ins = ts(ONEW[0:nt, i, :], cbf("iota", nt), pos3[0:nt, i, bass.ds(e, 1)],
                             cwp3[0:nt, i, bass.ds(e, 1)], ALU.is_equal, ALU.mult)
                ins.then_inc(S("onew"), 1)

            def gathered(g):
                for c in range(2):
                    ve.wait_ge(S("hg_high"), g + (c - 1))
                    tt(HGL[:, 4 * c:4 * c + 4, :], v3(B[1 + 2 * c][:, :], 4), HGH[:, 4 * c:4 * c + 4, :], ALU.subtract)\
                        .then_inc(S("e_in"), 1)

            def scattered(el, j):
                ve.wait_ge(S("e_sc_mm"), el * KD + (j + 2))
                tt(hT[:, j, :], hT[:, j, :], B[4 + j % 2][:, 0:T], ALU.add).then_inc(S("e_scatter"), 1)

            for z in (B[2], B[6], B[7]):
                go(ve.memset(z[:, :], 0.0))
            do(ve.memset(cwp[:, :], 0.0))
            cwp3 = v3(cwp[:, :], 3)
            do(cp(cwp3[:, :, 0:NE], cw3))
            onehot(0)
            gathered(2)

            def expert(e, el, r):
                def turned(c):
                    ve.wait_ge(S("e_turn_high"), el * NCH + (c + 1))
                    tt(EATL[:, c % 2, :], B[4 + c % 2][:, :], EATH[:, c % 2, :], ALU.subtract).then_inc(S("e_actT"), 1)

                for j in range(PARTS):
                    e_split_low(ve, el, j)
                for j in range(PER_E - 2):
                    kind, c = ORDER[j // 2]
                    if 2 <= j < 2 + KD // 2:
                        scattered(el, 2 * (j - 2))
                        scattered(el, 2 * (j - 2) + 1)
                    if kind == GATE and j % 2 and c:
                        turned(c - 1)
                    if kind == UP and j % 2:
                        ve.wait_ge(S("e_silu"), el * NCH + (c + 1))
                        ve.wait_ge(S("e_up_mm"), el * (2 * NCH) + (2 * c + 2))
                        tt(EA[:, c % 2, :], EA[:, c % 2, :], B[2 + c % 2][:, :], ALU.mult).then_inc(S("e_act"), 1)
                    if j == PER_E - 4:
                        gathered(el * 2 + (2 * r + 4))
                        turned(NCH - 1)
                    if j + PARTS < PER_E:
                        e_split_low(ve, el, j + PARTS)
                    if j == 10:
                        ve.wait_ge(S("e_wT_mm"), el + 1)
                        onehot_weights(e)
                    if j == 14:
                        ve.wait_ge(S("e_gather_mm"), el * 2 + (2 * r + 2))
                        onehot(e + 1)

            def tail(el):
                for j in range(KD):
                    scattered(el, j)
                ve.wait_ge(S("e_scatter"), el * KD + (KD + 1))

            with ve.Fori(0, NE) as e:
                expert(e, e, 0)
            more = ve.value_load(flag[0:1, 0:1], min_val=0, max_val=1)
            with ve.If(more > 0):
                with ve.Fori(1, MAXPASS) as r:
                    ve.wait_ge(S("onew"), r * NE)
                    ve.wait_ge(S("onehot"), r * (NE + 1))
                    ts(pos[:, :], pos[:, :], -float(CAP), None, ALU.add).then_inc(S("shifted"), 1)
                    ve.wait_ge(S("shifted"), r)
                    ve.wait_ge(S("e_gather_mm"), r * (2 * (NE + 1)))
                    onehot(0)
                    gathered(r * (2 * (NE + 1)) + 2)
                    with ve.Fori(0, NE) as e:
                        expert(e, r * NE + e, r)
                tail(NE * MAXPASS)
            with ve.If(more < 1):
                tail(NE)

            for j in range(KD):
                residual(hT[:, j, :], j, 48 + 40, "x_moe")
            norm(5, 96, 104)
            ve.wait_ge(S("h_norm"), KD * 5)
            ve.wait_ge(S("vec_own"), own.n["vec_own"])
            go(cp(rt[:, 0:1], rs[:, 0:1]), "y_done")


def tiles(a):
    *lead, r, c = a.shape
    return np.moveaxis(a.reshape(*lead, r // P, P, c), -2, -3)


def halves(a, width=CH, rows=KD // 2):
    r, c = a.shape
    t = a.reshape(r // P // rows, rows, P, c // width, width).transpose(3, 0, 2, 1, 4)
    return np.ascontiguousarray(t).reshape(-1, P, rows * width)


def columns(v):
    return np.moveaxis(v.reshape(*v.shape[:-1], -1, P), -1, 0)


def lay_out(x):
    f = np.float32
    out = {}
    xs = np.concatenate([x["x_prompt"].reshape(TP, D), x["x_sample"].reshape(TS, D)], 0)
    out["xT"] = tiles(xs.T)
    q, k, v, lr, g, qkv, a, b, z = np.split(x["w_in"], np.cumsum([256, 256, 512, 16, 512, 1536, 4, 4]), axis=-1)
    big = np.concatenate([qkv, q, k, v, g, z], -1)
    first = np.zeros((DEPTH, D, P), f)
    first[:, :, :LR], first[:, :, AB:AB + 2 * NH] = lr, np.concatenate([a, b], -1)
    big = np.concatenate([first, big, np.zeros((DEPTH, D, P), f)], -1)
    out["w_in"] = np.stack([halves(big[l], 2 * P, KD) for l in range(DEPTH)])
    out["w_out"] = np.stack([halves(x["w_out"][l], 2 * P, KD) for l in range(DEPTH)])
    out["ada"] = np.concatenate([halves(w) for w in (x["w_ada"][0], x["w_ada"][1], x["w_ada_final"])])
    gate, up = x["w_ff_gate"][0].reshape(D, FD, 1, P), x["w_ff_up"][0].reshape(D, FD, 1, P)
    out["gu"] = halves(np.concatenate([gate, up], 2).reshape(D, 2 * FD * P), 2 * P, KD)
    out["down"] = halves(x["w_ff_down"][0], P, FD // 2)
    moe = np.empty((NE, len(ORDER), 2, P, HALF), f)
    for e in range(NE):
        by_kind = [halves(x["w_exp_gate"][0, e]), halves(x["w_exp_up"][0, e]), halves(x["w_exp_down"][0, e], D, 2)]
        for i, (kind, c) in enumerate(ORDER):
            moe[e, i] = by_kind[kind][2 * c:2 * c + 2]
    out["moe"] = moe.reshape(NE * PER_E, P, HALF)
    out["wgate"] = x["w_gla_gate"]
    out["wrt"] = tiles(x["w_router"][0])
    sm = np.zeros((P, N_SM), f)

    def put(name, val):
        at, n = SM[name]
        sm[:, at:at + n] = val.reshape(P, n)

    c = np.concatenate([x["c_prompt"], x["c_sample"]], 0)
    put("c", tiles(c.T))
    put("b_ada", columns(np.concatenate([x["b_ada"][0], x["b_ada"][1], x["b_ada_final"]])))
    for l in range(DEPTH):
        put(f"nm{l}", columns(x["norm_mix"][l]))
        put(f"nf{l}", columns(x["norm_ffn"][l]))
        put(f"bg{l}", columns(x["b_gla_gate"][l]))
        put(f"wconv{l}", columns(x["w_conv"][l]).transpose(0, 2, 1))
        put(f"glan{l}", columns(x["gla_norm"][l]))
        put(f"gdnn{l}", columns(x["gdn_norm"][l]))
        put(f"alog{l}", np.broadcast_to(x["a_log"][l], (P, NH)))
        put(f"dtb{l}", np.broadcast_to(x["dt_bias"][l], (P, NH)))
    put("nfin", columns(x["norm_final"]))
    out["small"] = sm
    out["cf"], out["cb"] = shape_constants()
    out["s_conv"] = columns(x["state_conv"]).transpose(1, 0, 4, 2, 3)
    out["s_gla"] = x["state_gla"].reshape(DEPTH, NSEQ, 2, P, GV).transpose(0, 2, 3, 1, 4)
    out["s_gdn"] = x["state_gdn"].transpose(0, 3, 2, 1, 4)
    return {k: np.ascontiguousarray(v) for k, v in out.items()}


OUTS = {"y": (P, KD, T), "conv": (DEPTH, P, CT, NC_, 3), "gla_p": (DEPTH, P, 2, GV), "gla_s": (DEPTH, 2, P, NSEQ, GV),
        "gdn_p": (DEPTH, P, NH, NK), "gdn_s": (DEPTH, P, NH, NSEQ, NK)}


def kernel(**inputs):
    import concourse.bacc as bacc
    from concourse.bass_utils import run_bass_kernel_spmd as run

    arrays = lay_out({k: np.asarray(v) for k, v in inputs.items()})
    nc = bacc.Bacc("TRN2", target_bir_lowering=False, num_devices=1)
    A = {k: nc.dram_tensor(f"in_{k}", v.shape, mybir.dt.from_np(v.dtype), kind="ExternalInput").ap()
         for k, v in arrays.items()}
    O = {k: nc.dram_tensor(f"out_{k}", s, F32, kind="ExternalOutput").ap() for k, s in OUTS.items()}
    build(nc, A, O)
    got = run(nc, [{f"in_{k}": v for k, v in arrays.items()}], core_ids=[0]).results[0]
    r = {k: got[f"out_{k}"] for k in OUTS}
    y = np.ascontiguousarray(r["y"].transpose(2, 1, 0)).reshape(T, D)
    conv = r["conv"].transpose(0, 3, 4, 2, 1).reshape(DEPTH, NC_, 3, CT * P)
    gla_p = r["gla_p"].transpose(0, 2, 1, 3).reshape(DEPTH, 1, GH, GK, GV)
    gla_s = r["gla_s"].transpose(0, 3, 1, 2, 4).reshape(DEPTH, NSEQ, GH, GK, GV)
    gdn_p = r["gdn_p"].transpose(0, 2, 1, 3).reshape(DEPTH, 1, NH, NK, NK)
    gdn_s = r["gdn_s"].transpose(0, 3, 2, 1, 4)
    full = [y[:TP].reshape(1, TP, D), y[TP:].reshape(NSEQ, LSEQ, D), gla_p, gdn_p, conv[:, 0:1], gla_s, gdn_s, conv[:, 1:]]
    return tuple(np.ascontiguousarray(a) for a in full)
```
